# Optimizing a Trainium2 kernel written in Bass

```python
import jax, jax.numpy as jnp
from jax import lax
import numpy as np
import math
import jax
import jax.numpy as jnp

D_MODEL = 1024
BATCH = 1
SEQ = 512
DEPTH = 2

N_MIXERS = 2
N_MLA = (DEPTH + 1) // 2
N_HGRN = DEPTH // 2

MLA_HEADS = 8
MLA_Q_LORA = 512
MLA_KV_LORA = 256
MLA_NOPE = 128
MLA_ROPE = 64
MLA_V = 128
ROPE_BASE = 10000.0
ATTN_BLOCK = 128

HGRN_HEADS = 8
HGRN_DK = D_MODEL // HGRN_HEADS
HGRN_DV = D_MODEL // HGRN_HEADS
HGRN_CHUNK = 32

D_FF = 4 * D_MODEL

EPS = 1e-6


def rms_norm(x, g):
    xf = x.astype(jnp.float32)
    y = xf * lax.rsqrt(jnp.mean(xf * xf, axis=-1, keepdims=True) + EPS)
    return (y * g.astype(jnp.float32)).astype(x.dtype)

def rope_cos_sin(positions):
    inv_freq = jnp.power(ROPE_BASE, -jnp.arange(0, MLA_ROPE, 2, dtype=jnp.float32) / MLA_ROPE)
    ang = positions.astype(jnp.float32)[..., None] * inv_freq
    return jnp.cos(ang), jnp.sin(ang)

def apply_rope(t, cos, sin):
    tf = t.astype(jnp.float32)
    t1, t2 = jnp.split(tf, 2, axis=-1)
    return jnp.concatenate([t1 * cos - t2 * sin, t1 * sin + t2 * cos], axis=-1).astype(t.dtype)

def mla_mixer(h, cos, sin, w_in, q_norm, kv_norm, w_uq, w_ukv, w_o):
    B, S, _ = h.shape
    H = MLA_HEADS
    proj = h @ w_in
    c_q, c_kv, k_r = jnp.split(proj, [MLA_Q_LORA, MLA_Q_LORA + MLA_KV_LORA], axis=-1)
    q = (rms_norm(c_q, q_norm) @ w_uq).reshape(B, S, H, MLA_NOPE + MLA_ROPE)
    q_nope = q[..., :MLA_NOPE]
    q_rope = apply_rope(q[..., MLA_NOPE:], cos[:, :, None, :], sin[:, :, None, :])
    kv = (rms_norm(c_kv, kv_norm) @ w_ukv).reshape(B, S, H, MLA_NOPE + MLA_V)
    k_nope, v = kv[..., :MLA_NOPE], kv[..., MLA_NOPE:]
    k_rope = apply_rope(k_r, cos, sin)
    scale = (MLA_NOPE + MLA_ROPE) ** -0.5
    nb = S // ATTN_BLOCK
    qn_b = q_nope.reshape(B, nb, ATTN_BLOCK, H, MLA_NOPE).transpose(1, 0, 2, 3, 4)
    qr_b = q_rope.reshape(B, nb, ATTN_BLOCK, H, MLA_ROPE).transpose(1, 0, 2, 3, 4)
    k_pos = jnp.arange(S)

    def block(args):
        qn, qr, blk = args
        s = (jnp.einsum('bqhd,bkhd->bhqk', qn, k_nope)
             + jnp.einsum('bqhr,bkr->bhqk', qr, k_rope)).astype(jnp.float32) * scale
        q_pos = blk * ATTN_BLOCK + jnp.arange(ATTN_BLOCK)
        s = jnp.where(q_pos[:, None] >= k_pos[None, :], s, -jnp.inf)
        p = jax.nn.softmax(s, axis=-1).astype(v.dtype)
        return jnp.einsum('bhqk,bkhd->bqhd', p, v)

    o = lax.map(block, (qn_b, qr_b, jnp.arange(nb)))
    o = o.transpose(1, 0, 2, 3, 4).reshape(B, S, H * MLA_V)
    return o @ w_o

def hgrn2_mixer(h, lb, w_in, o_norm, w_o):
    B, S, _ = h.shape
    H, DK, DV, C = HGRN_HEADS, HGRN_DK, HGRN_DV, HGRN_CHUNK
    nc = S // C
    HK, HV = H * DK, H * DV
    proj = h @ w_in
    q_x, f_x, i_x, g_x = jnp.split(proj, [HK, 2 * HK, 2 * HK + HV], axis=-1)

    def heads(t, d):
        return t.astype(jnp.float32).reshape(B, nc, C, H, d).transpose(0, 3, 1, 2, 4)

    f = lb + (1.0 - lb) * jax.nn.sigmoid(f_x.astype(jnp.float32))
    q = heads(jax.nn.silu(q_x.astype(jnp.float32)), DK)
    k = heads(1.0 - f, DK)
    log_f = heads(jnp.log(f), DK)
    v = heads(i_x, DV)

    b = jnp.cumsum(log_f, axis=3)
    b_ref = b[:, :, :, C // 2:C // 2 + 1, :]
    b_last = b[:, :, :, -1:, :]
    q_rel = q * jnp.exp(b - b_ref)
    k_rel = k * jnp.exp(b_ref - b)
    causal = jnp.tril(jnp.ones((C, C), dtype=bool))
    a = jnp.where(causal, jnp.einsum('bhncd,bhnsd->bhncs', q_rel, k_rel), 0.0)
    o_intra = jnp.einsum('bhncs,bhnse->bhnce', a, v)

    q_dec = q * jnp.exp(b)
    k_dec = k * jnp.exp(b_last - b)
    chunk_decay = jnp.exp(b_last[:, :, :, 0, :])

    def step(state, xs):
        qd, kd, vc, dec = xs
        o_inter = jnp.einsum('bhcd,bhde->bhce', qd, state)
        state = dec[..., None] * state + jnp.einsum('bhcd,bhce->bhde', kd, vc)
        return state, o_inter

    mv = lambda t: jnp.moveaxis(t, 2, 0)
    s0 = jnp.zeros((B, H, DK, DV), jnp.float32)
    _, o_inter = lax.scan(step, s0, (mv(q_dec), mv(k_dec), mv(v), mv(chunk_decay)))
    o = o_intra + jnp.moveaxis(o_inter, 0, 2)
    o = o.transpose(0, 2, 3, 1, 4).reshape(B, S, H, DV)
    gate = jax.nn.silu(g_x.astype(jnp.float32)).reshape(B, S, H, DV)
    o = rms_norm(o, o_norm) * gate
    return o.reshape(B, S, HV).astype(h.dtype) @ w_o

def sq_relu_mlp(h, w1, w2):
    a = jax.nn.relu(h @ w1)
    return (a * a) @ w2

def first_inputs(seed: int = 0) -> dict:
    key = jax.random.key(seed)
    ks = jax.random.split(key, 16)
    f32 = jnp.float32
    nrm = lambda k, shape, fan_in: jax.random.normal(k, shape, f32) * (fan_in ** -0.5)
    mla_in_w = MLA_Q_LORA + MLA_KV_LORA + MLA_ROPE
    hgrn_in_w = 3 * HGRN_HEADS * HGRN_DK + HGRN_HEADS * HGRN_DV
    return {
        "x": jax.random.normal(ks[0], (BATCH, SEQ, D_MODEL), f32),
        "positions": jnp.broadcast_to(jnp.arange(SEQ, dtype=jnp.int32), (BATCH, SEQ)),
        "norm_gains": 1.0 + 0.1 * jax.random.normal(ks[1], (DEPTH, 4, D_MODEL), f32),
        "mla_w_in": nrm(ks[2], (N_MLA, D_MODEL, mla_in_w), D_MODEL),
        "mla_q_norm": 1.0 + 0.1 * jax.random.normal(ks[3], (N_MLA, MLA_Q_LORA), f32),
        "mla_kv_norm": 1.0 + 0.1 * jax.random.normal(ks[4], (N_MLA, MLA_KV_LORA), f32),
        "mla_w_uq": nrm(ks[5], (N_MLA, MLA_Q_LORA, MLA_HEADS * (MLA_NOPE + MLA_ROPE)), MLA_Q_LORA),
        "mla_w_ukv": nrm(ks[6], (N_MLA, MLA_KV_LORA, MLA_HEADS * (MLA_NOPE + MLA_V)), MLA_KV_LORA),
        "mla_w_o": nrm(ks[7], (N_MLA, MLA_HEADS * MLA_V, D_MODEL), MLA_HEADS * MLA_V),
        "hgrn_w_in": nrm(ks[8], (N_HGRN, D_MODEL, hgrn_in_w), D_MODEL),
        "hgrn_lb_logits": 0.1 * jax.random.normal(ks[9], (DEPTH, HGRN_HEADS * HGRN_DK), f32),
        "hgrn_o_norm": 1.0 + 0.1 * jax.random.normal(ks[10], (N_HGRN, HGRN_DV), f32),
        "hgrn_w_o": nrm(ks[11], (N_HGRN, HGRN_HEADS * HGRN_DV, D_MODEL), HGRN_HEADS * HGRN_DV),
        "mlp_w1": nrm(ks[12], (DEPTH, D_MODEL, D_FF), D_MODEL),
        "mlp_w2": nrm(ks[13], (DEPTH, D_FF, D_MODEL), D_FF),
    }

def first_block(x, positions, norm_gains, mla_w_in, mla_q_norm, mla_kv_norm, mla_w_uq, mla_w_ukv,
              mla_w_o, hgrn_w_in, hgrn_lb_logits, hgrn_o_norm, hgrn_w_o, mlp_w1, mlp_w2):
    cos, sin = rope_cos_sin(positions)
    p = jax.nn.softmax(hgrn_lb_logits.astype(jnp.float32), axis=0)
    lower_bounds = jnp.cumsum(p, axis=0) - p[0]
    h = x
    for layer in range(DEPTH):
        slot = layer // N_MIXERS
        a = rms_norm(h, norm_gains[layer, 0])
        if layer % N_MIXERS == 0:
            m = mla_mixer(a, cos, sin, mla_w_in[slot], mla_q_norm[slot], mla_kv_norm[slot],
                          mla_w_uq[slot], mla_w_ukv[slot], mla_w_o[slot])
        else:
            m = hgrn2_mixer(a, lower_bounds[layer], hgrn_w_in[slot], hgrn_o_norm[slot], hgrn_w_o[slot])
        h = h + rms_norm(m, norm_gains[layer, 1])
        a = rms_norm(h, norm_gains[layer, 2])
        h = h + rms_norm(sq_relu_mlp(a, mlp_w1[layer], mlp_w2[layer]), norm_gains[layer, 3])
    return h


DEPTH_2 = 1

HEAD_DIM = 64
DSA_HEADS = 16
DSA_KV_DIM = 64
IDX_HEADS = 8
IDX_DIM = 32
DSA_TOPK = 256
NSA_HEADS = 16
NSA_KV_HEADS = 2
NSA_GROUP = NSA_HEADS // NSA_KV_HEADS
CMP_BLOCK = 32
CMP_STRIDE = 16
SEL_BLOCK = 64
SEL_TOPN = 4
WINDOW = 512
SSD_INNER = 2 * D_MODEL
SSD_HEAD_DIM = 64
SSD_HEADS = SSD_INNER // SSD_HEAD_DIM
SSD_GROUPS = 4
SSD_HPG = SSD_HEADS // SSD_GROUPS
SSD_STATE = 128
SSD_CONV_DIM = SSD_INNER + 2 * SSD_GROUPS * SSD_STATE
CONV_WIDTH = 4
SSD_CHUNK = 128
D_FF_2 = 4 * D_MODEL
Q_BLOCK = 128
NEG = -1e30
IN_SPLITS = (DSA_HEADS * HEAD_DIM, DSA_KV_DIM, DSA_KV_DIM, IDX_HEADS * IDX_DIM, IDX_DIM, IDX_HEADS,
             NSA_HEADS * HEAD_DIM, 6 * NSA_KV_HEADS * HEAD_DIM, 3 * NSA_HEADS,
             SSD_INNER, SSD_CONV_DIM, SSD_HEADS, 3 * D_MODEL)
D_IN = sum(IN_SPLITS)


def rms_norm_2(x, g):
    xf = x.astype(jnp.float32)
    y = xf * lax.rsqrt(jnp.mean(xf * xf, axis=-1, keepdims=True) + EPS)
    return (y * g).astype(x.dtype)

def _to_blocks(a):
    b, s = a.shape[:2]
    return jnp.moveaxis(a.reshape((b, s // Q_BLOCK, Q_BLOCK) + a.shape[2:]), 1, 0)

def _from_blocks(a):
    nb, b = a.shape[:2]
    return jnp.moveaxis(a, 0, 1).reshape((b, nb * a.shape[2]) + a.shape[3:])

def dsa_mixer(q, k, v, iq, ik, iw):
    seq = q.shape[1]
    n_sel = min(DSA_TOPK, seq // 4)
    key_pos = jnp.arange(seq)
    scale = HEAD_DIM ** -0.5
    gather = jax.vmap(lambda a, i: a[i])

    def block(args):
        qb, iqb, iwb, start = args
        t = start + jnp.arange(Q_BLOCK)
        idx = jnp.einsum('bqhd,bsd->bqhs', iqb, ik)
        idx = jnp.einsum('bqh,bqhs->bqs', iwb, jax.nn.relu(idx)).astype(jnp.float32)
        idx = jnp.where((key_pos[None, :] <= t[:, None])[None], idx, -jnp.inf)
        _, sel = lax.top_k(idx, n_sel)
        k_sel = gather(k, sel)
        v_sel = gather(v, sel)
        s = jnp.einsum('bqhd,bqkd->bqhk', qb, k_sel).astype(jnp.float32) * scale
        s = jnp.where((sel <= t[None, :, None])[:, :, None, :], s, NEG)
        p = jax.nn.softmax(s, axis=-1).astype(v.dtype)
        return jnp.einsum('bqhk,bqkd->bqhd', p, v_sel)

    starts = jnp.arange(seq // Q_BLOCK) * Q_BLOCK
    out = lax.map(block, (_to_blocks(q), _to_blocks(iq), _to_blocks(iw), starts))
    return _from_blocks(out)

def nsa_mixer(q, kc, vc, ks, vs, kw, vw, gates, k_norm_g, cmp_pos, cmp_w):
    bsz, seq = q.shape[:2]
    scale = HEAD_DIM ** -0.5
    n_cmp = (seq - CMP_BLOCK) // CMP_STRIDE + 1
    win_idx = jnp.arange(n_cmp)[:, None] * CMP_STRIDE + jnp.arange(CMP_BLOCK)[None, :]

    def compress(a, pos, w):
        blocks = a[:, win_idx] + pos[None, None, :, None, :]
        return jnp.einsum('bnlgd,lde->bnge', blocks, w)

    k_cmp = rms_norm_2(compress(kc, cmp_pos[0], cmp_w[0]), k_norm_g[0])
    v_cmp = compress(vc, cmp_pos[1], cmp_w[1])
    cmp_start = jnp.arange(n_cmp) * CMP_STRIDE
    cmp_end = cmp_start + CMP_BLOCK - 1
    n_blk = seq // SEL_BLOCK
    n_sel = min(SEL_TOPN, n_blk)
    blk_start = jnp.arange(n_blk) * SEL_BLOCK
    cover = ((cmp_start[:, None] < blk_start[None, :] + SEL_BLOCK)
             & (cmp_start[:, None] + CMP_BLOCK > blk_start[None, :])).astype(jnp.float32)
    ks = rms_norm_2(ks, k_norm_g[1])
    ks_blocks = ks.reshape(bsz, n_blk, SEL_BLOCK, NSA_KV_HEADS, HEAD_DIM).transpose(0, 3, 1, 2, 4)
    vs_blocks = vs.reshape(bsz, n_blk, SEL_BLOCK, NSA_KV_HEADS, HEAD_DIM).transpose(0, 3, 1, 2, 4)
    gather_blocks = jax.vmap(jax.vmap(lambda blk, i: blk[i]))
    kw = rms_norm_2(kw, k_norm_g[2])
    pad = ((0, 0), (WINDOW, 0), (0, 0), (0, 0))
    kw_pad = jnp.pad(kw, pad)
    vw_pad = jnp.pad(vw, pad)
    n_slc_keys = n_sel * SEL_BLOCK

    def block(args):
        qb, gb, start = args
        t = start + jnp.arange(Q_BLOCK)
        s = jnp.einsum('bqghd,bngd->bqghn', qb, k_cmp).astype(jnp.float32) * scale
        vis = (cmp_end[None, :] <= t[:, None])[None, :, None, None, :]
        s = jnp.where(vis, s, NEG)
        p_cmp = jax.nn.softmax(s, axis=-1) * vis
        o_cmp = jnp.einsum('bqghn,bngd->bqghd', p_cmp.astype(v_cmp.dtype), v_cmp)
        imp = jnp.einsum('bqghn,nj->bqgj', p_cmp, cover)
        cur = t // SEL_BLOCK
        j = jnp.arange(n_blk)
        forced = ((j[None, :] == cur[:, None]) | (j[None, :] == 0))[None, :, None, :]
        future = (j[None, :] > cur[:, None])[None, :, None, :]
        imp = jnp.where(forced, jnp.inf, jnp.where(future, -jnp.inf, imp))
        _, sel = lax.top_k(imp, n_sel)
        sel_t = sel.transpose(0, 2, 1, 3)
        bq = qb.shape[0]
        k_sel = gather_blocks(ks_blocks, sel_t).reshape(bq, NSA_KV_HEADS, Q_BLOCK, n_slc_keys, HEAD_DIM)
        v_sel = gather_blocks(vs_blocks, sel_t).reshape(bq, NSA_KV_HEADS, Q_BLOCK, n_slc_keys, HEAD_DIM)
        pos = (sel_t[..., None] * SEL_BLOCK + jnp.arange(SEL_BLOCK)).reshape(bq, NSA_KV_HEADS, Q_BLOCK, n_slc_keys)
        ok = (pos <= t[None, None, :, None]).transpose(0, 2, 1, 3)[:, :, :, None, :]
        s = jnp.einsum('bqghd,bgqkd->bqghk', qb, k_sel).astype(jnp.float32) * scale
        s = jnp.where(ok, s, NEG)
        p = jax.nn.softmax(s, axis=-1).astype(v_sel.dtype)
        o_slc = jnp.einsum('bqghk,bgqkd->bqghd', p, v_sel)
        kwb = lax.dynamic_slice_in_dim(kw_pad, start, WINDOW + Q_BLOCK, axis=1)
        vwb = lax.dynamic_slice_in_dim(vw_pad, start, WINDOW + Q_BLOCK, axis=1)
        pos_w = start - WINDOW + jnp.arange(WINDOW + Q_BLOCK)
        ok_w = ((pos_w[None, :] <= t[:, None]) & (pos_w[None, :] > t[:, None] - WINDOW)
                & (pos_w[None, :] >= 0))[None, :, None, None, :]
        s = jnp.einsum('bqghd,bkgd->bqghk', qb, kwb).astype(jnp.float32) * scale
        s = jnp.where(ok_w, s, NEG)
        p = jax.nn.softmax(s, axis=-1).astype(vwb.dtype)
        o_win = jnp.einsum('bqghk,bkgd->bqghd', p, vwb)
        return gb[..., 0:1] * o_cmp + gb[..., 1:2] * o_slc + gb[..., 2:3] * o_win

    starts = jnp.arange(seq // Q_BLOCK) * Q_BLOCK
    out = lax.map(block, (_to_blocks(q), _to_blocks(gates), starts))
    return _from_blocks(out)

def causal_conv(x, w, b):
    out = lax.conv_general_dilated(x, w[:, None, :], window_strides=(1,), padding=[(CONV_WIDTH - 1, 0)],
                                   dimension_numbers=('NWC', 'WIO', 'NWC'), feature_group_count=x.shape[-1])
    return out + b

def ssd_mixer(z, xbc, dt, conv_w, conv_b, dt_bias, a_log, d_skip, norm_g):
    bsz, seq = z.shape[:2]
    nc = seq // SSD_CHUNK
    xbc = jax.nn.silu(causal_conv(xbc, conv_w, conv_b))
    gn = SSD_GROUPS * SSD_STATE
    xs = xbc[..., :SSD_INNER].reshape(bsz, nc, SSD_CHUNK, SSD_GROUPS, SSD_HPG, SSD_HEAD_DIM)
    bm = xbc[..., SSD_INNER:SSD_INNER + gn].reshape(bsz, nc, SSD_CHUNK, SSD_GROUPS, SSD_STATE)
    cm = xbc[..., SSD_INNER + gn:].reshape(bsz, nc, SSD_CHUNK, SSD_GROUPS, SSD_STATE)
    dtc = jax.nn.softplus(dt.astype(jnp.float32) + dt_bias).reshape(bsz, nc, SSD_CHUNK, SSD_GROUPS, SSD_HPG)
    a = -jnp.exp(a_log.astype(jnp.float32)).reshape(SSD_GROUPS, SSD_HPG)
    a_cum = jnp.cumsum(dtc * a, axis=2)
    seg = a_cum[:, :, :, None] - a_cum[:, :, None, :]
    tril = jnp.tril(jnp.ones((SSD_CHUNK, SSD_CHUNK), dtype=bool))[None, None, :, :, None, None]
    lmat = jnp.exp(jnp.where(tril, seg, -jnp.inf))
    cb = jnp.einsum('bcign,bcjgn->bcijg', cm, bm)
    y_diag = jnp.einsum('bcijg,bcijgh,bcjgh,bcjghp->bcighp', cb, lmat, dtc, xs)
    decay_states = jnp.exp(a_cum[:, :, -1:] - a_cum)
    states = jnp.einsum('bcjgn,bcjgh,bcjghp->bcghpn', bm, decay_states * dtc, xs)
    chunk_decay = jnp.exp(a_cum[:, :, -1])

    def step(h, inp):
        s_c, d_c = inp
        return h * d_c[..., None, None] + s_c, h

    h0 = jnp.zeros((bsz, SSD_GROUPS, SSD_HPG, SSD_HEAD_DIM, SSD_STATE), states.dtype)
    _, h_in = lax.scan(step, h0, (jnp.moveaxis(states, 1, 0), jnp.moveaxis(chunk_decay, 1, 0)))
    h_in = jnp.moveaxis(h_in, 0, 1)
    y_off = jnp.einsum('bcign,bcghpn,bcigh->bcighp', cm, h_in, jnp.exp(a_cum))
    y = y_diag + y_off + xs * d_skip.reshape(SSD_GROUPS, SSD_HPG)[:, :, None]
    y = y.reshape(bsz, seq, SSD_INNER)
    y = rms_norm_2(y * jax.nn.silu(z.astype(jnp.float32)), norm_g)
    return y.astype(z.dtype)

def second_inputs(seed: int = 0) -> dict:
    key = jax.random.key(seed)
    ks = jax.random.split(key, 24)
    f32 = jnp.float32

    def nrm(k, shape, scale):
        return jax.random.normal(k, shape, f32) * scale

    def gain(k, shape):
        return 1.0 + 0.02 * jax.random.normal(k, shape, f32)

    dt0 = jnp.exp(jax.random.uniform(ks[12], (DEPTH_2, SSD_HEADS), f32, math.log(1e-3), math.log(1e-1)))
    return {
        'x': nrm(ks[0], (BATCH, SEQ, D_MODEL), 1.0),
        'norm1_g': gain(ks[1], (DEPTH_2, D_MODEL)),
        'w_in': nrm(ks[2], (DEPTH_2, D_MODEL, D_IN), D_MODEL ** -0.5),
        'dsa_q_norm': gain(ks[3], (DEPTH_2, HEAD_DIM)),
        'dsa_k_norm': gain(ks[4], (DEPTH_2, DSA_KV_DIM)),
        'nsa_q_norm': gain(ks[5], (DEPTH_2, HEAD_DIM)),
        'nsa_k_norm': gain(ks[6], (DEPTH_2, 3, HEAD_DIM)),
        'nsa_cmp_pos': nrm(ks[7], (DEPTH_2, 2, CMP_BLOCK, HEAD_DIM), 0.02),
        'nsa_cmp_w': nrm(ks[8], (DEPTH_2, 2, CMP_BLOCK, HEAD_DIM, HEAD_DIM), (CMP_BLOCK * HEAD_DIM) ** -0.5),
        'ssd_conv_w': nrm(ks[9], (DEPTH_2, CONV_WIDTH, SSD_CONV_DIM), CONV_WIDTH ** -0.5),
        'ssd_conv_b': nrm(ks[10], (DEPTH_2, SSD_CONV_DIM), 0.02),
        'ssd_dt_bias': dt0 + jnp.log(-jnp.expm1(-dt0)),
        'ssd_a_log': jnp.log(jax.random.uniform(ks[11], (DEPTH_2, SSD_HEADS), f32, 1.0, 16.0)),
        'ssd_d': gain(ks[13], (DEPTH_2, SSD_HEADS)),
        'ssd_norm_g': gain(ks[14], (DEPTH_2, SSD_INNER)),
        'w_br_dsa': nrm(ks[15], (DEPTH_2, DSA_HEADS * HEAD_DIM, D_MODEL), (DSA_HEADS * HEAD_DIM) ** -0.5),
        'w_br_nsa': nrm(ks[16], (DEPTH_2, NSA_HEADS * HEAD_DIM, D_MODEL), (NSA_HEADS * HEAD_DIM) ** -0.5),
        'w_br_ssd': nrm(ks[17], (DEPTH_2, SSD_INNER, D_MODEL), SSD_INNER ** -0.5),
        'w_out': nrm(ks[18], (DEPTH_2, D_MODEL, D_MODEL), D_MODEL ** -0.5),
        'norm2_g': gain(ks[19], (DEPTH_2, D_MODEL)),
        'w_ff1': nrm(ks[20], (DEPTH_2, D_MODEL, D_FF_2), D_MODEL ** -0.5),
        'w_ff2': nrm(ks[21], (DEPTH_2, D_FF_2, D_MODEL), D_FF_2 ** -0.5),
    }

def second_block(x, norm1_g, w_in, dsa_q_norm, dsa_k_norm, nsa_q_norm, nsa_k_norm, nsa_cmp_pos, nsa_cmp_w,
              ssd_conv_w, ssd_conv_b, ssd_dt_bias, ssd_a_log, ssd_d, ssd_norm_g,
              w_br_dsa, w_br_nsa, w_br_ssd, w_out, norm2_g, w_ff1, w_ff2):
    bsz, seq = x.shape[:2]
    offsets = [int(o) for o in np.cumsum(IN_SPLITS)[:-1]]
    for l in range(DEPTH_2):
        h = rms_norm_2(x, norm1_g[l])
        u = h @ w_in[l]
        (dq, dk, dv, iq, ik, iw, nq, nkv, ng, sz, sxbc, sdt, mg) = jnp.split(u, offsets, axis=-1)
        y_a = dsa_mixer(rms_norm_2(dq.reshape(bsz, seq, DSA_HEADS, HEAD_DIM), dsa_q_norm[l]),
                        rms_norm_2(dk, dsa_k_norm[l]), dv,
                        iq.reshape(bsz, seq, IDX_HEADS, IDX_DIM), ik, iw)
        y_a = y_a.reshape(bsz, seq, DSA_HEADS * HEAD_DIM)
        nkv = nkv.reshape(bsz, seq, 6, NSA_KV_HEADS, HEAD_DIM)
        y_b = nsa_mixer(rms_norm_2(nq.reshape(bsz, seq, NSA_KV_HEADS, NSA_GROUP, HEAD_DIM), nsa_q_norm[l]),
                        nkv[:, :, 0], nkv[:, :, 1], nkv[:, :, 2], nkv[:, :, 3], nkv[:, :, 4], nkv[:, :, 5],
                        jax.nn.sigmoid(ng.reshape(bsz, seq, NSA_KV_HEADS, NSA_GROUP, 3)),
                        nsa_k_norm[l], nsa_cmp_pos[l], nsa_cmp_w[l])
        y_b = y_b.reshape(bsz, seq, NSA_HEADS * HEAD_DIM)
        y_c = ssd_mixer(sz, sxbc, sdt, ssd_conv_w[l], ssd_conv_b[l], ssd_dt_bias[l], ssd_a_log[l],
                        ssd_d[l], ssd_norm_g[l])
        gates = jax.nn.sigmoid(mg.reshape(bsz, seq, 3, D_MODEL))
        mix = (gates[:, :, 0] * (y_a @ w_br_dsa[l]) + gates[:, :, 1] * (y_b @ w_br_nsa[l])
               + gates[:, :, 2] * (y_c @ w_br_ssd[l]))
        x = x + mix @ w_out[l]
        h = rms_norm_2(x, norm2_g[l])
        x = x + jnp.square(jax.nn.relu(h @ w_ff1[l])) @ w_ff2[l]
    return x


def setup_inputs(seed=0):
    out = dict(first_inputs(seed))
    for name, value in second_inputs(seed + 1).items():
        if name != "x":
            out[name + "_2"] = value
    return out


def reference(
    x, positions, norm_gains, mla_w_in, mla_q_norm, mla_kv_norm, mla_w_uq, mla_w_ukv, mla_w_o,
    hgrn_w_in, hgrn_lb_logits, hgrn_o_norm, hgrn_w_o, mlp_w1, mlp_w2, norm1_g_2, w_in_2,
    dsa_q_norm_2, dsa_k_norm_2, nsa_q_norm_2, nsa_k_norm_2, nsa_cmp_pos_2, nsa_cmp_w_2,
    ssd_conv_w_2, ssd_conv_b_2, ssd_dt_bias_2, ssd_a_log_2, ssd_d_2, ssd_norm_g_2, w_br_dsa_2,
    w_br_nsa_2, w_br_ssd_2, w_out_2, norm2_g_2, w_ff1_2, w_ff2_2,
):
    x = first_block(
        x, positions, norm_gains, mla_w_in, mla_q_norm, mla_kv_norm, mla_w_uq, mla_w_ukv,
        mla_w_o, hgrn_w_in, hgrn_lb_logits, hgrn_o_norm, hgrn_w_o, mlp_w1, mlp_w2,
    )
    return second_block(
        x, norm1_g_2, w_in_2, dsa_q_norm_2, dsa_k_norm_2, nsa_q_norm_2, nsa_k_norm_2,
        nsa_cmp_pos_2, nsa_cmp_w_2, ssd_conv_w_2, ssd_conv_b_2, ssd_dt_bias_2, ssd_a_log_2,
        ssd_d_2, ssd_norm_g_2, w_br_dsa_2, w_br_nsa_2, w_br_ssd_2, w_out_2, norm2_g_2, w_ff1_2,
        w_ff2_2,
    )


_drawn_inputs = setup_inputs


def setup_inputs(seed=0):
    import zlib

    import numpy as np

    out = dict(_drawn_inputs(seed))
    spreads = {}
    factors = {'hgrn_lb_logits': 8.0,
     'norm1_g_2': 6.174,
     'dsa_q_norm_2': 8.0,
     'dsa_k_norm_2': 8.0,
     'nsa_q_norm_2': 8.0,
     'nsa_k_norm_2': 8.0,
     'nsa_cmp_pos_2': 8.0,
     'ssd_conv_b_2': 8.0,
     'ssd_d_2': 8.0,
     'ssd_norm_g_2': 8.0,
     'norm2_g_2': 4.874}
    for name, (base, spread) in spreads.items():
        noise = np.random.default_rng([zlib.crc32(name.encode()), seed]).standard_normal(out[name].shape)
        drawn = base * np.exp(spread * noise) if base else spread * noise
        out[name] = jnp.asarray(drawn.astype(out[name].dtype))
    for name, factor in factors.items():
        out[name] = (out[name] * factor).astype(out[name].dtype)
    return out
```

```python
from contextlib import ExitStack

import numpy as np

import concourse.bass as bass
from concourse import mybir

P = 128
F32 = mybir.dt.float32
I32 = mybir.dt.int32
ALU = mybir.AluOpType
ACT = mybir.ActivationFunctionType
AX_X = mybir.AxisListType.X

T = 512
D = 1024
NT = D // P
QT = T // P
RING = 4
BLK = 8
NEG = -1e30
EPS = 1e-6
TAKEN = -float(2 ** 127)
TOPK = 128
MLA_H, MLA_NOPE, MLA_ROPE = 8, 128, 64
MLA_SCALE = float((MLA_NOPE + MLA_ROPE) ** -0.5)
CH = 32
N_CH = T // CH
NCMP = 31
SEL_N = 8
IDX_H = 8
PAIRS = 8
GRPS, HPG = 4, 8

S_AT = [1024, 1024 + 128, 512, 0]
S_LEN = [P * (i + 1) for i in range(QT)]
PT_AT = [0, 512, 1024, 1024 + 256]
PT_LEN = [T - P * k for k in range(QT)]
CAUSAL_AT = [0, 128, 384, 768]

COUNTS = [
    ("mla_in", 7), ("mla_rope", 2), ("mla_heads", 8), ("mla_o", 8),
    ("mlp0_up", 32), ("mlp0_down", 32),
    ("hgrn_heads", 32), ("hgrn_o", 8),
    ("mlp1_up", 32), ("mlp1_down", 32),
    ("dsa_in", 14), ("dsa_out", 16),
    ("nsa_in", 15), ("nsa_cmp", 8), ("nsa_out", 16),
    ("ssd_in", 41), ("ssd_out", 24), ("mix_out", 8),
    ("ff_up", 32), ("ff_down", 32),
]
FIRST = {}
N_BLOCKS = 0
for _name, _n in COUNTS:
    FIRST[_name] = N_BLOCKS
    N_BLOCKS += _n
N_PAD = -N_BLOCKS % RING

COLS = {}
N_COLS = 0
for _name, _n in [
    ("gains", 64), ("q_norm", 4), ("kv_norm", 2), ("lb", 16), ("o_norm", 1),
    ("norm1", 8), ("dsa_q", 1), ("dsa_k", 1), ("nsa_q", 1), ("nsa_k", 3), ("cmp_pos", 64),
    ("conv_w", 96), ("conv_b", 24), ("dt_bias", 1), ("a_log", 1), ("ssd_d", 16), ("ssd_norm", 16),
    ("norm2", 8), ("freq", 1), ("sign", 1),
]:
    COLS[_name] = N_COLS
    N_COLS += _n

TABS = {}
N_TABS = 0
for _name, _n in [
    ("ident", 128), ("ones", 128), ("halves", 128), ("causal", 1280), ("tri", 128), ("chunks", 128),
    ("restart32", 512), ("restart128", 512), ("cmp_bias", 128), ("cmp_seen", 128), ("sel_bias", 32),
    ("before", 64),
]:
    TABS[_name] = N_TABS
    N_TABS += _n


def tables():
    t = np.zeros((P, N_TABS), np.float32)

    def put(name, v):
        v = np.asarray(v, np.float32).reshape(v.shape[0], -1)
        t[:v.shape[0], TABS[name]:TABS[name] + v.shape[1]] = v

    p = np.arange(P)
    put("ident", np.eye(P))
    put("ones", np.ones((P, P)))
    put("halves", (p[:, None] // 64 == p[None] // 64))
    causal = np.zeros((P, 1280), np.float32)
    for i in range(QT):
        k = np.arange(S_LEN[i])
        causal[:, CAUSAL_AT[i]:CAUSAL_AT[i] + S_LEN[i]] = np.where(k[None] <= (P * i + p)[:, None], 0.0, NEG)
    put("causal", causal)
    put("tri", p[None] >= p[:, None])
    put("chunks", (p[:, None] // CH == p[None] // CH) & (p[:, None] <= p[None]))
    tok = np.arange(T)
    put("restart32", np.broadcast_to((tok % 32 != 0), (P, T)))
    put("restart128", np.broadcast_to((tok % 128 != 0), (P, T)))
    q = (P * np.arange(QT)[None, :] + p[:, None])[:, :, None]
    n = np.arange(32)[None, None]
    seen = (16 * n + 31 <= q) & (n < NCMP)
    put("cmp_bias", np.where(n < NCMP, np.where(seen, 0.0, NEG), 2 * NEG))
    put("cmp_seen", seen)
    j = np.arange(SEL_N)[None, None]
    cur = q // 64
    put("sel_bias", np.where((j == cur) | (j == 0), 1e30, np.where(j > cur, NEG, 0.0)))
    a = np.arange(SEL_N)
    put("before", np.broadcast_to((a[None] < a[:, None]).reshape(1, 64), (P, 64)))
    return t


KINDS = ("squared", "summed", "total", "root", "scaled", "added")
NORMS = {
    "norm_0": (8, 8, 1, 1, 8, 0), "q_lora": (4, 4, 1, 1, 4, 0), "kv_lora": (2, 2, 1, 1, 2, 0),
    "mla_o": (8, 10, 1, 1, 0, 8), "norm_1": (8, 8, 1, 1, 8, 0), "mlp0_down": (8, 10, 1, 1, 0, 8),
    "norm_2": (8, 8, 1, 1, 8, 0), "hgrn_o": (8, 10, 1, 1, 0, 8), "norm_3": (8, 8, 1, 1, 8, 0),
    "mlp1_down": (8, 10, 1, 1, 0, 8), "norm_4": (8, 8, 1, 1, 8, 0),
    "dsa_norm": (9, 0, 9, 9, 9, 0), "nsa_norm": (11, 0, 11, 11, 11, 0),
    "ssd_norm": (16, 16, 1, 1, 16, 0), "norm_5": (8, 8, 1, 1, 8, 0),
}


class Memory:

    def __init__(self, nc, ctx):
        def sb(name, *free, dt=F32):
            return ctx.enter_context(nc.sbuf_tensor(name, [P, *free], dt))

        self.sem_of = {}
        self.new_sem = lambda name: ctx.enter_context(nc.semaphore(name))
        self.ring = sb("ring", RING, BLK * P)
        self.tab = sb("tab", N_TABS)
        self.col = sb("col", N_COLS)
        self.h = sb("h", NT, T)
        self.a = sb("a", NT, T)
        self.m = sb("m", NT, T)
        self.big = sb("big", 32, T)
        self.sq = sb("sq", 2, T)
        self.ssum = sb("ssum", T)
        self.std = sb("std", T)
        self.rstd = sb("rstd", T)
        self.extra = sb("extra", 4, T)
        self.work = sb("work", 10752)
        self.ps = ctx.enter_context(nc.psum_tensor("ps", [P, 8 * T], F32))

    def sem(self, name):
        if name not in self.sem_of:
            self.sem_of[name] = self.new_sem(name)
        return self.sem_of[name]

    def past(self, name, kind):
        names = list(NORMS)
        return sum(NORMS[n][KINDS.index(kind)] for n in names[:names.index(name)])

    def bank(self, b, rows=slice(0, P)):
        return self.ps[rows, b * T:(b + 1) * T]

    def t(self, name, n, rows=slice(0, P), at=0):
        return self.tab[rows, TABS[name] + at:TABS[name] + at + n]

    def c(self, name, k=0, rows=slice(0, P)):
        return self.col[rows, COLS[name] + k:COLS[name] + k + 1]

    def carve(self, at, *free):
        n = int(np.prod(free))
        v = self.work[:, at:at + n]
        assert at + n <= 10752, (at, free)
        if len(free) == 2:
            v = v.rearrange("p (a b) -> p a b", a=free[0])
        if len(free) == 3:
            v = v.rearrange("p (a b c) -> p a b c", a=free[0], b=free[1])
        return v, at + n



def stream_weights(sp, M, wall, blocks):
    for u in range(RING):
        sp.dma_start(M.ring[:, u, :], wall[u]).then_inc(M.sem(f"weights_in{u}"), 16)
    with sp.Fori(0, (blocks + RING - 1) // RING - 1) as i:
        for u in range(RING):
            sp.wait_ge(M.sem("blocks_used"), i * RING + (u + 1))
            src = wall[bass.ds(i * RING + (RING + u), 1), :, :].rearrange("a p n -> (a p) n")
            sp.dma_start(M.ring[:, u, :], src).then_inc(M.sem(f"weights_in{u}"), 16)
    for u in range(RING):
        sp.wait_ge(M.sem(f"weights_in{u}"), 16 * ((blocks + RING - 1) // RING))


def block_tile(M, b, j):
    return M.ring[:, b % RING, j * P:(j + 1) * P]


def wait_block(pe, M, b, i=None, step=0):
    need = 16 * (b // RING + 1)
    pe.wait_ge(M.sem(f"weights_in{b % RING}"), need if i is None else i * (16 * step // RING) + need)


def gemm_pe(pe, M, name, tiles, per_tile, rhs, unroll, banks=4, looped=True):
    used, free = M.sem("blocks_used"), M.sem(f"{name}_free")

    def tile(i, u):
        pe.wait_ge(free, u + 1 if i is None else i * unroll + (u + 1))
        for blk in range(per_tile):
            b = FIRST[name] + u * per_tile + blk
            wait_block(pe, M, b, i, unroll * per_tile)
            for k in range(BLK):
                kk = blk * BLK + k
                mm = pe.matmul(M.bank(u % banks), block_tile(M, b, k), rhs(kk),
                               start=(kk == 0), stop=(kk == per_tile * BLK - 1))
            mm.then_inc(used, 1)

    if looped:
        with pe.Fori(0, tiles // unroll) as i:
            for u in range(unroll):
                tile(i, u)
    else:
        for u in range(tiles):
            tile(None, u)


def gemm_out(eng, M, name, tiles, per_tile, unroll, banks, move, looped=True):
    used, free = M.sem("blocks_used"), M.sem(f"{name}_free")
    eng.drain().then_inc(free, banks)

    def tile(i, u):
        done = FIRST[name] + (u + 1) * per_tile
        eng.wait_ge(used, done if i is None else i * (unroll * per_tile) + done)
        move(u if i is None else i * unroll + u, u).then_inc(free, 1)

    if looped:
        with eng.Fori(0, tiles // unroll) as i:
            for u in range(unroll):
                tile(i, u)
    else:
        for u in range(tiles):
            tile(None, u)


def gemm_ready(eng, M, name, tiles, banks):
    eng.wait_ge(M.sem(f"{name}_free"), banks + tiles)



def norm_act(act, M, name, src, n, dim):
    for k in range(n):
        if k >= 2:
            act.wait_ge(M.sem("norm_summed"), k - 1 + M.past(name, "summed"))
        act.activation(M.sq[:, k % 2, :], src(k), ACT.Square).then_inc(M.sem("norm_squared"), 1)
    norm_act_root(act, M, name, dim)


def norm_act_root(act, M, name, dim):
    act.wait_ge(M.sem("norm_total"), 1 + M.past(name, "total"))
    act.activation(M.std[:, :], M.bank(7), ACT.Sqrt, bias=M.eps, scale=1.0 / dim)\
       .then_inc(M.sem("norm_root"), 1)


def norm_pe(pe, M, name, n, table="ones"):
    pe.wait_ge(M.sem("norm_summed"), n + M.past(name, "summed"))
    pe.matmul(M.bank(7), M.t(table, P), M.ssum[:, :], start=True, stop=True)\
      .then_inc(M.sem("norm_total"), 1)


def norm_dve(dve, M, name, n):
    for k in range(n):
        dve.wait_ge(M.sem("norm_squared"), k + 1 + M.past(name, "squared"))
        if k == 0:
            dve.tensor_copy(M.ssum[:, :], M.sq[:, 0, :]).then_inc(M.sem("norm_summed"), 1)
        else:
            dve.drain()
            dve.tensor_tensor(M.ssum[:, :], M.ssum[:, :], M.sq[:, k % 2, :], ALU.add)\
               .then_inc(M.sem("norm_summed"), 1)
    norm_dve_root(dve, M, name)


def norm_dve_root(dve, M, name):
    dve.wait_ge(M.sem("norm_root"), 1 + M.past(name, "root"))
    dve.reciprocal(M.rstd[:, :], M.std[:, :])
    dve.drain()


def scale_dve(dve, M, name, src, dst, gain, n):
    for k in range(n):
        dve.scalar_tensor_tensor(out=dst(k), in0=src(k), scalar=gain(k), in1=M.rstd[:, :],
                                 op0=ALU.mult, op1=ALU.mult).then_inc(M.sem("norm_scaled"), 1)


def add_norm_dve(dve, M, name, gain):
    for k in range(NT):
        dve.scalar_tensor_tensor(out=M.m[:, k, :], in0=M.m[:, k, :], scalar=gain(k),
                                 in1=M.rstd[:, :], op0=ALU.mult, op1=ALU.mult)
        dve.drain()
        dve.tensor_tensor(M.h[:, k, :], M.h[:, k, :], M.m[:, k, :], ALU.add)\
           .then_inc(M.sem("norm_added"), 1)



def att_scores_pe(pe, M, A, terms):
    for i in range(QT):
        for n, (q, k) in enumerate(terms):
            mm = pe.matmul(M.ps[:, S_AT[i]:S_AT[i] + S_LEN[i]], q[:, i * P:(i + 1) * P],
                           k[:, 0:S_LEN[i]], start=(n == 0), stop=(n == len(terms) - 1))
    mm.then_inc(M.sem(f"{A}_scores"), 1)


def att_mask_dve(dve, M, A, V, n, base, mask, scale):
    dve.wait_ge(M.sem(f"{A}_scores"), base + (n + 1))
    dve.memset(V.inv[:, n % 2, :], 0.0)
    for i in range(QT):
        s = V.p[n % 2][:, CAUSAL_AT[i]:CAUSAL_AT[i] + S_LEN[i]]
        dve.tensor_tensor_reduce(s, M.ps[:, S_AT[i]:S_AT[i] + S_LEN[i]], mask(i), scale, -3.0e38,
                                 ALU.add, ALU.max, V.top[:, n % 2, i:i + 1])
    dve.drain()
    dve.tensor_scalar(V.ntop[:, n % 2, :], V.top[:, n % 2, :], -1.0, None, ALU.mult)\
       .then_inc(M.sem(f"{A}_masked"), 1)


def att_exp_act(act, M, A, V, n, base):
    act.wait_ge(M.sem(f"{A}_masked"), base + (n + 1))
    for i in range(QT):
        s = V.p[n % 2][:, CAUSAL_AT[i]:CAUSAL_AT[i] + S_LEN[i]]
        e = act.activation(s, s, ACT.Exp, bias=V.ntop[:, n % 2, i:i + 1], scale=1.0,
                           accum_out=V.sum[:, n % 2, i:i + 1])
    e.then_inc(M.sem(f"{A}_exp"), 1)


def att_divide_dve(dve, M, A, V, n, base, gate=None):
    dve.wait_ge(M.sem(f"{A}_exp"), base + (n + 1))
    dve.reciprocal(V.inv[:, n % 2, :], V.sum[:, n % 2, :])
    dve.drain()
    if gate is not None:
        dve.tensor_tensor(V.inv[:, n % 2, :], V.inv[:, n % 2, :], gate, ALU.mult)
        dve.drain()
    for i in range(QT):
        s = V.p[n % 2][:, CAUSAL_AT[i]:CAUSAL_AT[i] + S_LEN[i]]
        d = dve.tensor_scalar(s, s, V.inv[:, n % 2, i:i + 1], None, ALU.mult)
    d.then_inc(M.sem(f"{A}_probs"), 1)


def att_turn_pe(pe, M, A, V, n, base):
    pe.wait_ge(M.sem(f"{A}_probs"), base + (n + 1))
    for k in range(QT):
        for i in range(k, QT):
            at = 3 * T + PT_AT[k] + (i - k) * P
            s = V.p[n % 2][:, CAUSAL_AT[i] + k * P:CAUSAL_AT[i] + (k + 1) * P]
            mm = pe.transpose(M.ps[:, at:at + P], s, M.t("ident", P))
    mm.then_inc(M.sem(f"{A}_turned"), 1)


def att_turned_act(act, M, A, V, n, base):
    act.wait_ge(M.sem(f"{A}_turned"), base + (n + 1))
    for at, n_col in ((0, 512), (512, 384), (1024, 384)):
        c = act.activation(V.pt[:, at:at + n_col], M.ps[:, 3 * T + at:3 * T + at + n_col], ACT.Copy)
    c.then_inc(M.sem(f"{A}_kept"), 1)


def att_out_pe(pe, M, A, V, n, base, values, bank, rows=slice(0, P)):
    pe.wait_ge(M.sem(f"{A}_kept"), base + (n + 1))
    for k in range(QT):
        mm = pe.matmul(M.ps[rows, bank * T + k * P:(bank + 1) * T], values(k),
                       V.pt[:, PT_AT[k]:PT_AT[k] + PT_LEN[k]], start=(k == 0), stop=(k == QT - 1))
    mm.then_inc(M.sem(f"{A}_out"), 1)


class AttView:

    def __init__(self, M, at):
        p0, at = M.carve(at, 1280)
        p1, at = M.carve(at, 1280)
        self.p = [p0, p1]
        self.pt, at = M.carve(at, 1408)
        self.top, at = M.carve(at, 2, QT)
        self.ntop, at = M.carve(at, 2, QT)
        self.sum, at = M.carve(at, 2, QT)
        self.inv, at = M.carve(at, 2, QT)
        self.end = at


def tile_at(buf, t):
    if isinstance(t, int):
        return buf[:, t, :]
    return buf[:, bass.ds(t, 1), :].rearrange("p a b -> p (a b)")



def to_m_act(act, M, name, per_tile, unroll, banks):
    squared, summed = M.sem("norm_squared"), M.sem("norm_summed")

    def move(t, u):
        act.wait_ge(summed, t + (1 + M.past(name, "summed")))
        act.activation(M.sq[:, u % 2, :], M.bank(u % banks), ACT.Square).then_inc(squared, 1)
        return act.activation(tile_at(M.m, t), M.bank(u % banks), ACT.Copy)

    gemm_out(act, M, name, NT, per_tile, unroll, banks, move)
    norm_act_root(act, M, name, D)


def to_m_dve(dve, M, name):
    squared, summed = M.sem("norm_squared"), M.sem("norm_summed")
    dve.memset(M.ssum[:, :], 0.0)
    dve.drain().then_inc(summed, 2)
    with dve.Fori(0, NT // 2) as i:
        for u in range(2):
            dve.wait_ge(squared, i * 2 + (u + 1) + M.past(name, "squared"))
            dve.tensor_tensor(M.ssum[:, :], M.ssum[:, :], M.sq[:, u, :], ALU.add)
            dve.drain().then_inc(summed, 1)
    norm_dve_root(dve, M, name)



class Mla:
    def __init__(self, M):
        b = M.big
        self.proj = b[:, 0:7, :]
        self.qr = b[:, 7:11, :]
        self.cos, self.sin = b[:, 11, :], b[:, 12, :]
        self.krz = b[:, 13:15, :]
        self.q, self.k, self.v = b[:, 15:17, :], b[:, 17:19, :], b[:, 19:21, :]
        self.ra, self.rb = b[:, 21, :], b[:, 22, :]
        self.pos = b[:, 23, :].bitcast(I32)
        self.angle, self.turns, self.rest = b[:, 24, :], b[:, 25, :], b[:, 26, :]
        self.att = AttView(M, 0)


TURN = float(2 * np.pi)
TURN_1 = 6.28125
TURN_2 = float(np.float32(np.round((TURN - TURN_1) * 2 ** 20) / 2 ** 20))
TURN_3 = float(TURN - TURN_1 - TURN_2)
ROUND = 12582912.0
PI = 3.1415925


def rope_angles_dve(dve, M, R):
    dve.wait_ge(M.sem("positions_in"), 16)
    dve.wait_ge(M.sem("tables_in"), 32)
    dve.tensor_copy(R.rest, R.pos)
    dve.drain()
    dve.tensor_scalar(R.angle, R.rest, M.c("freq"), None, ALU.mult)
    dve.drain()
    for out, quarter in ((R.ra, 0.0), (R.rb, 0.25)):
        dve.tensor_scalar(R.turns, R.angle, 1.0 / TURN, quarter, ALU.mult, ALU.add)
        dve.drain()
        dve.tensor_scalar(R.turns, R.turns, ROUND, ROUND, ALU.add, ALU.subtract)
        dve.drain()
        dve.scalar_tensor_tensor(out=R.rest, in0=R.turns, scalar=-TURN_1, in1=R.angle, op0=ALU.mult, op1=ALU.add)
        dve.drain()
        dve.scalar_tensor_tensor(out=R.rest, in0=R.turns, scalar=-TURN_2, in1=R.rest, op0=ALU.mult, op1=ALU.add)
        dve.drain()
        dve.scalar_tensor_tensor(out=R.rest, in0=R.turns, scalar=-TURN_3, in1=R.rest, op0=ALU.mult, op1=ALU.add)
        dve.drain()
        dve.tensor_scalar(R.rest, R.rest, quarter * TURN, PI, ALU.add, ALU.min)
        dve.drain()
        dve.tensor_scalar(out, R.rest, -PI, None, ALU.max)
        dve.drain()
    dve.nop().then_inc(M.sem("rope_angles"), 1)


def rope_tables_act(act, M, R):
    act.wait_ge(M.sem("rope_angles"), 1)
    act.activation(R.sin, R.ra, ACT.Sin)
    act.activation(R.cos, R.rb, ACT.Sin)
    act.drain().then_inc(M.sem("rope_waves"), 1)


def rope_sign_dve(dve, M, R):
    dve.wait_ge(M.sem("rope_waves"), 1)
    dve.tensor_scalar(R.sin, R.sin, M.c("sign"), None, ALU.mult)
    dve.memset(R.krz, 0.0)
    dve.drain()


def rope_swap_act(act, R, src):
    act.activation(R.ra, src, ACT.Copy)
    for g in range(4):
        o = 32 * (g ^ 1)
        act.activation(R.rb[o:o + 32, :], src[32 * g:32 * g + 32, :], ACT.Copy)
    return act.drain()


def rope_turn_dve(dve, R, dst):
    dve.tensor_tensor(R.ra, R.ra, R.cos, ALU.mult)
    dve.tensor_tensor(R.rb, R.rb, R.sin, ALU.mult)
    dve.drain()
    for rows, out in dst:
        dve.tensor_tensor(out, R.ra[rows, :], R.rb[rows, :], ALU.add)
    return dve.drain()


def mla_pe(pe, M, R):
    gemm_pe(pe, M, "mla_in", 7, 1, lambda k: M.a[:, k, :], 7, looped=False)
    norm_pe(pe, M, "q_lora", 4)
    norm_pe(pe, M, "kv_lora", 2)
    pe.wait_ge(M.sem("norm_scaled"), 4 + M.past("q_lora", "scaled"))
    for pair in range(4):
        b, at = FIRST["mla_rope"] + pair // 2, 4 * (pair % 2)
        if pair % 2 == 0:
            wait_block(pe, M, b)
        for k in range(4):
            mm = pe.matmul(M.bank(pair), block_tile(M, b, at + k), R.proj[:, k, :], start=(k == 0), stop=(k == 3))
        if pair % 2:
            mm.then_inc(M.sem("blocks_used"), 1)
    pe.wait_ge(M.sem("norm_scaled"), 2 + M.past("kv_lora", "scaled"))
    pe.wait_ge(M.sem("rope_read"), 5)

    def head(h):
        b = FIRST["mla_heads"] + h
        wait_block(pe, M, b)
        for k in range(4):
            pe.matmul(M.bank(0), block_tile(M, b, k), R.proj[:, k, :], start=(k == 0), stop=(k == 3))
        for k in range(2):
            pe.matmul(M.bank(1), block_tile(M, b, 4 + k), R.proj[:, 4 + k, :], start=(k == 0), stop=(k == 1))
        for t in range(QT):
            for k in range(2):
                mm = pe.matmul(M.bank(2)[:, t * P:(t + 1) * P], R.proj[:, 4 + k, t * P:(t + 1) * P],
                               block_tile(M, b, 6 + k), start=(k == 0), stop=(k == 1))
        mm.then_inc(M.sem("blocks_used"), 1)

    def scores(h):
        pe.wait_ge(M.sem("mla_heads_free"), h + 1)
        if h == 0:
            pe.wait_ge(M.sem("rope_turned"), 5)
        half = slice(0, P)
        att_scores_pe(pe, M, "mla", [(R.q[:, h % 2, :], R.k[:, h % 2, :]),
                                     (R.qr[half, h // 2, :], R.krz[:, h % 2, :])])

    head(0)
    scores(0)
    for h in range(MLA_H):
        if h + 1 < MLA_H:
            pe.wait_ge(M.sem("mla_masked"), h + 1)
            head(h + 1)
        att_turn_pe(pe, M, "mla", R.att, h, 0)
        if h + 1 < MLA_H:
            scores(h + 1)
        att_out_pe(pe, M, "mla", R.att, h, 0, lambda k: R.v[:, h % 2, k * P:(k + 1) * P], 6)
    gemm_ready(pe, M, "mla_y", MLA_H, 0)
    gemm_pe(pe, M, "mla_o", NT, 1, lambda k: M.a[:, k, :], 4)
    norm_pe(pe, M, "mla_o", NT + 2)


def mla_act(act, M, R):
    rope_tables_act(act, M, R)
    gemm_out(act, M, "mla_in", 7, 1, 7, 4,
             lambda t, u: act.activation(R.proj[:, t, :], M.bank(u % 4), ACT.Copy), looped=False)
    act.drain()
    norm_act(act, M, "q_lora", lambda k: R.proj[:, k, :], 4, 512)
    norm_act(act, M, "kv_lora", lambda k: R.proj[:, 4 + k, :], 2, 256)
    act.wait_ge(M.sem("norm_scaled"), 2 + M.past("kv_lora", "scaled"))
    rope_swap_act(act, R, R.proj[:, 6, :]).then_inc(M.sem("rope_read"), 1)
    for pair in range(4):
        act.wait_ge(M.sem("blocks_used"), FIRST["mla_rope"] + pair // 2 + 1)
        act.wait_ge(M.sem("rope_turned"), pair + 1)
        rope_swap_act(act, R, M.bank(pair)).then_inc(M.sem("rope_read"), 1)

    def head(h):
        act.wait_ge(M.sem("blocks_used"), FIRST["mla_heads"] + h + 1)
        act.activation(R.q[:, h % 2, :], M.bank(0), ACT.Copy)
        act.activation(R.k[:, h % 2, :], M.bank(1), ACT.Copy)
        act.activation(R.v[:, h % 2, :], M.bank(2), ACT.Copy)
        act.drain().then_inc(M.sem("mla_heads_free"), 1)

    head(0)
    att_exp_act(act, M, "mla", R.att, 0, 0)
    for h in range(MLA_H):
        if h + 1 < MLA_H:
            head(h + 1)
        att_turned_act(act, M, "mla", R.att, h, 0)
        if h + 1 < MLA_H:
            att_exp_act(act, M, "mla", R.att, h + 1, 0)
        act.wait_ge(M.sem("mla_out"), h + 1)
        act.activation(M.a[:, h, :], M.bank(6), ACT.Copy).then_inc(M.sem("mla_y_free"), 1)
    to_m_act(act, M, "mla_o", 1, 4, 4)


def mla_dve(dve, M, R):
    rope_sign_dve(dve, M, R)
    norm_dve(dve, M, "q_lora", 4)
    scale_dve(dve, M, "q_lora", lambda k: R.proj[:, k, :], lambda k: R.proj[:, k, :], lambda k: M.c("q_norm", k), 4)
    norm_dve(dve, M, "kv_lora", 2)
    scale_dve(dve, M, "kv_lora", lambda k: R.proj[:, 4 + k, :], lambda k: R.proj[:, 4 + k, :],
              lambda k: M.c("kv_norm", k), 2)
    lower, upper = slice(0, 64), slice(64, P)
    for n in range(5):
        dve.wait_ge(M.sem("rope_read"), n + 1)
        if n == 0:
            dst = [(lower, R.krz[lower, 0, :]), (upper, R.krz[upper, 1, :])]
        else:
            dst = [(slice(0, P), R.qr[:, n - 1, :])]
        rope_turn_dve(dve, R, dst).then_inc(M.sem("rope_turned"), 1)
    mask = lambda i: M.t("causal", S_LEN[i], at=CAUSAL_AT[i])
    att_mask_dve(dve, M, "mla", R.att, 0, 0, mask, MLA_SCALE)
    for h in range(MLA_H):
        att_divide_dve(dve, M, "mla", R.att, h, 0)
        if h + 1 < MLA_H:
            att_mask_dve(dve, M, "mla", R.att, h + 1, 0, mask, MLA_SCALE)
    to_m_dve(dve, M, "mla_o")
    add_norm_dve(dve, M, "mla_o", lambda k: M.c("gains", 8 + k))



def mlp_pe(pe, M, name):
    up, down = f"{name}_up", f"{name}_down"
    gemm_pe(pe, M, up, 32, 1, lambda k: M.a[:, k, :], 4)
    pe.wait_ge(M.sem(f"{name}_hidden"), 32)
    gemm_pe(pe, M, down, NT, 4, lambda k: M.big[:, k, :], 2, banks=2)
    norm_pe(pe, M, down, NT + 2)


def mlp_act(act, M, name):
    gemm_out(act, M, f"{name}_up", 32, 1, 4, 4,
             lambda t, u: act.activation(tile_at(M.big, t), M.bank(u % 4), ACT.Relu))
    to_m_act(act, M, f"{name}_down", 4, 2, 2)


def mlp_dve(dve, M, name, gain):
    with dve.Fori(0, 8) as i:
        for u in range(4):
            dve.wait_ge(M.sem(f"{name}_up_free"), i * 4 + (u + 5))
            r = tile_at(M.big, i * 4 + u)
            dve.tensor_tensor(r, r, r, ALU.mult).then_inc(M.sem(f"{name}_hidden"), 1)
    to_m_dve(dve, M, f"{name}_down")
    add_norm_dve(dve, M, f"{name}_down", gain)



class Hgrn:
    def __init__(self, M):
        b = M.big
        (self.sq, self.sf, self.sg, self.v, self.k, self.logf, self.b, self.d_ref, self.d_last,
         self.e_ref, self.e_neg, self.e_b, self.e_last, self.masked) = [b[:, n, :] for n in range(14)]
        self.f = b[:, 14, :]
        self.q_rel, self.k_rel, self.q_dec, self.k_dec = [b[:, n, :] for n in range(15, 19)]
        self.gate = b[:, 19, :]
        self.norm = b[:, 20, :]
        self.y = b[:, 24:32, :]
        self.kz, at = M.carve(0, 4, T)
        self.state, at = M.carve(at, N_CH, P)
        self.lb, at = M.carve(at, 8)
        self.one_lb, at = M.carve(at, 8)
        self.tmp, at = M.carve(at, 5, 8)


def hgrn_bounds_act(act, M, R):
    act.wait_ge(M.sem("hg_logits"), 1)
    act.activation(R.tmp[:, 1:3, :], R.tmp[:, 1:3, :], ACT.Exp).then_inc(M.sem("hg_logits_exp"), 1)


def hgrn_bounds_dve(dve, M, R):
    l0 = M.col[:, COLS["lb"]:COLS["lb"] + 8]
    l1 = M.col[:, COLS["lb"] + 8:COLS["lb"] + 16]
    t = [R.tmp[:, n, :] for n in range(5)]
    dve.tensor_tensor(t[0], l0, l1, ALU.max)
    dve.drain()
    dve.tensor_tensor(t[1], l0, t[0], ALU.subtract)
    dve.tensor_tensor(t[2], l1, t[0], ALU.subtract)
    dve.drain().then_inc(M.sem("hg_logits"), 1)
    dve.wait_ge(M.sem("hg_logits_exp"), 1)
    dve.tensor_tensor(t[3], t[1], t[2], ALU.add)
    dve.drain()
    dve.reciprocal(t[4], t[3])
    dve.drain()
    dve.tensor_tensor(t[1], t[1], t[4], ALU.mult)
    dve.tensor_tensor(t[2], t[2], t[4], ALU.mult)
    dve.drain()
    dve.tensor_tensor(t[2], t[2], t[1], ALU.add)
    dve.drain()
    dve.tensor_tensor(R.lb, t[2], t[1], ALU.subtract)
    dve.drain()
    dve.tensor_scalar(R.one_lb, R.lb, -1.0, 1.0, ALU.mult, ALU.add)
    dve.memset(R.kz, 0.0)
    dve.memset(R.masked, 0.0)
    dve.drain()


def hgrn_pe(pe, M, R):
    used = M.sem("blocks_used")

    def project(j, i, ahead):
        b = FIRST["hgrn_heads"] + 4 * ahead + j
        wait_block(pe, M, b, i, 4)
        if ahead:
            pe.wait_ge(M.sem("hg_banks_free"), i + 1)
        if j != 2:
            for k in range(BLK):
                mm = pe.matmul(M.bank(j), block_tile(M, b, k), M.a[:, k, :], start=(k == 0), stop=(k == 7))
        else:
            for t in range(QT):
                for k in range(BLK):
                    mm = pe.matmul(M.bank(2)[:, t * P:(t + 1) * P], M.a[:, k, t * P:(t + 1) * P],
                                   block_tile(M, b, k), start=(k == 0), stop=(k == 7))
        mm.then_inc(used, 1)

    def states(tt, bank):
        for r in range(4):
            mm = pe.matmul(M.bank(bank)[:, r * P:(r + 1) * P], R.kz[:, r, tt * P:(tt + 1) * P],
                           R.v[:, tt * P:(tt + 1) * P], start=True, stop=True)
        mm.then_inc(M.sem("hg_chunk_states"), 1)

    def head(i, nxt):
        if nxt:
            project(0, i, 1)
            project(1, i, 1)
        pe.wait_ge(M.sem("hg_rel"), i + 1)
        for t in range(QT):
            s = slice(t * P, (t + 1) * P)
            mm = pe.matmul(M.bank(4)[:, s], R.k_rel[:, s], R.q_rel[:, s], start=True, stop=True)
        mm.then_inc(M.sem("hg_pairs"), 1)
        pe.wait_ge(M.sem("hg_dec"), i + 1)
        for t in range(QT):
            s = slice(t * P, (t + 1) * P)
            mm = pe.transpose(M.bank(5)[:, s], R.k_dec[:, s], M.t("ident", P))
        mm.then_inc(M.sem("hg_keys_turned"), 1)
        if nxt:
            project(2, i, 1)
        pe.wait_ge(M.sem("hg_keys_kept"), i + 1)
        states(0, 6)
        states(1, 5)
        pe.wait_ge(M.sem("hg_chained"), i * 4 + 1)
        states(2, 6)
        pe.wait_ge(M.sem("hg_chained"), i * 4 + 2)
        states(3, 5)
        if nxt:
            project(3, i, 1)
        pe.wait_ge(M.sem("hg_chained"), i * 4 + 4)
        pe.wait_ge(M.sem("hg_pairs_masked"), i + 1)
        for t in range(QT):
            s = slice(t * P, (t + 1) * P)
            pe.matmul(M.bank(4)[:, s], R.v[:, s], R.masked[:, s], start=(t == 0), stop=False,
                      skip_group_check=True)
            for r in range(4):
                c = 4 * t + r
                w = slice(c * CH, (c + 1) * CH)
                mm = pe.matmul(M.bank(4)[:, w], R.state[:, c, :], R.q_dec[:, w], start=False, stop=(c == N_CH - 1),
                               skip_group_check=True)
        mm.then_inc(M.sem("hg_out"), 1)
        pe.wait_ge(M.sem("hg_squared"), i + 1)
        pe.matmul(M.bank(7), M.t("ones", P), M.sq[:, 0, :], start=True, stop=True).then_inc(M.sem("hg_total"), 1)

    for j in range(4):
        project(j, 0, 0)
    with pe.Fori(0, MLA_H - 1) as i:
        head(i, True)
    head(7, False)
    pe.wait_ge(M.sem("hg_y"), 8)
    gemm_pe(pe, M, "hgrn_o", NT, 1, lambda k: R.y[:, k, :], 4)
    norm_pe(pe, M, "hgrn_o", NT + 2)


def hgrn_act(act, M, R):
    hgrn_bounds_act(act, M, R)
    with act.Fori(0, 8) as i:
        act.wait_ge(M.sem("blocks_used"), i * 4 + FIRST["hgrn_heads"] + 4)
        act.activation(R.sf, M.bank(1), ACT.Sigmoid).then_inc(M.sem("hg_sig"), 1)
        act.activation(R.sq, M.bank(0), ACT.Sigmoid).then_inc(M.sem("hg_sig"), 1)
        act.activation(R.sg, M.bank(3), ACT.Sigmoid).then_inc(M.sem("hg_sig"), 1)
        act.activation(R.v, M.bank(2), ACT.Copy).then_inc(M.sem("hg_sig"), 1)
        act.wait_ge(M.sem("hg_f"), i + 1)
        act.activation(R.logf, R.f, ACT.Ln).then_inc(M.sem("hg_logf"), 1)
        act.wait_ge(M.sem("hg_diffs"), i + 1)
        act.activation(R.e_ref, R.d_ref, ACT.Exp).then_inc(M.sem("hg_exp"), 1)
        act.activation(R.e_neg, R.d_ref, ACT.Exp, scale=-1.0).then_inc(M.sem("hg_exp"), 1)
        act.activation(R.e_last, R.d_last, ACT.Exp).then_inc(M.sem("hg_exp"), 1)
        act.activation(R.e_b, R.b, ACT.Exp).then_inc(M.sem("hg_exp"), 1)
        act.wait_ge(M.sem("hg_keys_turned"), i + 1)
        for r in range(4):
            rows = slice(32 * r, 32 * r + 32)
            act.activation(R.kz[rows, r, :], M.bank(5, rows), ACT.Copy)
        act.drain().then_inc(M.sem("hg_keys_kept"), 1)
        act.wait_ge(M.sem("hg_out"), i + 1)
        act.activation(M.sq[:, 0, :], M.bank(4), ACT.Square).then_inc(M.sem("hg_squared"), 1)
        act.wait_ge(M.sem("hg_total"), i + 1)
        act.activation(M.std[:, :], M.bank(7), ACT.Sqrt, bias=M.eps, scale=1.0 / P).then_inc(M.sem("hg_root"), 1)
    to_m_act(act, M, "hgrn_o", 1, 4, 4)


def hgrn_dve(dve, M, R):
    hgrn_bounds_dve(dve, M, R)
    chunks = lambda x: x.rearrange("p (c t) -> p c t", t=CH)
    mask = M.t("chunks", P).bitcast(I32).unsqueeze(1).broadcast_to([P, QT, P])
    with dve.Fori(0, 8) as i:
        dve.wait_ge(M.sem("hg_sig"), i * 4 + 1)
        dve.tensor_scalar(R.f, R.sf, R.one_lb[:, bass.ds(i, 1)], R.lb[:, bass.ds(i, 1)], ALU.mult, ALU.add)
        dve.drain().then_inc(M.sem("hg_f"), 1)
        dve.tensor_scalar(R.k, R.f, -1.0, 1.0, ALU.mult, ALU.add)
        dve.wait_ge(M.sem("hg_sig"), i * 4 + 4)
        dve.tensor_tensor(R.sq, R.sq, M.bank(0), ALU.mult)
        dve.tensor_tensor(R.gate, R.sg, M.bank(3), ALU.mult)
        dve.drain().then_inc(M.sem("hg_banks_free"), 1)
        dve.wait_ge(M.sem("hg_logf"), i + 1)
        dve.tensor_tensor_scan(R.b, M.t("restart32", T), R.logf, 0.0, ALU.mult, ALU.add)
        dve.drain()
        b = chunks(R.b)
        dve.tensor_tensor(chunks(R.d_ref), b, b[:, :, 16:17].broadcast_to([P, N_CH, CH]), ALU.subtract)
        dve.tensor_tensor(chunks(R.d_last), b[:, :, 31:32].broadcast_to([P, N_CH, CH]), b, ALU.subtract)
        dve.drain().then_inc(M.sem("hg_diffs"), 1)
        dve.wait_ge(M.sem("hg_exp"), i * 4 + 2)
        dve.tensor_tensor(R.q_rel, R.sq, R.e_ref, ALU.mult)
        dve.tensor_tensor(R.k_rel, R.k, R.e_neg, ALU.mult)
        dve.drain().then_inc(M.sem("hg_rel"), 1)
        dve.wait_ge(M.sem("hg_exp"), i * 4 + 4)
        dve.tensor_tensor(R.k_dec, R.k, R.e_last, ALU.mult)
        dve.tensor_tensor(R.q_dec, R.sq, R.e_b, ALU.mult)
        dve.drain().then_inc(M.sem("hg_dec"), 1)
        dve.wait_ge(M.sem("hg_pairs"), i + 1)
        dve.memset(R.state[:, 0, :], 0.0)
        dve.copy_predicated(R.masked.rearrange("p (a b) -> p a b", a=QT), mask,
                            M.bank(4).rearrange("p (a b) -> p a b", a=QT))
        dve.drain().then_inc(M.sem("hg_pairs_masked"), 1)
        for t in range(QT):
            dve.wait_ge(M.sem("hg_chunk_states"), i * 4 + (t + 1))
            for r in range(4):
                c = 4 * t + r
                if c == N_CH - 1:
                    continue
                dve.scalar_tensor_tensor(out=R.state[:, c + 1, :], in0=R.state[:, c, :],
                                         scalar=R.e_b[:, c * CH + 31:c * CH + 32],
                                         in1=M.bank(6 - t % 2)[:, r * P:(r + 1) * P], op0=ALU.mult, op1=ALU.add)
                dve.drain()
            dve.nop().then_inc(M.sem("hg_chained"), 1)
        dve.wait_ge(M.sem("hg_root"), i + 1)
        dve.reciprocal(M.rstd[:, :], M.std[:, :])
        dve.drain()
        dve.scalar_tensor_tensor(out=R.norm, in0=M.bank(4), scalar=M.c("o_norm"), in1=M.rstd[:, :],
                                 op0=ALU.mult, op1=ALU.mult)
        dve.drain()
        dve.tensor_tensor(tile_at(R.y, i), R.norm, R.gate, ALU.mult).then_inc(M.sem("hg_y"), 1)
    to_m_dve(dve, M, "hgrn_o")
    add_norm_dve(dve, M, "hgrn_o", lambda k: M.c("gains", 40 + k))



LOWER, UPPER = slice(0, 64), slice(64, P)
HALVES = (LOWER, UPPER)
SCALE_64 = 0.125


def head_norms_pe(pe, M, name, n):
    for k in range(n):
        pe.wait_ge(M.sem("norm_squared"), k + 1 + M.past(name, "squared"))
        if k:
            pe.wait_ge(M.sem("norm_root"), k + M.past(name, "root"))
        pe.matmul(M.bank(7), M.t("halves", P), M.sq[:, k % 2, :], start=True, stop=True)\
          .then_inc(M.sem("norm_total"), 1)


def head_norms_act(act, M, name, srcs, cols=T):
    for k, src in enumerate(srcs):
        if k >= 2:
            act.wait_ge(M.sem("norm_total"), k - 1 + M.past(name, "total"))
        act.activation(M.sq[:, k % 2, 0:cols], src, ACT.Square).then_inc(M.sem("norm_squared"), 1)
        if k >= 1:
            head_root_act(act, M, name, k - 1, cols)
    head_root_act(act, M, name, len(srcs) - 1, cols)


def head_root_act(act, M, name, k, cols):
    act.wait_ge(M.sem("norm_total"), k + 1 + M.past(name, "total"))
    if k:
        act.wait_ge(M.sem("norm_scaled"), k + M.past(name, "scaled"))
    act.activation(M.std[:, 0:cols], M.bank(7)[:, 0:cols], ACT.Sqrt, bias=M.eps, scale=1.0 / 64)\
       .then_inc(M.sem("norm_root"), 1)


def head_norms_dve(dve, M, name, srcs, gains, cols=T):
    for k, (src, gain) in enumerate(zip(srcs, gains)):
        dve.wait_ge(M.sem("norm_root"), k + 1 + M.past(name, "root"))
        dve.reciprocal(M.rstd[:, 0:cols], M.std[:, 0:cols])
        dve.drain()
        dve.scalar_tensor_tensor(out=src, in0=src, scalar=gain, in1=M.rstd[:, 0:cols],
                                 op0=ALU.mult, op1=ALU.mult)
        dve.drain().then_inc(M.sem("norm_scaled"), 1)


class Pairs:

    def __init__(self, M, name, unroll, q, att, staged, kinds, y, more=None):
        self.more = more
        self.name, self.unroll, self.q, self.att, self.staged, self.kinds, self.y = \
            name, unroll, q, att, staged, kinds, y
        self.units = [(u, half, kind) for u in range(unroll) for half in range(2) for kind in range(len(kinds))]
        self.turns = PAIRS // unroll

    def stage_pool(self, pool, M, i):
        pool.wait_ge(M.sem(f"{self.name}_restage"), i + 1)
        for u in range(self.unroll):
            pool.tensor_copy(self.staged[:, u, :], tile_at(self.q, i * self.unroll + u))
        if self.more is not None:
            self.more(pool, i)
        pool.drain().then_inc(M.sem(f"{self.name}_staged"), 1)

    def pe(self, pe, M, extra=None):
        A, V, per = self.name, self.att, len(self.units)
        with pe.Fori(0, self.turns) as i:
            base = i * per
            pe.wait_ge(M.sem(f"{A}_staged"), i + 1)

            def scores(n):
                u, half, kind = self.units[n]
                if n:
                    pe.wait_ge(M.sem(f"{A}_masked"), base + n)
                rows = HALVES[half]
                att_scores_pe(pe, M, A, [(self.staged[rows, u, :], self.kinds[kind][0][rows, :])])

            scores(0)
            for n, (u, half, kind) in enumerate(self.units):
                if n + 1 < per:
                    scores(n + 1)
                att_turn_pe(pe, M, A, V, n, base)
                rows = HALVES[half]
                pe.wait_ge(M.sem(f"{A}_kept"), base + (n + 1))
                bank = 6 + u % 2
                first = kind == 0
                if extra and kind == 0:
                    extra(i, u, half, bank)
                    first = False
                values = self.kinds[kind][1]
                for k in range(QT):
                    mm = pe.matmul(M.ps[rows, bank * T + k * P:(bank + 1) * T],
                                   values[:, k * P + 64 * half:k * P + 64 * half + 64],
                                   V.pt[:, PT_AT[k]:PT_AT[k] + PT_LEN[k]],
                                   start=(first and k == 0), stop=(kind == len(self.kinds) - 1 and k == QT - 1),
                                   skip_group_check=True)
                mm.then_inc(M.sem(f"{A}_out"), 1)
            pe.nop().then_inc(M.sem(f"{A}_restage"), 1)

    def act(self, act, M):
        A, V, per = self.name, self.att, len(self.units)
        with act.Fori(0, self.turns) as i:
            base = i * per
            att_exp_act(act, M, A, V, 0, base)
            for n, (u, half, kind) in enumerate(self.units):
                att_turned_act(act, M, A, V, n, base)
                if n + 1 < per:
                    att_exp_act(act, M, A, V, n + 1, base)
                if half and kind == len(self.kinds) - 1:
                    act.wait_ge(M.sem(f"{A}_out"), base + (n + 1))
                    act.activation(tile_at(self.y, i * self.unroll + u), M.bank(6 + u % 2), ACT.Copy)\
                       .then_inc(M.sem(f"{A}_y"), 1)

    def dve(self, dve, M, gate=None):
        A, V, per = self.name, self.att, len(self.units)
        with dve.Fori(0, self.turns) as i:
            base = i * per

            def mask(n):
                u, half, kind = self.units[n]
                m = self.kinds[kind][2](half)
                att_mask_dve(dve, M, A, V, n, base,
                             lambda t: m[:, CAUSAL_AT[t]:CAUSAL_AT[t] + S_LEN[t]], SCALE_64)

            mask(0)
            for n, (u, half, kind) in enumerate(self.units):
                att_divide_dve(dve, M, A, V, n, base, gate and gate(i, u, half, kind))
                if n + 1 < per:
                    mask(n + 1)



def branch_out_pe(pe, M, name, y, per_tile, unroll):
    used = M.sem("blocks_used")
    with pe.Fori(0, NT // unroll) as i:
        for u in range(unroll):
            pe.wait_ge(M.sem(f"{name}_free"), i * unroll + (u + 1))
            b = FIRST[name] + u * (1 + per_tile)
            wait_block(pe, M, b, i, unroll * (1 + per_tile))
            for k in range(BLK):
                mm = pe.matmul(M.bank(2 * (u % 2)), block_tile(M, b, k), M.a[:, k, :], start=(k == 0), stop=(k == 7))
            mm.then_inc(used, 1)
            for blk in range(per_tile):
                wait_block(pe, M, b + 1 + blk, i, unroll * (1 + per_tile))
                for k in range(BLK):
                    kk = blk * BLK + k
                    mm = pe.matmul(M.bank(2 * (u % 2) + 1), block_tile(M, b + 1 + blk, k), y(kk),
                                   start=(kk == 0), stop=(kk == per_tile * BLK - 1))
                mm.then_inc(used, 1)


def branch_out_act(act, M, name, per_tile, unroll):
    with act.Fori(0, NT // unroll) as i:
        for u in range(unroll):
            act.wait_ge(M.sem(f"{name}_free"), i * unroll + (u + 1))
            act.wait_ge(M.sem("blocks_used"), i * (unroll * (1 + per_tile)) + FIRST[name] + u * (1 + per_tile) + 1)
            act.activation(M.sq[:, u % 2, :], M.bank(2 * (u % 2)), ACT.Sigmoid).then_inc(M.sem(f"{name}_gate"), 1)


def branch_out_dve(dve, M, name, per_tile, unroll, first):
    dve.drain().then_inc(M.sem(f"{name}_free"), 2)
    with dve.Fori(0, NT // unroll) as i:
        for u in range(unroll):
            dve.wait_ge(M.sem(f"{name}_gate"), i * unroll + (u + 1))
            dve.wait_ge(M.sem("blocks_used"), i * (unroll * (1 + per_tile)) + FIRST[name] + (u + 1) * (1 + per_tile))
            m = tile_at(M.m, i * unroll + u)
            if first:
                dve.tensor_tensor(m, M.bank(2 * (u % 2) + 1), M.sq[:, u % 2, :], ALU.mult)
            else:
                dve.tensor_tensor(M.ssum[:, :], M.bank(2 * (u % 2) + 1), M.sq[:, u % 2, :], ALU.mult)
                dve.drain()
                dve.tensor_tensor(m, m, M.ssum[:, :], ALU.add)
            dve.drain().then_inc(M.sem(f"{name}_free"), 1)



class Dsa:
    def __init__(self, M):
        b = M.big
        self.proj = b[:, 0:14, :]
        self.key, self.value_t = b[:, 0, :], b[:, 1, :]
        self.iq = b[:, 2:4, :]
        self.q = b[:, 6:14, :]
        self.value = b[:, 14, :]
        self.y = b[:, 24:32, :]
        self.relu = b[:, 15:17, :]
        self.ikz = b[:, 17:21, :]
        self.att = AttView(M, 0)
        self.mask, at = M.carve(self.att.end, 1280)
        self.staged, at = M.carve(at, 4, T)
        self.iw, at = M.carve(at, QT, 8)
        self.best, at = M.carve(at, 8)
        self.pairs = Pairs(M, "dsa", 4, self.q, self.att, self.staged,
                           [(self.key, self.value, lambda half: self.mask)], self.y)


def dsa_pe(pe, M, R):
    used, free = M.sem("blocks_used"), M.sem("dsa_in_free")

    def project(t):
        pe.wait_ge(free, t + 1)
        b = FIRST["dsa_in"] + t
        wait_block(pe, M, b)
        for k in range(BLK):
            mm = pe.matmul(M.bank(t % 2), block_tile(M, b, k), M.a[:, k, :], start=(k == 0), stop=(k == 7))
        mm.then_inc(used, 1)

    for t in range(6):
        project(t)
    pe.wait_ge(free, 2 + 6)
    for n, src in enumerate((R.value_t, R.proj[:, 5, :])):
        for t in range(QT):
            mm = pe.transpose(M.bank(2 + n)[:, t * P:(t + 1) * P], src[:, t * P:(t + 1) * P], M.t("ident", P))
    mm.then_inc(M.sem("dsa_turned_in"), 1)
    pe.wait_ge(M.sem("dsa_ikz"), 1)
    n = 0
    for i in range(1, QT):
        for h in range(IDX_H):
            if n >= 2:
                pe.wait_ge(M.sem("dsa_relu"), n - 1)
            pe.matmul(M.bank(4 + n % 2)[:, 0:S_LEN[i]], R.iq[:, h // 4, i * P:(i + 1) * P],
                      R.ikz[:, h % 4, 0:S_LEN[i]], start=True, stop=True).then_inc(M.sem("dsa_index"), 1)
            n += 1
    for t in range(6, 14):
        project(t)
    head_norms_pe(pe, M, "dsa_norm", 9)
    R.pairs.pe(pe, M)
    pe.wait_ge(M.sem("dsa_y"), PAIRS)
    branch_out_pe(pe, M, "dsa_out", lambda k: R.y[:, k, :], 1, 2)


def dsa_act(act, M, R):
    def out(t):
        act.wait_ge(M.sem("blocks_used"), FIRST["dsa_in"] + t + 1)
        if t == 4:
            for j in range(4):
                rows = slice(32 * j, 32 * j + 32)
                act.activation(R.ikz[rows, j, :], M.bank(0, rows), ACT.Copy)
            act.drain().then_inc(M.sem("dsa_ikz"), 1)
            act.nop().then_inc(M.sem("dsa_in_free"), 1)
        else:
            act.activation(R.proj[:, t, :], M.bank(t % 2), ACT.Copy).then_inc(M.sem("dsa_in_free"), 1)

    act.wait_ge(M.sem("dsa_zeroed"), 1)
    act.drain().then_inc(M.sem("dsa_in_free"), 2)
    for t in range(6):
        out(t)
    act.wait_ge(M.sem("dsa_turned_in"), 1)
    act.activation(R.value, M.bank(2), ACT.Copy)
    act.activation(R.iw, M.bank(3).rearrange("p (t c) -> p t c", t=QT)[:, :, 0:8], ACT.Copy)
    act.drain().then_inc(M.sem("dsa_iw"), 1)
    n = 0
    for i in range(1, QT):
        for h in range(IDX_H):
            act.wait_ge(M.sem("dsa_index"), n + 1)
            if n >= 2:
                act.wait_ge(M.sem("dsa_weighted"), n - 1)
            act.activation(R.relu[:, n % 2, 0:S_LEN[i]], M.bank(4 + n % 2)[:, 0:S_LEN[i]], ACT.Relu)\
               .then_inc(M.sem("dsa_relu"), 1)
            n += 1
    for t in range(6, 14):
        out(t)
    act.drain()
    head_norms_act(act, M, "dsa_norm", [R.key] + [R.q[:, k, :] for k in range(8)])
    R.pairs.act(act, M)
    branch_out_act(act, M, "dsa_out", 1, 2)


def dsa_dve(dve, M, R):
    dve.memset(R.ikz, 0.0)
    dve.tensor_copy(R.mask[:, 0:P], M.t("causal", P))
    dve.drain().then_inc(M.sem("dsa_zeroed"), 1)
    dve.wait_ge(M.sem("dsa_iw"), 1)
    n = 0
    for i in range(1, QT):
        s = R.mask[:, CAUSAL_AT[i]:CAUSAL_AT[i] + S_LEN[i]]
        for h in range(IDX_H):
            dve.wait_ge(M.sem("dsa_relu"), n + 1)
            dve.scalar_tensor_tensor(out=s, in0=R.relu[:, n % 2, 0:S_LEN[i]], scalar=R.iw[:, i, h:h + 1],
                                     in1=s if h else M.t("causal", S_LEN[i], at=CAUSAL_AT[i]),
                                     op0=ALU.mult, op1=ALU.add)
            dve.drain().then_inc(M.sem("dsa_weighted"), 1)
            n += 1
    for i in range(1, QT):
        s = R.mask[:, CAUSAL_AT[i]:CAUSAL_AT[i] + S_LEN[i]]
        for r in range(TOPK // 8):
            dve.max(R.best, s)
            dve.drain()
            dve.match_replace(s, R.best, s, TAKEN)
            dve.drain()
        dve.tensor_scalar(s, s, TAKEN, NEG, ALU.not_equal, ALU.mult)
    dve.drain()
    head_norms_dve(dve, M, "dsa_norm", [R.key] + [R.q[:, k, :] for k in range(8)],
                   [M.c("dsa_k")] + [M.c("dsa_q")] * 8)
    R.pairs.dve(dve, M)
    branch_out_dve(dve, M, "dsa_out", 1, 2, first=True)


def dsa_pool(pool, M, R):
    pairs_pool(pool, M, R.pairs, "dsa_norm", 9)


def pairs_pool(pool, M, pairs, normed, n):
    pool.wait_ge(M.sem("norm_scaled"), n + M.past(normed, "scaled"))
    pool.drain().then_inc(M.sem(f"{pairs.name}_restage"), 1)
    with pool.Fori(0, pairs.turns) as i:
        pairs.stage_pool(pool, M, i)



assert T <= 512, "the window of 512 tokens holds all keys up to the query"


class Nsa:
    def __init__(self, M):
        b = M.big
        self.proj = b[:, 0:15, :]
        self.kc, self.vc, self.ks, self.vs, self.kw, self.vw, self.ng = [b[:, n, :] for n in range(7)]
        self.q = b[:, 7:15, :]
        flat = lambda t, n: b[:, t:t + 2, :].rearrange("p a b -> p (a b)")[:, 0:n]
        self.kin = flat(15, 32 * NCMP).rearrange("p (l n) -> p l n", n=NCMP)
        self.vin = flat(17, 32 * NCMP).rearrange("p (l n) -> p l n", n=NCMP)
        self.p = b[:, 19:23, :]
        self.pt = b[:, 15:19, :]
        self.pt_flat = self.pt.rearrange("p a b -> p (a b)")
        self.kcmp = b[:, 23, :]
        self.val_s, self.val_w = b[:, 0, :], b[:, 1, :]
        self.y = b[:, 24:32, :]
        self.att = AttView(M, 0)
        self.masks, at = M.carve(self.att.end, 2, 1280)
        self.staged, at = M.carve(at, 2, T)
        self.pt_staged, at = M.carve(at, 2, 2 * P)
        self.vcmp, at = M.carve(at, 4, 32)
        self.vz, at = M.carve(at, QT, P)
        self.gates, at = M.carve(at, 48, QT)
        self.imp, at = M.carve(at, 8, SEL_N)
        self.z, at = M.carve(at, 8, 36)
        self.rank, at = M.carve(at, 64)
        self.gt, at = M.carve(at, 8, 64)
        self.eq, at = M.carve(at, 8, 64)
        self.scores, at = M.carve(at, 8, SEL_N)
        self.top, at = M.carve(at, 16)
        self.sum, at = M.carve(at, 16)
        self.part, at = M.carve(at, P)
        self.pairs = Pairs(M, "nsa", 2, self.q, self.att, self.staged,
                           [(self.ks, self.val_s, lambda half: self.masks[:, half, :]),
                            (self.kw, self.val_w, lambda half: M.t("causal", 1280))], self.y, self.stage_pt)

    def stage_pt(self, pool, i):
        for half in range(2):
            pool.tensor_copy(self.pt_staged[:, half, :], self.pt_flat[:, bass.ds(i * (2 * P) + 8 * P * half, 2 * P)])


def nsa_pe(pe, M, R):
    used = M.sem("blocks_used")
    pe.wait_ge(M.sem("dsa_out_free"), NT + 2)
    gemm_pe(pe, M, "nsa_in", 15, 1, lambda k: M.a[:, k, :], 15, looped=False)
    pe.wait_ge(M.sem("nsa_windows"), 1)
    for b in range(8):
        wait_block(pe, M, FIRST["nsa_cmp"] + b)
        for j in range(4):
            l = 4 * b + j
            for n, src in enumerate((R.kin, R.vin)):
                mm = pe.matmul(M.bank(4 + n)[:, 0:NCMP], block_tile(M, FIRST["nsa_cmp"] + b, 2 * j + n),
                               src[:, l, :], start=(l == 0), stop=(l == 31))
        mm.then_inc(used, 1)
    gemm_ready(pe, M, "nsa_in", 15, 4)
    for n, src in enumerate((R.vs, R.vw, R.ng)):
        for t in range(QT):
            mm = pe.transpose(M.bank(n)[:, t * P:(t + 1) * P], src[:, t * P:(t + 1) * P], M.t("ident", P))
    mm.then_inc(M.sem("nsa_turned_in"), 1)
    pe.wait_ge(M.sem("nsa_vcmp"), 1)
    pe.transpose(M.bank(3)[:, 0:P], R.vcmp.rearrange("p a b -> p (a b)"), M.t("ident", P))\
      .then_inc(M.sem("nsa_vcmp_turned"), 1)
    head_norms_pe(pe, M, "nsa_norm", 11)
    pe.wait_ge(M.sem("norm_scaled"), 11 + M.past("nsa_norm", "scaled"))
    for n in range(4):
        half, quad = n // 2, n % 2
        for j in range(4):
            for i in range(QT):
                at = j * P + i * 32
                mm = pe.matmul(M.bank(n)[:, at:at + 32], R.q[HALVES[half], 4 * quad + j, i * P:(i + 1) * P],
                               R.kcmp[HALVES[half], 0:32], start=True, stop=True)
        mm.then_inc(M.sem("nsa_cmp_scores"), 1)
    for n in range(4):
        pe.wait_ge(M.sem("nsa_cmp_gated"), n + 1)
        if n >= 2:
            pe.wait_ge(M.sem("nsa_cmp_kept"), n - 1)
        for j in range(4):
            mm = pe.transpose(M.bank(4 + n % 2)[:, j * P:(j + 1) * P], R.p[:, n, j * P:(j + 1) * P], M.t("ident", P))
        mm.then_inc(M.sem("nsa_cmp_turned"), 1)
    pe.wait_ge(M.sem("nsa_cmp_kept"), 4)

    def compressed(i, u, half, bank):
        for t in range(QT):
            pe.matmul(M.ps[HALVES[half], bank * T + t * P:bank * T + (t + 1) * P],
                      R.vz[:, t, 64 * half:64 * half + 64],
                      R.pt_staged[:, half, u * P:(u + 1) * P],
                      start=(t == 0), stop=False, skip_group_check=True)

    R.pairs.pe(pe, M, compressed)
    pe.wait_ge(M.sem("nsa_y"), PAIRS)
    branch_out_pe(pe, M, "nsa_out", lambda k: R.y[:, k, :], 1, 2)


def nsa_act(act, M, R):
    def out(t, u):
        if t == 6:
            return act.activation(R.ng, M.bank(u % 4), ACT.Sigmoid)
        return act.activation(R.proj[:, t, :], M.bank(u % 4), ACT.Copy)

    gemm_out(act, M, "nsa_in", 15, 1, 15, 4, out, looped=False)
    act.wait_ge(M.sem("blocks_used"), FIRST["nsa_cmp"] + 8)
    act.wait_ge(M.sem("nsa_zeroed"), 1)
    act.activation(R.kcmp[:, 0:NCMP], M.bank(4)[:, 0:NCMP], ACT.Copy)
    for c in range(4):
        act.activation(R.vcmp[:, c, 0:NCMP], M.bank(5)[:, 0:NCMP], ACT.Copy)
    act.drain().then_inc(M.sem("nsa_vcmp"), 1)
    act.wait_ge(M.sem("nsa_turned_in"), 1)
    act.activation(R.val_s, M.bank(0), ACT.Copy)
    act.activation(R.val_w, M.bank(1), ACT.Copy)
    act.activation(R.gates.rearrange("p g t -> p t g"),
                   M.bank(2).rearrange("p (t c) -> p t c", t=QT)[:, :, 0:48], ACT.Copy)
    act.wait_ge(M.sem("nsa_vcmp_turned"), 1)
    for c in range(4):
        rows = slice(32 * c, 32 * c + 32)
        act.activation(R.vz[rows, c, :], M.bank(3, rows)[:, 0:P], ACT.Copy)
    act.drain().then_inc(M.sem("nsa_turned_kept"), 1)
    head_norms_act(act, M, "nsa_norm", [R.kcmp, R.ks, R.kw] + [R.q[:, k, :] for k in range(8)])
    for n in range(4):
        act.wait_ge(M.sem("nsa_cmp_less_top"), n + 1)
        act.activation(R.p[:, n, :], R.p[:, n, :], ACT.Exp).then_inc(M.sem("nsa_cmp_exp"), 1)
    for n in range(4):
        act.wait_ge(M.sem("nsa_cmp_turned"), n + 1)
        act.activation(R.pt[:, n, :], M.bank(4 + n % 2), ACT.Copy).then_inc(M.sem("nsa_cmp_kept"), 1)
    R.pairs.act(act, M)
    branch_out_act(act, M, "nsa_out", 1, 2)


def nsa_dve(dve, M, R):
    dve.memset(R.kcmp, 0.0)
    dve.memset(R.vcmp, 0.0)
    dve.memset(R.vz, 0.0)
    dve.memset(R.z, 0.0)
    dve.drain().then_inc(M.sem("nsa_zeroed"), 1)
    dve.wait_ge(M.sem("nsa_in_free"), 4 + 2)
    for n, (src, dst) in enumerate(((R.kc, R.kin), (R.vc, R.vin))):
        tok = src.rearrange("p (n l) -> p l n", l=16)
        for part in range(2):
            at = COLS["cmp_pos"] + 32 * n + 16 * part
            pos = M.col[:, at:at + 16].unsqueeze(2).broadcast_to([P, 16, NCMP])
            dve.tensor_tensor(dst[:, 16 * part:16 * part + 16, :], tok[:, :, part:part + NCMP], pos, ALU.add)
    dve.drain().then_inc(M.sem("nsa_windows"), 1)
    dve.wait_ge(M.sem("nsa_turned_kept"), 1)
    head_norms_dve(dve, M, "nsa_norm", [R.kcmp, R.ks, R.kw] + [R.q[:, k, :] for k in range(8)],
                   [M.c("nsa_k", k) for k in range(3)] + [M.c("nsa_q")] * 8)
    rows16 = lambda x: x.rearrange("p (g n) -> p g n", n=32)
    wide = lambda x: x.unsqueeze(2).broadcast_to([P, 16, 32])
    four = lambda x: x.unsqueeze(1).broadcast_to([P, 4, P])
    heads = lambda x: x.rearrange("p (j x) -> p j x", j=4)
    for n in range(4):
        dve.wait_ge(M.sem("nsa_cmp_scores"), n + 1)
        p = R.p[:, n, :]
        dve.scalar_tensor_tensor(out=heads(p), in0=heads(M.bank(n)), scalar=SCALE_64,
                                 in1=four(M.t("cmp_bias", P)), op0=ALU.mult, op1=ALU.add)
        dve.drain()
        dve.tensor_reduce(R.top, rows16(p), AX_X, ALU.max)
        dve.drain()
        dve.tensor_tensor(rows16(p), rows16(p), wide(R.top), ALU.subtract)
        dve.drain().then_inc(M.sem("nsa_cmp_less_top"), 1)
    for n in range(4):
        half, quad = n // 2, n % 2
        dve.wait_ge(M.sem("nsa_cmp_exp"), n + 1)
        p = R.p[:, n, :]
        dve.tensor_reduce(R.sum, rows16(p), AX_X, ALU.add)
        dve.drain()
        dve.reciprocal(R.top, R.sum)
        dve.drain()
        dve.tensor_tensor(rows16(p), rows16(p), wide(R.top), ALU.mult)
        dve.drain()
        dve.tensor_tensor(heads(p), heads(p), four(M.t("cmp_seen", P)), ALU.mult)
        dve.drain()
        z = R.z[:, 4 * half:4 * half + 4, 1:33]
        dve.tensor_reduce(R.part, p.rearrange("p (j x) -> p x j", j=4), AX_X, ALU.add)
        dve.drain()
        part = R.part.rearrange("p (i n) -> p i n", n=32)
        dve.tensor_tensor(z, z, part, ALU.add)
        g = R.gates[:, 8 * half + 4 * quad:8 * half + 4 * quad + 4, :].rearrange("p j i -> p (j i)")
        dve.tensor_tensor(rows16(p), rows16(p), wide(g), ALU.mult)
        dve.drain().then_inc(M.sem("nsa_cmp_gated"), 1)
    dve.tensor_reduce(R.imp, R.z[:, :, 0:32].rearrange("p g (j m) -> p g j m", m=4), AX_X, ALU.add)
    dve.drain()
    dve.tensor_tensor(R.imp, R.imp, R.z[:, :, 4:36:4], ALU.add)
    dve.drain()
    bias = M.t("sel_bias", 32).rearrange("p (i j) -> p i j", j=SEL_N)
    for g in range(2):
        dve.tensor_tensor(R.imp[:, 4 * g:4 * g + 4, :], R.imp[:, 4 * g:4 * g + 4, :], bias, ALU.add)
    dve.drain()
    for r in range(8):
        own = R.imp[:, r, :].unsqueeze(2).broadcast_to([P, 8, 8])
        other = R.imp[:, r, :].unsqueeze(1).broadcast_to([P, 8, 8])
        square = lambda x: x.rearrange("p (a b) -> p a b", b=8)
        dve.tensor_tensor(square(R.gt[:, r, :]), other, own, ALU.is_gt)
        dve.tensor_tensor(square(R.eq[:, r, :]), other, own, ALU.is_equal)
    dve.drain()
    dve.tensor_tensor(R.eq, R.eq, M.t("before", 64).unsqueeze(1).broadcast_to([P, 8, 64]), ALU.mult)
    dve.drain()
    dve.tensor_tensor(R.gt, R.gt, R.eq, ALU.add)
    dve.drain()
    dve.tensor_reduce(R.rank, R.gt.rearrange("p r (j a) -> p (r j) a", a=8), AX_X, ALU.add)
    dve.drain()
    dve.tensor_scalar(R.rank, R.rank, 3.5, NEG, ALU.is_gt, ALU.mult)
    dve.drain()
    for g in range(2):
        for i in range(QT):
            n = 2 * (i + 1)
            sel = R.rank[:, (4 * g + i) * 8:(4 * g + i) * 8 + n].unsqueeze(2).broadcast_to([P, n, 64])
            blocks = lambda x: x.rearrange("p (b k) -> p b k", k=64)
            dve.tensor_tensor(blocks(R.masks[:, g, CAUSAL_AT[i]:CAUSAL_AT[i] + S_LEN[i]]),
                              blocks(M.t("causal", S_LEN[i], at=CAUSAL_AT[i])), sel, ALU.add)
    dve.drain()
    R.pairs.dve(dve, M, lambda i, u, half, kind: R.gates[:, bass.ds(i * 2 + (16 * (kind + 1) + 8 * half + u), 1), :]
                .rearrange("p a b -> p (a b)"))
    branch_out_dve(dve, M, "nsa_out", 1, 2, first=False)



def input_norm_pe(pe, M, name):
    norm_pe(pe, M, name, NT)
    pe.wait_ge(M.sem("norm_scaled"), NT + M.past(name, "scaled"))


def input_norm_act(act, M, name, after):
    if after:
        act.wait_ge(M.sem("norm_added"), NT + M.past(after, "added"))
    norm_act(act, M, name, lambda k: M.h[:, k, :], NT, D)


def input_norm_dve(dve, M, name, gain):
    norm_dve(dve, M, name, NT)
    scale_dve(dve, M, name, lambda k: M.h[:, k, :], lambda k: M.a[:, k, :], gain, NT)



STEPS = 10
N_STATE = QT - 1


class Ssd:
    def __init__(self, M):
        tiles = [M.big[:, n, :] for n in range(16)]
        at = 0
        for _ in range(21):
            t, at = M.carve(at, T)
            tiles.append(t)
        take = lambda n: [tiles.pop(0) for _ in range(n)]
        self.conv = [take(6), take(6)]
        self.gate = [take(4), take(4)]
        self.x_tok = take(4)
        self.b_tok, self.cb = take(2)
        self.decay = take(2)
        self.c_dec = take(2)
        self.state = [None] + take(3)
        self.xw = take(3)
        self.sig = [M.sq[:, 0, :], M.sq[:, 1, :]]
        self.acum = M.extra[:, 0, :]
        self.dt = M.extra[:, 1, :]
        self.acol = M.extra[:, 2, 0:128].rearrange("p (c h) -> p c h", c=QT)
        self.dtc = M.extra[:, 2, 128:256].rearrange("p (c h) -> p c h", c=QT)
        self.to_end = M.extra[:, 2, 256:384].rearrange("p (c h) -> p c h", c=QT)
        self.chunk_decay = M.extra[:, 2, 384:512].rearrange("p (c h) -> p c h", c=QT)
        self.a = M.extra[:, 3, 0:2]
        self.y = M.big[:, 16:32, :]


def ssd_block(g, s):
    return FIRST["ssd_in"] + 1 + STEPS * g + s


def head_cols(x, e):
    return x[:, e * 64:(e + 1) * 64]


def ssd_pe(pe, M, R):
    used = M.sem("blocks_used")
    ones_row = lambda k: M.t("ident", 1, at=k).broadcast_to([P, P])

    def project(g, s):
        n = STEPS * g + s + 1
        pe.wait_ge(M.sem("ssd_free"), n + 1)
        wait_block(pe, M, FIRST["ssd_in"] + n)
        for k in range(BLK):
            mm = pe.matmul(M.bank(n % 2), block_tile(M, FIRST["ssd_in"] + n, k), M.a[:, k, :],
                           start=(k == 0), stop=(k == 7))
        mm.then_inc(used, 1)

    def turn(g):
        cv = R.conv[g % 2]
        pe.wait_ge(M.sem("ssd_x"), 6 * (g + 1))
        if g:
            pe.wait_ge(M.sem("ssd_y"), 4 * g)
        for c in range(QT):
            s = slice(c * P, (c + 1) * P)
            mm = pe.transpose(M.bank(2)[:, s], cv[4][:, s], M.t("ident", P))
        mm.then_inc(M.sem("ssd_b_turned"), 1)
        for c in range(QT):
            s = slice(c * P, (c + 1) * P)
            for k in range(4):
                mm = pe.transpose(M.bank(3 + c)[:, k * P:(k + 1) * P], cv[k][:, s], M.t("ident", P))
            mm.then_inc(M.sem("ssd_x_turned"), 1)
        for c in range(QT):
            s = slice(c * P, (c + 1) * P)
            mm = pe.matmul(M.bank(7)[:, s], cv[4][:, s], cv[5][:, s], start=True, stop=True)
        mm.then_inc(M.sem("ssd_cb"), 1)

    def states(g):
        pe.wait_ge(M.sem("ssd_b_kept"), g + 1)
        for c in range(N_STATE):
            pe.wait_ge(M.sem("ssd_xw"), N_STATE * g + c + 1)
            pe.matmul(M.bank(3 + c), R.b_tok[:, c * P:(c + 1) * P], R.xw[c], start=True, stop=True)\
              .then_inc(M.sem("ssd_added"), 1)

    def cumulated(g, e):
        h = 8 * g + e
        if e == 0:
            pe.wait_ge(M.sem("ssd_state"), N_STATE * (g + 1))
        if h >= 2:
            pe.wait_ge(M.sem("ssd_exp_c"), h - 1)
            pe.wait_ge(M.sem("ssd_seg"), h - 1)
        pe.matmul(M.bank(4 + e % 2), ones_row(h), R.acum, start=True, stop=True)\
          .then_inc(M.sem("ssd_cumulated"), 1)

    def output(g, e):
        h = 8 * g + e
        pe.wait_ge(M.sem("ssd_decay_cb"), h + 1)
        pe.wait_ge(M.sem("ssd_c_dec"), h + 1)
        pair = h // 2
        if pair >= 2:
            pe.wait_ge(M.sem("ssd_y"), pair - 1)
        bank = 6 if pair % 2 == 0 else 3
        rows = HALVES[e % 2]
        for c in range(QT):
            s = slice(c * P, (c + 1) * P)
            mm = pe.matmul(M.bank(bank, rows)[:, s], head_cols(R.x_tok[c], e), R.decay[e % 2][:, s],
                           start=(c == 0), stop=False, skip_group_check=True)
            if c:
                mm = pe.matmul(M.bank(bank, rows)[:, s], head_cols(R.state[c], e), R.c_dec[e % 2][:, s],
                               start=False, stop=(c == QT - 1), skip_group_check=True)
        mm.then_inc(M.sem("ssd_out_mm"), 1)

    pe.wait_ge(M.sem("nsa_out_free"), NT + 2)
    project(0, -1)
    for s in range(2):
        project(0, s)
    pe.wait_ge(M.sem("ssd_dt"), 1)
    for n, src in enumerate((R.acum, R.dt)):
        for c in range(QT):
            mm = pe.transpose(M.bank(2 + n)[:, c * P:(c + 1) * P], src[:, c * P:(c + 1) * P], M.t("ident", P))
    mm.then_inc(M.sem("ssd_dt_turned"), 1)
    project(0, 2)
    pe.wait_ge(M.sem("ssd_dt_kept"), 1)
    pe.matmul(M.bank(4)[:, 0:P], ones_row(P - 1), R.acol.rearrange("p c h -> p (c h)"), start=True, stop=True)\
      .then_inc(M.sem("ssd_last"), 1)
    for s in range(3, STEPS):
        project(0, s)
    pe.wait_ge(M.sem("ssd_to_end"), 1)
    for g in range(GRPS):
        for s in range(STEPS):
            if g + 1 < GRPS:
                project(g + 1, s)
            if s == 0:
                turn(g)
            if s == 1:
                states(g)
            if 1 <= s <= 8:
                cumulated(g, s - 1)
            if s >= 2:
                output(g, s - 2)
    norm_pe(pe, M, "ssd_norm", 16)
    pe.wait_ge(M.sem("norm_scaled"), 16 + M.past("ssd_norm", "scaled"))
    branch_out_pe(pe, M, "ssd_out", lambda k: R.y[:, k, :], 2, 4)


def ssd_act(act, M, R):
    def project(g, s):
        n = STEPS * g + s + 1
        if s < 6:
            act.wait_ge(M.sem("ssd_conv"), 6 * g + s + 1)
            src = R.conv[g % 2][s]
        else:
            act.wait_ge(M.sem("blocks_used"), FIRST["ssd_in"] + n + 1)
            src = M.bank(n % 2)
        if n >= 3:
            act.wait_ge(M.sem("ssd_x"), conv_tiles(n - 2))
            if gate_tiles(n - 2):
                act.wait_ge(M.sem("ssd_gate"), gate_tiles(n - 2))
        act.activation(R.sig[n % 2], src, ACT.Sigmoid).then_inc(M.sem("ssd_sig"), 1)

    def mix(g, s):
        if s == 0:
            act.wait_ge(M.sem("ssd_b_turned"), g + 1)
            act.activation(R.b_tok, M.bank(2), ACT.Copy).then_inc(M.sem("ssd_b_kept"), 1)
        if 1 <= s <= 8:
            e = s - 1
            h = 8 * g + e
            act.wait_ge(M.sem("ssd_seg"), h + 1)
            act.activation(R.c_dec[e % 2], M.bank(4 + e % 2), ACT.Exp).then_inc(M.sem("ssd_exp_c"), 1)
            act.activation(R.decay[e % 2], R.decay[e % 2], ACT.Exp).then_inc(M.sem("ssd_decay"), 1)

    act.activation(R.a[0:32, 0:1], M.c("a_log", rows=slice(0, 32)), ACT.Exp).then_inc(M.sem("ssd_a"), 1)
    act.wait_ge(M.sem("ssd_abs"), 1)
    act.activation(R.conv[1][1][0:32, :], R.conv[1][1][0:32, :], ACT.Exp, scale=-1.0).then_inc(M.sem("ssd_abs_exp"), 1)
    project(0, 0)
    project(0, 1)
    act.wait_ge(M.sem("ssd_dt_turned"), 1)
    for n, dst in enumerate((R.acol, R.dtc)):
        act.activation(dst, M.bank(2 + n).rearrange("p (c x) -> p c x", c=QT)[:, :, 0:32], ACT.Copy)
    act.drain().then_inc(M.sem("ssd_dt_kept"), 1)
    project(0, 2)
    act.wait_ge(M.sem("ssd_last"), 1)
    act.activation(R.chunk_decay.rearrange("p c h -> p (c h)"), M.bank(4)[:, 0:P], ACT.Exp)\
       .then_inc(M.sem("ssd_chunk_decay"), 1)
    act.wait_ge(M.sem("ssd_to_end_log"), 1)
    act.activation(R.to_end, R.to_end, ACT.Exp).then_inc(M.sem("ssd_to_end"), 1)
    for s in range(3, STEPS):
        project(0, s)
    for g in range(GRPS):
        for s in range(STEPS):
            if g + 1 < GRPS:
                project(g + 1, s)
            mix(g, s)
    act.wait_ge(M.sem("ssd_y"), 16)
    norm_act(act, M, "ssd_norm", lambda k: R.y[:, k, :], 16, 2048)
    branch_out_act(act, M, "ssd_out", 2, 4)


def conv_tiles(n):
    return 6 * ((n - 1) // STEPS) + min((n - 1) % STEPS + 1, 6) if n else 0


def gate_tiles(n):
    return n - conv_tiles(n)


def ssd_dve(dve, M, R):
    dve.drain().then_inc(M.sem("ssd_free"), 2)
    r32 = slice(0, 32)

    def project(g, s):
        n = STEPS * g + s + 1
        if s < 6:
            dve.wait_ge(M.sem("blocks_used"), FIRST["ssd_in"] + n + 1)
            tile = 4 * g + s if s < 4 else (16 + g if s == 4 else 20 + g)
            w = [M.c("conv_w", 24 * k + tile) for k in range(4)]
            out, src = R.conv[g % 2][s], M.bank(n % 2)
            dve.tensor_scalar(out, src, w[3], M.c("conv_b", tile), ALU.mult, ALU.add)
            dve.drain()
            for back in (1, 2, 3):
                dve.scalar_tensor_tensor(out=out[:, back:T], in0=src[:, 0:T - back], scalar=w[3 - back],
                                         in1=out[:, back:T], op0=ALU.mult, op1=ALU.add)
                dve.drain()
            dve.nop().then_inc(M.sem("ssd_conv"), 1)
            dve.nop().then_inc(M.sem("ssd_free"), 1)
        else:
            dve.wait_ge(M.sem("ssd_sig"), n)
            dve.tensor_tensor(R.gate[g % 2][s - 6], M.bank(n % 2), R.sig[n % 2], ALU.mult)
            dve.drain().then_inc(M.sem("ssd_gate"), 1)
            dve.nop().then_inc(M.sem("ssd_free"), 1)

    heads = lambda x: x.rearrange("p (h d) -> p h d", d=64)

    def by_head(x, c, g):
        return x[:, c, 8 * g:8 * g + 8].unsqueeze(2).broadcast_to([P, 8, 64])

    def mix(g, s):
        if s == 0:
            for c in range(QT):
                dve.wait_ge(M.sem("ssd_x_turned"), QT * g + c + 1)
                dve.tensor_tensor(heads(R.x_tok[c]), heads(M.bank(3 + c)), by_head(R.dtc, c, g), ALU.mult)\
                   .then_inc(M.sem("ssd_xdt"), 1)
            dve.wait_ge(M.sem("ssd_cb"), g + 1)
            four = lambda x: x.rearrange("p (c i) -> p c i", c=QT)
            dve.tensor_tensor(four(R.cb), four(M.bank(7)), M.t("tri", P).unsqueeze(1).broadcast_to([P, QT, P]),
                              ALU.mult)
            dve.drain()
        if s == 1:
            for c in range(N_STATE):
                dve.wait_ge(M.sem("ssd_added"), N_STATE * g + c + 1)
                if c == 0:
                    dve.tensor_copy(R.state[1], M.bank(3))
                else:
                    dve.tensor_tensor(heads(R.state[c + 1]), heads(R.state[c]), by_head(R.chunk_decay, c, g), ALU.mult)
                    dve.drain()
                    dve.tensor_tensor(R.state[c + 1], R.state[c + 1], M.bank(3 + c), ALU.add)
                dve.drain().then_inc(M.sem("ssd_state"), 1)
        if s >= 2:
            e = s - 2
            h = 8 * g + e
            dve.wait_ge(M.sem("ssd_decay"), h + 1)
            dve.tensor_tensor(R.decay[e % 2], R.decay[e % 2], R.cb, ALU.mult).then_inc(M.sem("ssd_decay_cb"), 1)
        if 1 <= s <= 8:
            e = s - 1
            h = 8 * g + e
            dve.wait_ge(M.sem("ssd_cumulated"), h + 1)
            if h >= 2:
                dve.wait_ge(M.sem("ssd_out_mm"), h - 1)
            for c in range(QT):
                w = slice(c * P, (c + 1) * P)
                dve.tensor_scalar(R.decay[e % 2][:, w], M.bank(4 + e % 2)[:, w], R.acol[:, c, h:h + 1], 0.0,
                                  ALU.subtract, ALU.min)
            dve.drain().then_inc(M.sem("ssd_seg"), 1)
        if s >= 4 and s % 2 == 0:
            pair_out(g, s // 2 - 2)

    def pair_out(g, k):
        pair = 4 * g + k
        dve.wait_ge(M.sem("ssd_out_mm"), 2 * (pair + 1))
        y = R.y[:, pair, :]
        dve.scalar_tensor_tensor(out=y, in0=R.conv[g % 2][k], scalar=M.c("ssd_d", pair),
                                 in1=M.bank(6 if pair % 2 == 0 else 3), op0=ALU.mult, op1=ALU.add)
        dve.drain()
        dve.tensor_tensor(y, y, R.gate[g % 2][k], ALU.mult)
        dve.drain().then_inc(M.sem("ssd_y"), 1)

    xa, ab, s_, t_, p_ = [R.conv[1][k][r32, :] for k in range(5)]
    dve.memset(R.acum, 0.0)
    dve.memset(R.dt, 0.0)
    dve.wait_ge(M.sem("blocks_used"), FIRST["ssd_in"] + 1)
    dve.tensor_scalar(xa, M.bank(0, r32), M.c("dt_bias", rows=r32), None, ALU.add)
    dve.drain().then_inc(M.sem("ssd_free"), 1)
    dve.scalar_tensor_tensor(out=ab, in0=xa, scalar=-1.0, in1=xa, op0=ALU.mult, op1=ALU.max)
    dve.drain().then_inc(M.sem("ssd_abs"), 1)
    dve.wait_ge(M.sem("ssd_abs_exp"), 1)
    dve.tensor_scalar(t_, ab, 2.0, None, ALU.add)
    dve.drain()
    dve.reciprocal(s_, t_)
    dve.drain()
    dve.tensor_tensor(s_, s_, ab, ALU.mult)
    dve.drain()
    dve.tensor_tensor(t_, s_, s_, ALU.mult)
    dve.drain()
    dve.tensor_scalar(p_, t_, 1.0 / 17, None, ALU.mult)
    dve.drain()
    for k in range(15, 2, -2):
        dve.scalar_tensor_tensor(out=p_, in0=p_, scalar=1.0 / k, in1=t_, op0=ALU.add, op1=ALU.mult)
        dve.drain()
    dve.scalar_tensor_tensor(out=p_, in0=p_, scalar=1.0, in1=s_, op0=ALU.add, op1=ALU.mult)
    dve.tensor_scalar(xa, xa, 0.0, None, ALU.max)
    dve.drain()
    dve.scalar_tensor_tensor(out=R.dt[r32, :], in0=p_, scalar=2.0, in1=xa, op0=ALU.mult, op1=ALU.add)
    dve.wait_ge(M.sem("ssd_a"), 1)
    dve.tensor_scalar(R.a[r32, 1:2], R.a[r32, 0:1], -1.0, None, ALU.mult)
    dve.drain()
    dve.tensor_scalar(t_, R.dt[r32, :], R.a[r32, 1:2], None, ALU.mult)
    dve.drain()
    dve.tensor_tensor_scan(R.acum[r32, :], M.t("restart128", T, rows=r32), t_, 0.0, ALU.mult, ALU.add)
    dve.drain().then_inc(M.sem("ssd_dt"), 1)
    for s in range(3):
        project(0, s)
    dve.wait_ge(M.sem("ssd_last"), 1)
    flat = lambda x: x.rearrange("p c h -> p (c h)")
    dve.wait_ge(M.sem("ssd_chunk_decay"), 1)
    dve.tensor_tensor(flat(R.to_end), M.bank(4)[:, 0:P], flat(R.acol), ALU.subtract)
    dve.drain().then_inc(M.sem("ssd_to_end_log"), 1)
    for s in range(3, STEPS):
        project(0, s)
    for g in range(GRPS):
        for s in range(STEPS):
            if g + 1 < GRPS:
                project(g + 1, s)
            mix(g, s)
        pair_out(g, 3)
    norm_dve(dve, M, "ssd_norm", 16)
    scale_dve(dve, M, "ssd_norm", lambda k: R.y[:, k, :], lambda k: R.y[:, k, :], lambda k: M.c("ssd_norm", k), 16)
    branch_out_dve(dve, M, "ssd_out", 2, 4, first=False)


def ssd_pool(pool, M, R):
    heads = lambda x: x.rearrange("p (h d) -> p h d", d=64)

    def project(g, s):
        if s < 6:
            n = STEPS * g + s + 1
            pool.wait_ge(M.sem("ssd_sig"), n)
            x = R.conv[g % 2][s]
            pool.tensor_tensor(x, x, R.sig[n % 2], ALU.mult).then_inc(M.sem("ssd_x"), 1)

    def mix(g, s):
        if s == 0:
            for c in range(N_STATE):
                pool.wait_ge(M.sem("ssd_xdt"), QT * g + c + 1)
                if g == 0 and c == 0:
                    pool.wait_ge(M.sem("ssd_to_end"), 1)
                w = R.to_end[:, c, 8 * g:8 * g + 8].unsqueeze(2).broadcast_to([P, 8, 64])
                pool.tensor_tensor(heads(R.xw[c]), heads(R.x_tok[c]), w, ALU.mult).then_inc(M.sem("ssd_xw"), 1)
        if 1 <= s <= 8:
            e = s - 1
            pool.wait_ge(M.sem("ssd_exp_c"), 8 * g + e + 1)
            pool.tensor_tensor(R.c_dec[e % 2], R.c_dec[e % 2], R.conv[g % 2][5], ALU.mult)\
                .then_inc(M.sem("ssd_c_dec"), 1)

    for s in range(STEPS):
        project(0, s)
    for g in range(GRPS):
        for s in range(STEPS):
            if g + 1 < GRPS:
                project(g + 1, s)
            mix(g, s)



def to_h_dve(dve, M, name, per_tile, unroll, banks):
    def move(t, u):
        h = tile_at(M.h, t)
        return dve.tensor_tensor(h, h, M.bank(u % banks), ALU.add)

    gemm_out(dve, M, name, NT, per_tile, unroll, banks, move)


def tail_pe(pe, M):
    pe.wait_ge(M.sem("ssd_out_free"), NT + 2)
    gemm_pe(pe, M, "mix_out", NT, 1, lambda k: M.m[:, k, :], 4)
    input_norm_pe(pe, M, "norm_5")
    gemm_pe(pe, M, "ff_up", 32, 1, lambda k: M.a[:, k, :], 4)
    pe.wait_ge(M.sem("ff_hidden"), 32)
    gemm_pe(pe, M, "ff_down", NT, 4, lambda k: M.big[:, k, :], 2, banks=2)


def tail_act(act, M):
    gemm_ready(act, M, "mix_out", NT, 4)
    input_norm_act(act, M, "norm_5", None)
    gemm_out(act, M, "ff_up", 32, 1, 4, 4,
             lambda t, u: act.activation(tile_at(M.big, t), M.bank(u % 4), ACT.Relu))


def tail_dve(dve, M):
    to_h_dve(dve, M, "mix_out", 1, 4, 4)
    input_norm_dve(dve, M, "norm_5", lambda k: M.c("norm2", k))
    with dve.Fori(0, 8) as i:
        for u in range(4):
            dve.wait_ge(M.sem("ff_up_free"), i * 4 + (u + 5))
            r = tile_at(M.big, i * 4 + u)
            dve.tensor_tensor(r, r, r, ALU.mult).then_inc(M.sem("ff_hidden"), 1)
    to_h_dve(dve, M, "ff_down", 4, 2, 2)


def program(nc, wall, cols, tabs, pos, x, out):
    with ExitStack() as ctx:
        M = Memory(nc, ctx)
        M.eps = EPS
        mla = Mla(M)
        hgrn = Hgrn(M)
        dsa = Dsa(M)
        nsa = Nsa(M)
        ssd = Ssd(M)
        block = ctx.enter_context(nc.Block())

        @block.sync
        def _(sp):
            sp.dma_start(M.h[:, :, :], x.rearrange("(k p) t -> p k t", p=P)).then_inc(M.sem("x_in"), 16)
            sp.dma_start(M.col[:, :], cols).then_inc(M.sem("tables_in"), 16)
            sp.dma_start(M.tab[:, :], tabs).then_inc(M.sem("tables_in"), 16)
            sp.dma_start(mla.pos, pos.partition_broadcast(P).rearrange("p a t -> p (a t)"))\
              .then_inc(M.sem("positions_in"), 16)
            stream_weights(sp, M, wall, N_BLOCKS)

        @block.gpsimd
        def _(pool):
            dsa_pool(pool, M, dsa)
            pool.wait_ge(M.sem("nsa_cmp_kept"), 4)
            pairs_pool(pool, M, nsa.pairs, "nsa_norm", 11)
            ssd_pool(pool, M, ssd)
            pool.wait_ge(M.sem("ff_down_free"), NT + 2)
            pool.dma_start(out.rearrange("(k p) t -> p k t", p=P), M.h[:, :, :]).then_inc(M.sem("out_done"), 16)
            pool.wait_ge(M.sem("out_done"), 16)

        @block.tensor
        def _(pe):
            pe.wait_ge(M.sem("tables_in"), 32)
            input_norm_pe(pe, M, "norm_0")
            mla_pe(pe, M, mla)
            input_norm_pe(pe, M, "norm_1")
            mlp_pe(pe, M, "mlp0")
            input_norm_pe(pe, M, "norm_2")
            hgrn_pe(pe, M, hgrn)
            input_norm_pe(pe, M, "norm_3")
            mlp_pe(pe, M, "mlp1")
            input_norm_pe(pe, M, "norm_4")
            dsa_pe(pe, M, dsa)
            nsa_pe(pe, M, nsa)
            ssd_pe(pe, M, ssd)
            tail_pe(pe, M)

        @block.scalar
        def _(act):
            act.wait_ge(M.sem("x_in"), 16)
            input_norm_act(act, M, "norm_0", None)
            mla_act(act, M, mla)
            input_norm_act(act, M, "norm_1", "mla_o")
            mlp_act(act, M, "mlp0")
            input_norm_act(act, M, "norm_2", "mlp0_down")
            hgrn_act(act, M, hgrn)
            input_norm_act(act, M, "norm_3", "hgrn_o")
            mlp_act(act, M, "mlp1")
            input_norm_act(act, M, "norm_4", "mlp1_down")
            dsa_act(act, M, dsa)
            nsa_act(act, M, nsa)
            ssd_act(act, M, ssd)
            tail_act(act, M)

        @block.vector
        def _(dve):
            rope_angles_dve(dve, M, mla)
            input_norm_dve(dve, M, "norm_0", lambda k: M.c("gains", k))
            mla_dve(dve, M, mla)
            input_norm_dve(dve, M, "norm_1", lambda k: M.c("gains", 16 + k))
            mlp_dve(dve, M, "mlp0", lambda k: M.c("gains", 24 + k))
            input_norm_dve(dve, M, "norm_2", lambda k: M.c("gains", 32 + k))
            hgrn_dve(dve, M, hgrn)
            input_norm_dve(dve, M, "norm_3", lambda k: M.c("gains", 48 + k))
            mlp_dve(dve, M, "mlp1", lambda k: M.c("gains", 56 + k))
            input_norm_dve(dve, M, "norm_4", lambda k: M.c("norm1", k))
            dsa_dve(dve, M, dsa)
            nsa_dve(dve, M, nsa)
            ssd_dve(dve, M, ssd)
            tail_dve(dve, M)





def pack(w, n_order=None, k_first=False):
    K, N = w.shape
    t = w.reshape(K // P, P, N // P, P).transpose(2, 0, 1, 3)
    return t.reshape(-1, P, P)


def lay_weights(v):
    wall = np.zeros((N_BLOCKS + N_PAD, P, BLK * P), np.float32)

    def put(name, tiles):
        n = dict(COUNTS)[name]
        tiles = np.asarray(tiles)
        full = np.zeros((n * BLK, P, P), np.float32)
        full[:len(tiles)] = tiles
        wall[FIRST[name]:FIRST[name] + n] = full.reshape(n, BLK, P, P).transpose(0, 2, 1, 3).reshape(n, P, BLK * P)

    w_in = v["mla_w_in"][0]
    kr = w_in[:, 768:832]
    put("mla_in", pack(np.concatenate([w_in[:, :768], kr, kr], 1)))
    uq = v["mla_w_uq"][0].reshape(512, MLA_H, 192)
    put("mla_rope", pack(np.ascontiguousarray(uq[:, :, 128:]).reshape(512, 512)))
    ukv = v["mla_w_ukv"][0].reshape(256, MLA_H, 256)
    put("mla_heads", np.concatenate([np.concatenate([
        uq[:, h, :128].reshape(4, P, P), ukv[:, h, :128].reshape(2, P, P), ukv[:, h, 128:].reshape(2, P, P)])
        for h in range(MLA_H)]))
    put("mla_o", pack(v["mla_w_o"][0]))
    for l in range(2):
        put(f"mlp{l}_up", pack(v["mlp_w1"][l]))
        put(f"mlp{l}_down", pack(v["mlp_w2"][l]))
    w = v["hgrn_w_in"][0].reshape(NT, P, 4, MLA_H, P).transpose(3, 2, 0, 1, 4)
    put("hgrn_heads", w.reshape(-1, P, P))
    put("hgrn_o", pack(v["hgrn_w_o"][0]))
    names = ["dq", "dk", "dv", "iq", "ik", "iw", "nq", "nkv", "ng", "sz", "sx", "sdt", "mg"]
    sizes = [1024, 64, 64, 256, 32, 8, 1024, 768, 48, 2048, 3072, 32, 3072]
    w = dict(zip(names, np.split(v["w_in_2"][0], np.cumsum(sizes)[:-1], axis=1)))
    none = np.zeros((D, P), np.float32)
    wide = lambda x: np.concatenate([x, none[:, x.shape[1]:]], 1)
    put("dsa_in", pack(np.concatenate([w["dk"]] * 2 + [w["dv"]] * 2 + [w["iq"]] + [w["ik"]] * 4
                                      + [wide(w["iw"]), w["dq"]], 1)))

    def branch(n, w_out):
        g = pack(w["mg"][:, n * D:(n + 1) * D]).reshape(NT, NT, P, P)
        o = pack(w_out).reshape(NT, -1, P, P)
        return np.concatenate([g, o], 1).reshape(-1, P, P)

    put("dsa_out", branch(0, v["w_br_dsa_2"][0]))
    nq = w["nq"].reshape(D, 2, 8, 64).transpose(0, 2, 1, 3).reshape(D, 1024)
    ng = w["ng"].reshape(D, 2, 8, 3).transpose(0, 3, 1, 2).reshape(D, 48)
    put("nsa_in", pack(np.concatenate([w["nkv"], wide(ng), nq], 1)))
    cw = v["nsa_cmp_w_2"][0]
    both = np.zeros((32, 2, P, P), np.float32)
    both[:, :, :64, :64] = cw.transpose(1, 0, 2, 3)
    both[:, :, 64:, 64:] = cw.transpose(1, 0, 2, 3)
    put("nsa_cmp", both.reshape(-1, P, P))
    w_nsa = v["w_br_nsa_2"][0].reshape(2, 8, 64, D).transpose(1, 0, 2, 3).reshape(D, D)
    put("nsa_out", branch(1, w_nsa))
    z, sx = w["sz"], w["sx"]
    order = [wide(w["sdt"])]
    for g in range(GRPS):
        order += [sx[:, 512 * g:512 * (g + 1)], sx[:, 2048 + P * g:2048 + P * (g + 1)],
                  sx[:, 2560 + P * g:2560 + P * (g + 1)], z[:, 512 * g:512 * (g + 1)]]
    put("ssd_in", pack(np.concatenate(order, 1)))
    put("ssd_out", branch(2, v["w_br_ssd_2"][0]))
    put("mix_out", pack(v["w_out_2"][0]))
    put("ff_up", pack(v["w_ff1_2"][0]))
    put("ff_down", pack(v["w_ff2_2"][0]))
    return wall


def lay_columns(v):
    c = np.zeros((P, N_COLS), np.float32)

    def put(name, x, k=0):
        x = np.asarray(x)
        c[:x.shape[0], COLS[name] + k:COLS[name] + k + x.shape[1]] = x

    rows = lambda x: np.asarray(x).reshape(-1, P).T
    put("gains", rows(v["norm_gains"]))
    put("q_norm", rows(v["mla_q_norm"]))
    put("kv_norm", rows(v["mla_kv_norm"]))
    put("lb", rows(v["hgrn_lb_logits"]))
    put("o_norm", rows(v["hgrn_o_norm"]))
    put("norm1", rows(v["norm1_g_2"]))
    twice = lambda x: np.concatenate([np.asarray(x)] * 2, -1).reshape(-1, P).T
    put("dsa_q", twice(v["dsa_q_norm_2"]))
    put("dsa_k", twice(v["dsa_k_norm_2"]))
    put("nsa_q", twice(v["nsa_q_norm_2"]))
    put("nsa_k", twice(v["nsa_k_norm_2"][0]))
    put("cmp_pos", twice(v["nsa_cmp_pos_2"][0].reshape(64, 64)))
    put("conv_w", rows(v["ssd_conv_w_2"]))
    put("conv_b", rows(v["ssd_conv_b_2"]))
    put("dt_bias", v["ssd_dt_bias_2"].T)
    put("a_log", v["ssd_a_log_2"].T)
    put("ssd_d", rows(np.repeat(v["ssd_d_2"][0], 64)))
    put("ssd_norm", rows(v["ssd_norm_g_2"]))
    put("norm2", rows(v["norm2_g_2"]))
    freq = np.power(np.float32(10000.0), -np.arange(0, 64, 2, dtype=np.float32) / np.float32(64))
    put("freq", np.tile(freq, 4)[:, None])
    put("sign", np.tile(np.repeat([-1.0, 1.0], 32), 2)[:, None])
    return c


def kernel(**inputs):
    import concourse.bacc as _bacc
    from concourse import mybir as _mybir
    from concourse.bass_utils import run_bass_kernel_spmd as _run

    nc = _bacc.Bacc("TRN2", target_bir_lowering=False, num_devices=1)
    v = {k: np.asarray(a) for k, a in inputs.items()}
    arrays = {
        "weights": lay_weights(v),
        "columns": lay_columns(v),
        "tables": tables(),
        "positions": np.ascontiguousarray(v["positions"], dtype=np.int32),
        "x": np.ascontiguousarray(v["x"][0].T),
    }
    args = [nc.dram_tensor(n, a.shape, _mybir.dt.from_np(a.dtype), kind="ExternalInput").ap()
            for n, a in arrays.items()]
    out = nc.dram_tensor("out", (D, T), F32, kind="ExternalOutput").ap()
    program(nc, *args, out)
    r = _run(nc, [arrays], core_ids=[0])
    return np.ascontiguousarray(r.results[0]["out"].T)[None]
```

```python
from contextlib import ExitStack

import numpy as np

import concourse.bass as bass
from concourse import mybir

P = 128
F32 = mybir.dt.float32
F32R = mybir.dt.float32r
I32 = mybir.dt.int32
ALU = mybir.AluOpType
ACT = mybir.ActivationFunctionType
AX_X = mybir.AxisListType.X

T = 512
D = 1024
NT = D // P
QT = T // P
RING = 4
BLK = 8
NEG = -1e30
EPS = 1e-6
TAKEN = -float(2 ** 127)
TOPK = 128
MLA_H, MLA_NOPE, MLA_ROPE = 8, 128, 64
MLA_SCALE = float((MLA_NOPE + MLA_ROPE) ** -0.5)
CH = 32
N_CH = T // CH
NCMP = 31
SEL_N = 8
IDX_H = 8
PAIRS = 8
GRPS, HPG = 4, 8

S_AT = [1024, 1024 + 128, 512, 0]
S_LEN = [P * (i + 1) for i in range(QT)]
PT_AT = [0, 512, 1024, 1024 + 256]
PT_LEN = [T - P * k for k in range(QT)]
CAUSAL_AT = [0, 128, 384, 768]

COUNTS = [
    ("mla_in", 7), ("mla_rope", 2), ("mla_heads", 8), ("mla_o", 8),
    ("mlp0_up0", 16), ("mlp0_down0", 16), ("mlp0_up1", 16), ("mlp0_down1", 16),
    ("hgrn_heads", 32), ("hgrn_o", 8),
    ("mlp1_up0", 16), ("mlp1_down0", 16), ("mlp1_up1", 16), ("mlp1_down1", 16),
    ("dsa_in", 14), ("dsa_out", 16),
    ("nsa_in", 15), ("nsa_cmp", 8), ("nsa_out", 16),
    ("ssd_in", 41), ("ssd_out", 24), ("mix_out", 8),
    ("ff_up0", 16), ("ff_down0", 16), ("ff_up1", 16), ("ff_down1", 16),
]
FIRST = {}
N_BLOCKS = 0
for _name, _n in COUNTS:
    FIRST[_name] = N_BLOCKS
    N_BLOCKS += _n
SPLITS = [(FIRST[n + "_up0"], FIRST[n + "_up0"] + 64) for n in ("mlp0", "mlp1", "ff")]


def is_split(b):
    return any(lo <= b < hi for lo, hi in SPLITS)


def splits_before(b):
    return sum(max(0, min(b, hi) - lo) for lo, hi in SPLITS)

COLS = {}
N_COLS = 0
for _name, _n in [
    ("gains", 64), ("q_norm", 4), ("kv_norm", 2), ("lb", 16), ("o_norm", 1),
    ("norm1", 8), ("dsa_q", 1), ("dsa_k", 1), ("nsa_q", 1), ("nsa_k", 3), ("cmp_pos", 64),
    ("conv_w", 96), ("conv_b", 24), ("dt_bias", 1), ("a_log", 1), ("ssd_d", 16), ("ssd_norm", 16),
    ("norm2", 8), ("freq", 1), ("sign", 1),
]:
    COLS[_name] = N_COLS
    N_COLS += _n

TABS = {}
N_TABS = 0
for _name, _n in [
    ("ident", 128), ("ones", 128), ("halves", 128), ("causal", 1280), ("tri", 128), ("chunks", 128),
    ("restart32", 512), ("restart128", 512), ("cmp_bias", 128), ("cmp_seen", 128), ("sel_bias", 32),
    ("before", 64),
]:
    TABS[_name] = N_TABS
    N_TABS += _n


def tables():
    t = np.zeros((P, N_TABS), np.float32)

    def put(name, v):
        v = np.asarray(v, np.float32).reshape(v.shape[0], -1)
        t[:v.shape[0], TABS[name]:TABS[name] + v.shape[1]] = v

    p = np.arange(P)
    put("ident", np.eye(P))
    put("ones", np.ones((P, P)))
    put("halves", (p[:, None] // 64 == p[None] // 64))
    causal = np.zeros((P, 1280), np.float32)
    for i in range(QT):
        k = np.arange(S_LEN[i])
        causal[:, CAUSAL_AT[i]:CAUSAL_AT[i] + S_LEN[i]] = np.where(k[None] <= (P * i + p)[:, None], 0.0, NEG)
    put("causal", causal)
    put("tri", p[None] >= p[:, None])
    put("chunks", (p[:, None] // CH == p[None] // CH) & (p[:, None] <= p[None]))
    tok = np.arange(T)
    put("restart32", np.broadcast_to((tok % 32 != 0), (P, T)))
    put("restart128", np.broadcast_to((tok % 128 != 0), (P, T)))
    q = (P * np.arange(QT)[None, :] + p[:, None])[:, :, None]
    n = np.arange(32)[None, None]
    seen = (16 * n + 31 <= q) & (n < NCMP)
    put("cmp_bias", np.where(n < NCMP, np.where(seen, 0.0, NEG), 2 * NEG))
    put("cmp_seen", seen)
    j = np.arange(SEL_N)[None, None]
    cur = q // 64
    put("sel_bias", np.where((j == cur) | (j == 0), 1e30, np.where(j > cur, NEG, 0.0)))
    a = np.arange(SEL_N)
    put("before", np.broadcast_to((a[None] < a[:, None]).reshape(1, 64), (P, 64)))
    return t


KINDS = ("squared", "summed", "total", "root", "inverse", "spread", "scaled", "added")
NORMS = {
    "norm_0": (8, 8, 0, 1, 1, 1, 8, 0), "q_lora": (4, 4, 1, 1, 1, 1, 4, 0), "kv_lora": (2, 2, 1, 1, 1, 1, 2, 0),
    "mla_o": (8, 10, 1, 1, 1, 1, 0, 8), "norm_1": (8, 8, 0, 1, 1, 1, 8, 0), "mlp0_down": (8, 8, 1, 1, 1, 1, 0, 8),
    "norm_2": (8, 8, 0, 1, 1, 1, 8, 0), "hgrn_o": (8, 10, 1, 1, 1, 1, 0, 8), "norm_3": (8, 8, 0, 1, 1, 1, 8, 0),
    "mlp1_down": (8, 8, 1, 1, 1, 1, 0, 8), "norm_4": (8, 8, 0, 1, 1, 1, 8, 0),
    "dsa_norm": (9, 9, 0, 1, 1, 9, 9, 0), "nsa_norm": (11, 11, 0, 1, 1, 11, 11, 0),
    "ssd_norm": (16, 16, 1, 1, 1, 1, 16, 0), "norm_5": (8, 8, 0, 1, 1, 1, 8, 0),
}


START = 96224


class Memory:

    def __init__(self, nc, ctx):
        def sb(name, *free, dt=F32):
            return ctx.enter_context(nc.sbuf_tensor(name, [P, *free], dt))

        self.sem_of = {}
        self.new_sem = lambda name: ctx.enter_context(nc.semaphore(name))
        self.ring = sb("ring", RING, BLK * P)
        self.tab = sb("tab", N_TABS)
        self.col = sb("col", N_COLS)
        self.h = sb("h", NT, T)
        self.m = sb("m", NT, T)
        self.sq = sb("sq", 2, T)
        self.ssum = sb("ssum", T)
        self.std = sb("std", T)
        self.rstd = sb("rstd", T)
        self.root = sb("root", 96)
        self.inv = sb("inv", 96)

        def at(name, place, *free, dt=F32):
            return nc.alloc_sbuf_tensor_at(name, [P, *free], dt, offset=START + 4 * place)

        self.a = at("a", 0, NT, T)
        self.big = at("big", 4096, 32, T)
        self.work = at("work", 20480, 10752)
        self.extra = at("extra", 31232, 4, T)
        self.a_hi = at("a_hi", 0, NT, T, dt=F32R)
        self.hid_hi = at("hid_hi", 4096, 16, T, dt=F32R)
        self.hid_lo = at("hid_lo", 12288, 16, T, dt=F32R)
        self.ring_hi = at("ring_hi", 20480, RING, BLK * P, dt=F32R)
        self.ring_lo = at("ring_lo", 24576, RING, BLK * P, dt=F32R)
        self.a_lo = at("a_lo", 28672, NT, T, dt=F32R)
        self.ps = ctx.enter_context(nc.psum_tensor("ps", [P, 8 * T], F32))

    def sem(self, name):
        if name not in self.sem_of:
            self.sem_of[name] = self.new_sem(name)
        return self.sem_of[name]

    def past(self, name, kind):
        names = list(NORMS)
        return sum(NORMS[n][KINDS.index(kind)] for n in names[:names.index(name)])

    def norm_bank(self, name):
        return self.bank(6 if name.startswith("norm_") else 7)

    def bank(self, b, rows=slice(0, P)):
        return self.ps[rows, b * T:(b + 1) * T]

    def t(self, name, n, rows=slice(0, P), at=0):
        return self.tab[rows, TABS[name] + at:TABS[name] + at + n]

    def c(self, name, k=0, rows=slice(0, P)):
        return self.col[rows, COLS[name] + k:COLS[name] + k + 1]

    def carve(self, at, *free):
        n = int(np.prod(free))
        v = self.work[:, at:at + n]
        assert at + n <= 10752, (at, free)
        if len(free) == 2:
            v = v.rearrange("p (a b) -> p a b", a=free[0])
        if len(free) == 3:
            v = v.rearrange("p (a b c) -> p a b c", a=free[0], b=free[1])
        return v, at + n



def stream_weights(sp, M, wall, blocks):
    for u in range(RING):
        sp.dma_start(M.ring[:, u, :], wall[u]).then_inc(M.sem(f"weights_in{u}"), 16)

    def load(b, i=None):
        step = 0 if i is None else i * RING
        if is_split(b - RING):
            sp.wait_ge(M.sem("blocks_split"), step + (splits_before(b - RING) + 1))
        else:
            sp.wait_ge(M.sem("blocks_used"), step + (b - RING + 1))
        src = wall[b] if i is None else wall[bass.ds(step + b, 1), :, :].rearrange("a p n -> (a p) n")
        sp.dma_start(M.ring[:, b % RING, :], src).then_inc(M.sem(f"weights_in{b % RING}"), 16)

    edges = sorted({RING, blocks} | {e + RING for pair in SPLITS for e in pair if e + RING < blocks})
    for start, end in zip(edges, edges[1:]):
        turns = (end - start) // RING
        if turns:
            with sp.Fori(0, turns) as i:
                for u in range(RING):
                    load(start + u, i)
        for b in range(start + turns * RING, end):
            load(b)
    for u in range(RING):
        sp.wait_ge(M.sem(f"weights_in{u}"), 16 * len(range(u, blocks, RING)))


def split_weights(pool, M, lo, hi):
    ones = M.t("ones", P).unsqueeze(1).broadcast_to([P, BLK, P])
    tiles = lambda x: x.rearrange("p (k c) -> p k c", c=P)

    def split(i, u):
        b = lo + u
        s = b % RING
        wait_block(pool, M, b, i, RING)
        if i is not None:
            pool.wait_ge(M.sem("blocks_used"), i * RING + (b - RING + 1))
        pool.tensor_tensor(tiles(M.ring_hi[:, s, :]), tiles(M.ring[:, s, :]), ones, ALU.mult)
        pool.drain()
        pool.tensor_tensor(M.ring_lo[:, s, :], M.ring[:, s, :], M.ring_hi[:, s, :].bitcast(F32), ALU.subtract)
        pool.drain().then_inc(M.sem("blocks_split"), 1)

    for u in range(RING):
        split(None, u)
    with pool.Fori(1, (hi - lo) // RING) as i:
        for u in range(RING):
            split(i, u)


def block_tile(M, b, j):
    return M.ring[:, b % RING, j * P:(j + 1) * P]


def wait_block(pe, M, b, i=None, step=0):
    need = 16 * (b // RING + 1)
    pe.wait_ge(M.sem(f"weights_in{b % RING}"), need if i is None else i * (16 * step // RING) + need)


def gemm_pe(pe, M, name, tiles, per_tile, rhs, unroll, banks=4, looped=True, first_wait=None):
    used, free = M.sem("blocks_used"), M.sem(f"{name}_free")

    def tile(i, u):
        pe.wait_ge(free, u + 1 if i is None else i * unroll + (u + 1))
        for blk in range(per_tile):
            b = FIRST[name] + u * per_tile + blk
            wait_block(pe, M, b, i, unroll * per_tile)
            for k in range(BLK):
                kk = blk * BLK + k
                if first_wait and u == 0:
                    first_wait(kk)
                mm = pe.matmul(M.bank(u % banks), block_tile(M, b, k), rhs(kk),
                               start=(kk == 0), stop=(kk == per_tile * BLK - 1))
            mm.then_inc(used, 1)

    if looped:
        with pe.Fori(0, tiles // unroll) as i:
            for u in range(unroll):
                tile(i, u)
    else:
        for u in range(tiles):
            tile(None, u)


def gemm_split_pe(pe, M, name, tiles, per_tile, hi, lo, unroll, banks=4, first_wait=None):
    used, free = M.sem("blocks_used"), M.sem(f"{name}_free")

    def tile(i, u, wait=None):
        pe.wait_ge(free, u + 1 if i is None else i * unroll + (u + 1))
        for blk in range(per_tile):
            b = FIRST[name] + u * per_tile + blk
            count = splits_before(b) + 1
            pe.wait_ge(M.sem("blocks_split"), count if i is None else i * (unroll * per_tile) + count)
            for k in range(BLK):
                kk = blk * BLK + k
                if wait:
                    wait(kk)
                w_hi = M.ring_hi[:, b % RING, k * P:(k + 1) * P]
                w_lo = M.ring_lo[:, b % RING, k * P:(k + 1) * P]
                pe.matmul(M.bank(u % banks), w_hi, hi(kk), start=(kk == 0), stop=False)
                pe.matmul(M.bank(u % banks), w_hi, lo(kk), start=False, stop=False)
                mm = pe.matmul(M.bank(u % banks), w_lo, hi(kk), start=False, stop=(kk == per_tile * BLK - 1))
            mm.then_inc(used, 1)

    for u in range(unroll):
        tile(None, u, first_wait if u == 0 else None)
    with pe.Fori(1, tiles // unroll) as i:
        for u in range(unroll):
            tile(i, u)


def gemm_out(eng, M, name, tiles, per_tile, unroll, banks, move, looped=True):
    used, free = M.sem("blocks_used"), M.sem(f"{name}_free")
    eng.drain().then_inc(free, banks)

    def tile(i, u):
        done = FIRST[name] + (u + 1) * per_tile
        eng.wait_ge(used, done if i is None else i * (unroll * per_tile) + done)
        move(u if i is None else i * unroll + u, u).then_inc(free, 1)

    if looped:
        with eng.Fori(0, tiles // unroll) as i:
            for u in range(unroll):
                tile(i, u)
    else:
        for u in range(tiles):
            tile(None, u)


def gemm_ready(eng, M, name, tiles, banks):
    eng.wait_ge(M.sem(f"{name}_free"), banks + tiles)



def norm_act(act, M, name, src, n, dim):
    for k in range(n):
        if k >= 2:
            act.wait_ge(M.sem("norm_summed"), k - 1 + M.past(name, "summed"))
        act.activation(M.sq[:, k % 2, :], src(k), ACT.Square).then_inc(M.sem("norm_squared"), 1)
    norm_act_root(act, M, name, dim)


def norm_act_root(act, M, name, dim):
    act.wait_ge(M.sem("norm_total"), 1 + M.past(name, "total"))
    act.activation(M.root[:, 0:QT], M.norm_bank(name)[:, 0:QT], ACT.Sqrt, bias=M.eps, scale=1.0 / dim)\
       .then_inc(M.sem("norm_root"), 1)


def norm_total_pe(pe, M, bank, src, first=True, last=True):
    for c in range(QT):
        mm = pe.matmul(bank[:, c:c + 1], src[:, c * P:(c + 1) * P], M.t("ones", 1),
                       start=(first and c == 0), stop=last, skip_group_check=True)
    return mm


def norm_spread_pe(pe, M, bank, columns):
    for c in range(QT):
        mm = pe.matmul(bank[:, c * P:(c + 1) * P], columns(c), M.t("ident", P), start=True, stop=True)
    return mm


def norm_pe(pe, M, name, n):
    pe.wait_ge(M.sem("norm_summed"), n + M.past(name, "summed"))
    norm_total_pe(pe, M, M.norm_bank(name), M.ssum).then_inc(M.sem("norm_total"), 1)
    norm_root_pe(pe, M, name)


def norm_root_pe(pe, M, name):
    pe.wait_ge(M.sem("norm_inverse"), 1 + M.past(name, "inverse"))
    norm_spread_pe(pe, M, M.norm_bank(name), lambda c: M.inv[:, c:c + 1].broadcast_to([P, P]))\
        .then_inc(M.sem("norm_spread"), 1)


def norm_dve(dve, M, name, n):
    for k in range(n):
        dve.wait_ge(M.sem("norm_squared"), k + 1 + M.past(name, "squared"))
        if k == 0:
            dve.tensor_copy(M.ssum[:, :], M.sq[:, 0, :]).then_inc(M.sem("norm_summed"), 1)
        else:
            dve.drain()
            dve.tensor_tensor(M.ssum[:, :], M.ssum[:, :], M.sq[:, k % 2, :], ALU.add)\
               .then_inc(M.sem("norm_summed"), 1)
    norm_dve_root(dve, M, name)


def norm_dve_root(dve, M, name):
    dve.wait_ge(M.sem("norm_root"), 1 + M.past(name, "root"))
    dve.reciprocal(M.inv[:, 0:QT], M.root[:, 0:QT]).then_inc(M.sem("norm_inverse"), 1)
    dve.wait_ge(M.sem("norm_spread"), 1 + M.past(name, "spread"))


def scale_dve(dve, M, name, src, dst, gain, n):
    for k in range(n):
        dve.scalar_tensor_tensor(out=dst(k), in0=src(k), scalar=gain(k), in1=M.norm_bank(name),
                                 op0=ALU.mult, op1=ALU.mult).then_inc(M.sem("norm_scaled"), 1)


def add_norm_dve(dve, M, name, gain):
    for k in range(NT):
        dve.scalar_tensor_tensor(out=M.m[:, k, :], in0=M.m[:, k, :], scalar=gain(k),
                                 in1=M.norm_bank(name), op0=ALU.mult, op1=ALU.mult)
        dve.drain()
        dve.tensor_tensor(M.h[:, k, :], M.h[:, k, :], M.m[:, k, :], ALU.add)\
           .then_inc(M.sem("norm_added"), 1)



def att_scores_pe(pe, M, A, terms):
    for i in range(QT):
        for n, (q, k) in enumerate(terms):
            mm = pe.matmul(M.ps[:, S_AT[i]:S_AT[i] + S_LEN[i]], q[:, i * P:(i + 1) * P],
                           k[:, 0:S_LEN[i]], start=(n == 0), stop=(n == len(terms) - 1))
    mm.then_inc(M.sem(f"{A}_scores"), 1)


def att_mask_dve(dve, M, A, V, n, base, mask, scale):
    dve.wait_ge(M.sem(f"{A}_scores"), base + (n + 1))
    dve.memset(V.inv[:, n % 2, :], 0.0)
    for i in range(QT):
        s = V.p[n % 2][:, CAUSAL_AT[i]:CAUSAL_AT[i] + S_LEN[i]]
        dve.tensor_tensor_reduce(s, M.ps[:, S_AT[i]:S_AT[i] + S_LEN[i]], mask(i), scale, -3.0e38,
                                 ALU.add, ALU.max, V.top[:, n % 2, i:i + 1])
    dve.drain()
    dve.tensor_scalar(V.ntop[:, n % 2, :], V.top[:, n % 2, :], -1.0, None, ALU.mult)\
       .then_inc(M.sem(f"{A}_masked"), 1)


def att_exp_act(act, M, A, V, n, base):
    act.wait_ge(M.sem(f"{A}_masked"), base + (n + 1))
    for i in range(QT):
        s = V.p[n % 2][:, CAUSAL_AT[i]:CAUSAL_AT[i] + S_LEN[i]]
        e = act.activation(s, s, ACT.Exp, bias=V.ntop[:, n % 2, i:i + 1], scale=1.0,
                           accum_out=V.sum[:, n % 2, i:i + 1])
    e.then_inc(M.sem(f"{A}_exp"), 1)


def att_divide_dve(dve, M, A, V, n, base, gate=None):
    dve.wait_ge(M.sem(f"{A}_exp"), base + (n + 1))
    dve.reciprocal(V.inv[:, n % 2, :], V.sum[:, n % 2, :])
    dve.drain()
    if gate is not None:
        dve.tensor_tensor(V.inv[:, n % 2, :], V.inv[:, n % 2, :], gate, ALU.mult)
        dve.drain()
    for i in range(QT):
        s = V.p[n % 2][:, CAUSAL_AT[i]:CAUSAL_AT[i] + S_LEN[i]]
        d = dve.tensor_scalar(s, s, V.inv[:, n % 2, i:i + 1], None, ALU.mult)
    d.then_inc(M.sem(f"{A}_probs"), 1)


def att_turn_pe(pe, M, A, V, n, base):
    pe.wait_ge(M.sem(f"{A}_probs"), base + (n + 1))
    for k in range(QT):
        for i in range(k, QT):
            at = 3 * T + PT_AT[k] + (i - k) * P
            s = V.p[n % 2][:, CAUSAL_AT[i] + k * P:CAUSAL_AT[i] + (k + 1) * P]
            mm = pe.transpose(M.ps[:, at:at + P], s, M.t("ident", P))
    mm.then_inc(M.sem(f"{A}_turned"), 1)


def att_turned_act(act, M, A, V, n, base):
    act.wait_ge(M.sem(f"{A}_turned"), base + (n + 1))
    for at, n_col in ((0, 512), (512, 384), (1024, 384)):
        c = act.activation(V.pt[:, at:at + n_col], M.ps[:, 3 * T + at:3 * T + at + n_col], ACT.Copy)
    c.then_inc(M.sem(f"{A}_kept"), 1)


def att_out_pe(pe, M, A, V, n, base, values, bank, rows=slice(0, P)):
    pe.wait_ge(M.sem(f"{A}_kept"), base + (n + 1))
    for k in range(QT):
        mm = pe.matmul(M.ps[rows, bank * T + k * P:(bank + 1) * T], values(k),
                       V.pt[:, PT_AT[k]:PT_AT[k] + PT_LEN[k]], start=(k == 0), stop=(k == QT - 1))
    mm.then_inc(M.sem(f"{A}_out"), 1)


class AttView:

    def __init__(self, M, at):
        p0, at = M.carve(at, 1280)
        p1, at = M.carve(at, 1280)
        self.p = [p0, p1]
        self.pt, at = M.carve(at, 1408)
        self.top, at = M.carve(at, 2, QT)
        self.ntop, at = M.carve(at, 2, QT)
        self.sum, at = M.carve(at, 2, QT)
        self.inv, at = M.carve(at, 2, QT)
        self.end = at


def tile_at(buf, t):
    if isinstance(t, int):
        return buf[:, t, :]
    return buf[:, bass.ds(t, 1), :].rearrange("p a b -> p (a b)")



def to_m_act(act, M, name, per_tile, unroll, banks):
    squared, summed = M.sem("norm_squared"), M.sem("norm_summed")

    def move(t, u):
        act.wait_ge(summed, t + (1 + M.past(name, "summed")))
        act.activation(M.sq[:, u % 2, :], M.bank(u % banks), ACT.Square).then_inc(squared, 1)
        return act.activation(tile_at(M.m, t), M.bank(u % banks), ACT.Copy)

    gemm_out(act, M, name, NT, per_tile, unroll, banks, move)
    norm_act_root(act, M, name, D)


def to_m_dve(dve, M, name):
    squared, summed = M.sem("norm_squared"), M.sem("norm_summed")
    dve.memset(M.ssum[:, :], 0.0)
    dve.drain().then_inc(summed, 2)
    with dve.Fori(0, NT // 2) as i:
        for u in range(2):
            dve.wait_ge(squared, i * 2 + (u + 1) + M.past(name, "squared"))
            dve.tensor_tensor(M.ssum[:, :], M.ssum[:, :], M.sq[:, u, :], ALU.add)
            dve.drain().then_inc(summed, 1)
    norm_dve_root(dve, M, name)



class Mla:
    def __init__(self, M):
        b = M.big
        self.proj = b[:, 0:7, :]
        self.qr = b[:, 7:11, :]
        self.cos, self.sin = b[:, 11, :], b[:, 12, :]
        self.krz = b[:, 13:15, :]
        self.q, self.k, self.v = b[:, 15:17, :], b[:, 17:19, :], b[:, 19:21, :]
        self.ra, self.rb = b[:, 21, :], b[:, 22, :]
        self.pos = b[:, 23, :].bitcast(I32)
        self.angle, self.turns, self.rest = b[:, 24, :], b[:, 25, :], b[:, 26, :]
        self.att = AttView(M, 0)


TURN = float(2 * np.pi)
TURN_1 = 6.28125
TURN_2 = float(np.float32(np.round((TURN - TURN_1) * 2 ** 20) / 2 ** 20))
TURN_3 = float(TURN - TURN_1 - TURN_2)
ROUND = 12582912.0
PI = 3.1415925


def rope_angles_dve(dve, M, R):
    dve.wait_ge(M.sem("positions_in"), 16)
    dve.wait_ge(M.sem("tables_in"), 32)
    dve.tensor_copy(R.rest, R.pos)
    dve.drain()
    dve.tensor_scalar(R.angle, R.rest, M.c("freq"), None, ALU.mult)
    dve.drain()
    for out, quarter in ((R.ra, 0.0), (R.rb, 0.25)):
        dve.tensor_scalar(R.turns, R.angle, 1.0 / TURN, quarter, ALU.mult, ALU.add)
        dve.drain()
        dve.tensor_scalar(R.turns, R.turns, ROUND, ROUND, ALU.add, ALU.subtract)
        dve.drain()
        dve.scalar_tensor_tensor(out=R.rest, in0=R.turns, scalar=-TURN_1, in1=R.angle, op0=ALU.mult, op1=ALU.add)
        dve.drain()
        dve.scalar_tensor_tensor(out=R.rest, in0=R.turns, scalar=-TURN_2, in1=R.rest, op0=ALU.mult, op1=ALU.add)
        dve.drain()
        dve.scalar_tensor_tensor(out=R.rest, in0=R.turns, scalar=-TURN_3, in1=R.rest, op0=ALU.mult, op1=ALU.add)
        dve.drain()
        dve.tensor_scalar(R.rest, R.rest, quarter * TURN, PI, ALU.add, ALU.min)
        dve.drain()
        dve.tensor_scalar(out, R.rest, -PI, None, ALU.max)
        dve.drain()
    dve.nop().then_inc(M.sem("rope_angles"), 1)


def rope_tables_act(act, M, R):
    act.wait_ge(M.sem("rope_angles"), 1)
    act.activation(R.sin, R.ra, ACT.Sin)
    act.activation(R.cos, R.rb, ACT.Sin)
    act.drain().then_inc(M.sem("rope_waves"), 1)


def rope_sign_dve(dve, M, R):
    dve.wait_ge(M.sem("rope_waves"), 1)
    dve.tensor_scalar(R.sin, R.sin, M.c("sign"), None, ALU.mult)
    dve.memset(R.krz, 0.0)
    dve.drain()


def rope_swap_act(act, R, src):
    act.activation(R.ra, src, ACT.Copy)
    for g in range(4):
        o = 32 * (g ^ 1)
        act.activation(R.rb[o:o + 32, :], src[32 * g:32 * g + 32, :], ACT.Copy)
    return act.drain()


def rope_turn_dve(dve, R, dst):
    dve.tensor_tensor(R.ra, R.ra, R.cos, ALU.mult)
    dve.tensor_tensor(R.rb, R.rb, R.sin, ALU.mult)
    dve.drain()
    for rows, out in dst:
        dve.tensor_tensor(out, R.ra[rows, :], R.rb[rows, :], ALU.add)
    return dve.drain()


def mla_pe(pe, M, R):
    gemm_pe(pe, M, "mla_in", 7, 1, lambda k: M.a[:, k, :], 7, looped=False, first_wait=wait_scaled(pe, M, "norm_0"))
    norm_pe(pe, M, "q_lora", 4)
    norm_pe(pe, M, "kv_lora", 2)
    pe.wait_ge(M.sem("norm_scaled"), 4 + M.past("q_lora", "scaled"))
    for pair in range(4):
        b, at = FIRST["mla_rope"] + pair // 2, 4 * (pair % 2)
        if pair % 2 == 0:
            wait_block(pe, M, b)
        for k in range(4):
            mm = pe.matmul(M.bank(pair), block_tile(M, b, at + k), R.proj[:, k, :], start=(k == 0), stop=(k == 3))
        if pair % 2:
            mm.then_inc(M.sem("blocks_used"), 1)
    pe.wait_ge(M.sem("norm_scaled"), 2 + M.past("kv_lora", "scaled"))
    pe.wait_ge(M.sem("rope_read"), 5)

    def head(h):
        b = FIRST["mla_heads"] + h
        wait_block(pe, M, b)
        for k in range(4):
            pe.matmul(M.bank(0), block_tile(M, b, k), R.proj[:, k, :], start=(k == 0), stop=(k == 3))
        for k in range(2):
            pe.matmul(M.bank(1), block_tile(M, b, 4 + k), R.proj[:, 4 + k, :], start=(k == 0), stop=(k == 1))
        for t in range(QT):
            for k in range(2):
                mm = pe.matmul(M.bank(2)[:, t * P:(t + 1) * P], R.proj[:, 4 + k, t * P:(t + 1) * P],
                               block_tile(M, b, 6 + k), start=(k == 0), stop=(k == 1))
        mm.then_inc(M.sem("blocks_used"), 1)

    def scores(h):
        pe.wait_ge(M.sem("mla_heads_free"), h + 1)
        if h == 0:
            pe.wait_ge(M.sem("rope_turned"), 5)
        half = slice(0, P)
        att_scores_pe(pe, M, "mla", [(R.q[:, h % 2, :], R.k[:, h % 2, :]),
                                     (R.qr[half, h // 2, :], R.krz[:, h % 2, :])])

    head(0)
    scores(0)
    for h in range(MLA_H):
        if h + 1 < MLA_H:
            pe.wait_ge(M.sem("mla_masked"), h + 1)
            head(h + 1)
        att_turn_pe(pe, M, "mla", R.att, h, 0)
        if h + 1 < MLA_H:
            scores(h + 1)
        att_out_pe(pe, M, "mla", R.att, h, 0, lambda k: R.v[:, h % 2, k * P:(k + 1) * P], 6)
    gemm_ready(pe, M, "mla_y", MLA_H, 0)
    gemm_pe(pe, M, "mla_o", NT, 1, lambda k: M.a[:, k, :], 4)
    norm_pe(pe, M, "mla_o", NT + 2)


def mla_act(act, M, R):
    gemm_out(act, M, "mla_in", 7, 1, 7, 4,
             lambda t, u: act.activation(R.proj[:, t, :], M.bank(u % 4), ACT.Copy), looped=False)
    act.drain()
    norm_act(act, M, "q_lora", lambda k: R.proj[:, k, :], 4, 512)
    norm_act(act, M, "kv_lora", lambda k: R.proj[:, 4 + k, :], 2, 256)
    rope_tables_act(act, M, R)
    act.wait_ge(M.sem("norm_scaled"), 2 + M.past("kv_lora", "scaled"))
    rope_swap_act(act, R, R.proj[:, 6, :]).then_inc(M.sem("rope_read"), 1)
    for pair in range(4):
        act.wait_ge(M.sem("blocks_used"), FIRST["mla_rope"] + pair // 2 + 1)
        act.wait_ge(M.sem("rope_turned"), pair + 1)
        rope_swap_act(act, R, M.bank(pair)).then_inc(M.sem("rope_read"), 1)

    def head(h):
        act.wait_ge(M.sem("blocks_used"), FIRST["mla_heads"] + h + 1)
        act.activation(R.q[:, h % 2, :], M.bank(0), ACT.Copy)
        act.activation(R.k[:, h % 2, :], M.bank(1), ACT.Copy)
        act.activation(R.v[:, h % 2, :], M.bank(2), ACT.Copy)
        act.drain().then_inc(M.sem("mla_heads_free"), 1)

    head(0)
    att_exp_act(act, M, "mla", R.att, 0, 0)
    for h in range(MLA_H):
        if h + 1 < MLA_H:
            head(h + 1)
        att_turned_act(act, M, "mla", R.att, h, 0)
        if h + 1 < MLA_H:
            att_exp_act(act, M, "mla", R.att, h + 1, 0)
        act.wait_ge(M.sem("mla_out"), h + 1)
        act.activation(M.a[:, h, :], M.bank(6), ACT.Copy).then_inc(M.sem("mla_y_free"), 1)
    to_m_act(act, M, "mla_o", 1, 4, 4)


def mla_dve(dve, M, R):
    norm_dve(dve, M, "q_lora", 4)
    scale_dve(dve, M, "q_lora", lambda k: R.proj[:, k, :], lambda k: R.proj[:, k, :], lambda k: M.c("q_norm", k), 4)
    norm_dve(dve, M, "kv_lora", 2)
    scale_dve(dve, M, "kv_lora", lambda k: R.proj[:, 4 + k, :], lambda k: R.proj[:, 4 + k, :],
              lambda k: M.c("kv_norm", k), 2)
    rope_sign_dve(dve, M, R)
    lower, upper = slice(0, 64), slice(64, P)
    for n in range(5):
        dve.wait_ge(M.sem("rope_read"), n + 1)
        if n == 0:
            dst = [(lower, R.krz[lower, 0, :]), (upper, R.krz[upper, 1, :])]
        else:
            dst = [(slice(0, P), R.qr[:, n - 1, :])]
        rope_turn_dve(dve, R, dst).then_inc(M.sem("rope_turned"), 1)
    mask = lambda i: M.t("causal", S_LEN[i], at=CAUSAL_AT[i])
    att_mask_dve(dve, M, "mla", R.att, 0, 0, mask, MLA_SCALE)
    for h in range(MLA_H):
        att_divide_dve(dve, M, "mla", R.att, h, 0)
        if h + 1 < MLA_H:
            att_mask_dve(dve, M, "mla", R.att, h + 1, 0, mask, MLA_SCALE)
    to_m_dve(dve, M, "mla_o")
    add_norm_dve(dve, M, "mla_o", lambda k: M.c("gains", 8 + k))



HALF = 16


def split_input_dve(dve, M, name, gain):
    for k in range(NT):
        t = M.sq[:, k % 2, :]
        dve.scalar_tensor_tensor(out=t, in0=M.h[:, k, :], scalar=gain(k), in1=M.norm_bank(name),
                                 op0=ALU.mult, op1=ALU.mult)
        dve.drain()
        split_dve(dve, t, M.a_hi[:, k, :], M.a_lo[:, k, :]).then_inc(M.sem("norm_scaled"), 1)


def split_dve(dve, src, hi, lo):
    dve.tensor_copy(hi, src)
    dve.drain()
    dve.tensor_tensor(lo, src, hi.bitcast(F32), ALU.subtract)
    return dve.drain()


def mlp_split_pool(pool, M, name):
    lo = FIRST[f"{name}_up0"]
    split_weights(pool, M, lo, lo + 4 * HALF)


def mlp_pe(pe, M, name, norm):
    for part in range(2):
        if part:
            gemm_ready(pe, M, f"{name}_down0", NT, 2)
        gemm_split_pe(pe, M, f"{name}_up{part}", HALF, 1, lambda k: M.a_hi[:, k, :], lambda k: M.a_lo[:, k, :], 4,
                      first_wait=None if part else wait_scaled(pe, M, norm))
        pe.wait_ge(M.sem(f"{name}_hidden"), HALF * (part + 1) + 2)
        gemm_split_pe(pe, M, f"{name}_down{part}", NT, 2, lambda k: M.hid_hi[:, k, :], lambda k: M.hid_lo[:, k, :],
                      2, banks=2)


def mlp_norm_pe(pe, M, name, norm):
    input_norm_pe(pe, M, norm)
    mlp_pe(pe, M, name, norm)


def hidden_act(act, M, name, part):
    def move(t, u):
        act.wait_ge(M.sem(f"{name}_hidden"), t + (HALF * part + 1))
        return act.activation(M.sq[:, u % 2, :], M.bank(u % 4), ACT.Relu)

    gemm_out(act, M, f"{name}_up{part}", HALF, 1, 4, 4, move)


def hidden_dve(dve, M, name, part):
    if part == 0:
        dve.drain().then_inc(M.sem(f"{name}_hidden"), 2)
    else:
        dve.wait_ge(M.sem("blocks_used"), FIRST[f"{name}_up1"])
    with dve.Fori(0, HALF // 4) as i:
        for u in range(4):
            dve.wait_ge(M.sem(f"{name}_up{part}_free"), i * 4 + (u + 5))
            dve.tensor_tensor(M.std[:, :], M.sq[:, u % 2, :], M.sq[:, u % 2, :], ALU.mult)
            dve.drain()
            split_dve(dve, M.std[:, :], tile_at(M.hid_hi, i * 4 + u), tile_at(M.hid_lo, i * 4 + u))\
                .then_inc(M.sem(f"{name}_hidden"), 1)


def mlp_act(act, M, name):
    down = f"{name}_down1"
    hidden_act(act, M, name, 0)
    gemm_out(act, M, f"{name}_down0", NT, 2, 2, 2,
             lambda t, u: act.activation(tile_at(M.m, t), M.bank(u % 2), ACT.Copy))
    hidden_act(act, M, name, 1)
    with act.Fori(0, NT // 2) as i:
        for u in range(2):
            act.wait_ge(M.sem(f"{down}_free"), i * 2 + (u + 3))
            act.activation(M.sq[:, u, :], tile_at(M.m, i * 2 + u), ACT.Square).then_inc(M.sem("norm_squared"), 1)
    norm_act_root(act, M, f"{name}_down", D)


def mlp_dve(dve, M, name, gain):
    down = f"{name}_down1"
    hidden_dve(dve, M, name, 0)
    hidden_dve(dve, M, name, 1)
    dve.memset(M.ssum[:, :], 0.0)
    dve.drain().then_inc(M.sem(f"{down}_free"), 2)
    with dve.Fori(0, NT // 2) as i:
        for u in range(2):
            dve.wait_ge(M.sem("blocks_used"), i * 4 + (FIRST[down] + 2 * (u + 1)))
            m = tile_at(M.m, i * 2 + u)
            dve.tensor_tensor(m, m, M.bank(u), ALU.add).then_inc(M.sem(f"{down}_free"), 1)
            dve.wait_ge(M.sem("norm_squared"), i * 2 + (u + 1) + M.past(f"{name}_down", "squared"))
            dve.tensor_tensor(M.ssum[:, :], M.ssum[:, :], M.sq[:, u, :], ALU.add)
            dve.drain().then_inc(M.sem("norm_summed"), 1)
    norm_dve_root(dve, M, f"{name}_down")
    add_norm_dve(dve, M, f"{name}_down", gain)



class Hgrn:
    def __init__(self, M):
        b = M.big
        (self.sq, self.sf, self.sg, self.v, self.k, self.logf, self.b, self.d_ref, self.d_last,
         self.e_ref, self.e_neg, self.e_b, self.e_last, self.masked) = [b[:, n, :] for n in range(14)]
        self.f = b[:, 14, :]
        self.q_rel, self.k_rel, self.q_dec, self.k_dec = [b[:, n, :] for n in range(15, 19)]
        self.gate = b[:, 19, :]
        self.norm = b[:, 20, :]
        self.y = b[:, 24:32, :]
        self.kz, at = M.carve(0, 4, T)
        self.state, at = M.carve(at, N_CH, P)
        self.lb, at = M.carve(at, 8)
        self.one_lb, at = M.carve(at, 8)
        self.tmp, at = M.carve(at, 5, 8)


def hgrn_bounds_act(act, M, R):
    act.wait_ge(M.sem("hg_logits"), 1)
    act.activation(R.tmp[:, 1:3, :], R.tmp[:, 1:3, :], ACT.Exp).then_inc(M.sem("hg_logits_exp"), 1)


def hgrn_bounds_dve(dve, M, R):
    l0 = M.col[:, COLS["lb"]:COLS["lb"] + 8]
    l1 = M.col[:, COLS["lb"] + 8:COLS["lb"] + 16]
    t = [R.tmp[:, n, :] for n in range(5)]
    dve.tensor_tensor(t[0], l0, l1, ALU.max)
    dve.drain()
    dve.tensor_tensor(t[1], l0, t[0], ALU.subtract)
    dve.tensor_tensor(t[2], l1, t[0], ALU.subtract)
    dve.drain().then_inc(M.sem("hg_logits"), 1)
    dve.wait_ge(M.sem("hg_logits_exp"), 1)
    dve.tensor_tensor(t[3], t[1], t[2], ALU.add)
    dve.drain()
    dve.reciprocal(t[4], t[3])
    dve.drain()
    dve.tensor_tensor(t[1], t[1], t[4], ALU.mult)
    dve.tensor_tensor(t[2], t[2], t[4], ALU.mult)
    dve.drain()
    dve.tensor_tensor(t[2], t[2], t[1], ALU.add)
    dve.drain()
    dve.tensor_tensor(R.lb, t[2], t[1], ALU.subtract)
    dve.drain()
    dve.tensor_scalar(R.one_lb, R.lb, -1.0, 1.0, ALU.mult, ALU.add)
    dve.memset(R.kz, 0.0)
    dve.memset(R.masked, 0.0)
    dve.drain()



def hgrn_pe(pe, M, R):
    used = M.sem("blocks_used")
    readers = ["hg_banks_free", "hg_banks_free", "hg_v", "hg_gate_free"]

    def project(j, i, ahead, between=None):
        b = FIRST["hgrn_heads"] + 4 * ahead + j
        wait_block(pe, M, b, i, 4)
        if ahead:
            pe.wait_ge(M.sem(readers[j]), i + 1)
        if j != 2:
            for k in range(BLK):
                if j == 0 and not ahead:
                    wait_scaled(pe, M, "norm_2")(k)
                if k == 4 and between:
                    between()
                mm = pe.matmul(M.bank(j), block_tile(M, b, k), M.a[:, k, :], start=(k == 0), stop=(k == 7))
        else:
            for t in range(QT):
                for k in range(BLK):
                    mm = pe.matmul(M.bank(2)[:, t * P:(t + 1) * P], M.a[:, k, t * P:(t + 1) * P],
                                   block_tile(M, b, k), start=(k == 0), stop=(k == 7))
        mm.then_inc(used, 1)

    def states(tt, bank):
        for r in range(4):
            mm = pe.matmul(M.bank(bank)[:, r * P:(r + 1) * P], R.kz[:, r, tt * P:(tt + 1) * P],
                           R.v[:, tt * P:(tt + 1) * P], start=True, stop=True)
        mm.then_inc(M.sem("hg_chunk_states"), 1)

    def total(i):
        pe.wait_ge(M.sem("hg_squared"), i + 1)
        norm_total_pe(pe, M, M.bank(7), M.sq[:, 0, :]).then_inc(M.sem("hg_total"), 1)

    def spread(i):
        pe.wait_ge(M.sem("hg_inverse"), i + 1)
        norm_spread_pe(pe, M, M.bank(7), lambda c: M.inv[:, c:c + 1].broadcast_to([P, P]))\
            .then_inc(M.sem("hg_spread"), 1)

    def head(i, nxt, prev):
        if nxt:
            project(0, i, 1, (lambda: total(i - 1)) if prev else None)
            project(1, i, 1, (lambda: spread(i - 1)) if prev else None)
        elif prev:
            total(i - 1)
            spread(i - 1)
        pe.wait_ge(M.sem("hg_rel"), i + 1)
        if prev:
            pe.wait_ge(M.sem("hg_y"), i)
        for t in range(QT):
            s = slice(t * P, (t + 1) * P)
            mm = pe.matmul(M.bank(4)[:, s], R.k_rel[:, s], R.q_rel[:, s], start=True, stop=True)
        mm.then_inc(M.sem("hg_pairs"), 1)
        pe.wait_ge(M.sem("hg_dec"), i + 1)
        for t in range(QT):
            s = slice(t * P, (t + 1) * P)
            mm = pe.transpose(M.bank(5)[:, s], R.k_dec[:, s], M.t("ident", P))
        mm.then_inc(M.sem("hg_keys_turned"), 1)
        if nxt:
            project(2, i, 1)
        pe.wait_ge(M.sem("hg_v"), i + 1)
        pe.wait_ge(M.sem("hg_keys_kept"), i + 1)
        states(0, 6)
        states(1, 5)
        pe.wait_ge(M.sem("hg_chained"), i * 4 + 1)
        states(2, 6)
        pe.wait_ge(M.sem("hg_chained"), i * 4 + 2)
        states(3, 5)
        if nxt:
            project(3, i, 1)
        pe.wait_ge(M.sem("hg_chained"), i * 4 + 4)
        pe.wait_ge(M.sem("hg_pairs_masked"), i + 1)
        for t in range(QT):
            s = slice(t * P, (t + 1) * P)
            pe.matmul(M.bank(4)[:, s], R.v[:, s], R.masked[:, s], start=(t == 0), stop=False,
                      skip_group_check=True)
            for r in range(4):
                c = 4 * t + r
                w = slice(c * CH, (c + 1) * CH)
                mm = pe.matmul(M.bank(4)[:, w], R.state[:, c, :], R.q_dec[:, w], start=False, stop=(c == N_CH - 1),
                               skip_group_check=True)
        mm.then_inc(M.sem("hg_out"), 1)

    for j in range(4):
        project(j, 0, 0)
    head(0, True, False)
    with pe.Fori(1, MLA_H - 1) as i:
        head(i, True, True)
    head(7, False, True)
    total(7)
    spread(7)
    pe.wait_ge(M.sem("hg_y"), 8)
    gemm_pe(pe, M, "hgrn_o", NT, 1, lambda k: R.y[:, k, :], 4)
    norm_pe(pe, M, "hgrn_o", NT + 2)


def hgrn_act(act, M, R):
    hgrn_bounds_act(act, M, R)

    def values(i, ahead):
        act.activation(R.v, M.bank(2), ACT.Copy).then_inc(M.sem("hg_v"), 1)

    def front(i, ahead):
        act.wait_ge(M.sem("blocks_used"), i * 4 + (FIRST["hgrn_heads"] + 4 * (ahead + 1)))
        act.activation(R.sf, M.bank(1), ACT.Sigmoid).then_inc(M.sem("hg_sig"), 1)
        act.activation(R.sq, M.bank(0), ACT.Sigmoid).then_inc(M.sem("hg_sig"), 1)
        act.activation(R.sg, M.bank(3), ACT.Sigmoid).then_inc(M.sem("hg_sig"), 1)
        if not ahead:
            values(i, 0)
        act.wait_ge(M.sem("hg_f"), i + (ahead + 1))
        act.activation(R.logf, R.f, ACT.Ln).then_inc(M.sem("hg_logf"), 1)
        act.wait_ge(M.sem("hg_diffs"), i + (ahead + 1))
        act.activation(R.e_ref, R.d_ref, ACT.Exp).then_inc(M.sem("hg_exp"), 1)
        act.activation(R.e_neg, R.d_ref, ACT.Exp, scale=-1.0).then_inc(M.sem("hg_exp"), 1)
        act.activation(R.e_last, R.d_last, ACT.Exp).then_inc(M.sem("hg_exp"), 1)
        act.activation(R.e_b, R.b, ACT.Exp).then_inc(M.sem("hg_exp"), 1)

    def body(i, nxt):
        act.wait_ge(M.sem("hg_keys_turned"), i + 1)
        for r in range(4):
            rows = slice(32 * r, 32 * r + 32)
            act.activation(R.kz[rows, r, :], M.bank(5, rows), ACT.Copy)
        act.drain().then_inc(M.sem("hg_keys_kept"), 1)
        if nxt:
            front(i, 1)
        act.wait_ge(M.sem("hg_out"), i + 1)
        act.activation(M.sq[:, 0, :], M.bank(4), ACT.Square).then_inc(M.sem("hg_squared"), 1)
        if nxt:
            values(i, 1)
        act.wait_ge(M.sem("hg_total"), i + 1)
        act.activation(M.root[:, 0:QT], M.bank(7)[:, 0:QT], ACT.Sqrt, bias=M.eps, scale=1.0 / P)\
           .then_inc(M.sem("hg_root"), 1)

    front(0, 0)
    with act.Fori(0, 7) as i:
        body(i, True)
    body(7, False)
    to_m_act(act, M, "hgrn_o", 1, 4, 4)


def hgrn_dve(dve, M, R):
    hgrn_bounds_dve(dve, M, R)
    chunks = lambda x: x.rearrange("p (c t) -> p c t", t=CH)
    mask = M.t("chunks", P).bitcast(I32).unsqueeze(1).broadcast_to([P, QT, P])

    def column(x, i, ahead):
        return x[:, i + ahead:i + ahead + 1] if isinstance(i, int) else x[:, bass.ds(i + ahead, 1)]

    def front(i, ahead):
        dve.wait_ge(M.sem("hg_sig"), i * 3 + (3 * ahead + 1))
        dve.tensor_scalar(R.f, R.sf, column(R.one_lb, i, ahead), column(R.lb, i, ahead), ALU.mult, ALU.add)
        dve.drain().then_inc(M.sem("hg_f"), 1)
        dve.tensor_scalar(R.k, R.f, -1.0, 1.0, ALU.mult, ALU.add)
        dve.wait_ge(M.sem("hg_sig"), i * 3 + (3 * ahead + 3))
        dve.tensor_tensor(R.sq, R.sq, M.bank(0), ALU.mult)
        dve.drain().then_inc(M.sem("hg_banks_free"), 1)
        dve.wait_ge(M.sem("hg_logf"), i + (ahead + 1))
        dve.tensor_tensor_scan(R.b, M.t("restart32", T), R.logf, 0.0, ALU.mult, ALU.add)
        dve.drain()
        b = chunks(R.b)
        dve.tensor_tensor(chunks(R.d_ref), b, b[:, :, 16:17].broadcast_to([P, N_CH, CH]), ALU.subtract)
        dve.tensor_tensor(chunks(R.d_last), b[:, :, 31:32].broadcast_to([P, N_CH, CH]), b, ALU.subtract)
        dve.drain().then_inc(M.sem("hg_diffs"), 1)
        dve.wait_ge(M.sem("hg_exp"), i * 4 + (4 * ahead + 2))
        dve.tensor_tensor(R.q_rel, R.sq, R.e_ref, ALU.mult)
        dve.tensor_tensor(R.k_rel, R.k, R.e_neg, ALU.mult)
        dve.drain().then_inc(M.sem("hg_rel"), 1)
        dve.wait_ge(M.sem("hg_exp"), i * 4 + (4 * ahead + 4))
        dve.tensor_tensor(R.k_dec, R.k, R.e_last, ALU.mult)
        dve.drain().then_inc(M.sem("hg_dec"), 1)

    def front_rest():
        dve.tensor_tensor(R.q_dec, R.sq, R.e_b, ALU.mult)
        dve.tensor_tensor(R.gate, R.sg, M.bank(3), ALU.mult)
        dve.drain().then_inc(M.sem("hg_gate_free"), 1)

    def body(i, nxt):
        dve.wait_ge(M.sem("hg_pairs"), i + 1)
        dve.memset(R.state[:, 0, :], 0.0)
        dve.copy_predicated(R.masked.rearrange("p (a b) -> p a b", a=QT), mask,
                            M.bank(4).rearrange("p (a b) -> p a b", a=QT))
        dve.drain().then_inc(M.sem("hg_pairs_masked"), 1)
        for t in range(QT):
            dve.wait_ge(M.sem("hg_chunk_states"), i * 4 + (t + 1))
            for r in range(4):
                c = 4 * t + r
                if c == N_CH - 1:
                    continue
                dve.scalar_tensor_tensor(out=R.state[:, c + 1, :], in0=R.state[:, c, :],
                                         scalar=R.e_b[:, c * CH + 31:c * CH + 32],
                                         in1=M.bank(6 - t % 2)[:, r * P:(r + 1) * P], op0=ALU.mult, op1=ALU.add)
                dve.drain()
            dve.nop().then_inc(M.sem("hg_chained"), 1)
        if nxt:
            front(i, 1)
        dve.wait_ge(M.sem("hg_root"), i + 1)
        dve.reciprocal(M.inv[:, 0:QT], M.root[:, 0:QT]).then_inc(M.sem("hg_inverse"), 1)
        dve.wait_ge(M.sem("hg_spread"), i + 1)
        dve.scalar_tensor_tensor(out=R.norm, in0=R.gate, scalar=M.c("o_norm"), in1=M.bank(7),
                                 op0=ALU.mult, op1=ALU.mult)
        dve.drain()
        dve.tensor_tensor(tile_at(R.y, i), R.norm, M.bank(4), ALU.mult).then_inc(M.sem("hg_y"), 1)
        if nxt:
            dve.drain()
            front_rest()

    front(0, 0)
    front_rest()
    with dve.Fori(0, 7) as i:
        body(i, True)
    body(7, False)
    to_m_dve(dve, M, "hgrn_o")
    add_norm_dve(dve, M, "hgrn_o", lambda k: M.c("gains", 40 + k))



LOWER, UPPER = slice(0, 64), slice(64, P)
HALVES = (LOWER, UPPER)
SCALE_64 = 0.125


def head_norms_pe(pe, M, name, n):
    for k in range(n):
        pe.wait_ge(M.sem("norm_squared"), k + 1 + M.past(name, "squared"))
        for c in range(QT):
            mm = pe.matmul(M.bank(7)[:, 8 * k + 2 * c:8 * k + 2 * c + 2], M.sq[:, k % 2, c * P:(c + 1) * P],
                           M.t("halves", P)[:, 0:P:64], start=True, stop=True)
        mm.then_inc(M.sem("norm_summed"), 1)
    pe.wait_ge(M.sem("norm_inverse"), 1 + M.past(name, "inverse"))
    for k in range(n):
        if k >= 2:
            pe.wait_ge(M.sem("norm_scaled"), k - 1 + M.past(name, "scaled"))
        for half in range(2):
            mm = norm_spread_pe(pe, M, M.bank(6 + k % 2, HALVES[half]), lambda c:
                                M.inv[:, 8 * k + 2 * c + half:8 * k + 2 * c + half + 1].broadcast_to([P, 64]))
        mm.then_inc(M.sem("norm_spread"), 1)


def head_norms_act(act, M, name, srcs):
    for k, src in enumerate(srcs):
        if k >= 2:
            act.wait_ge(M.sem("norm_summed"), k - 1 + M.past(name, "summed"))
        act.activation(M.sq[:, k % 2, :], src, ACT.Square).then_inc(M.sem("norm_squared"), 1)
    n = len(srcs)
    act.wait_ge(M.sem("norm_summed"), n + M.past(name, "summed"))
    act.activation(M.root[:, 0:8 * n], M.bank(7)[:, 0:8 * n], ACT.Sqrt, bias=M.eps, scale=1.0 / 64)\
       .then_inc(M.sem("norm_root"), 1)


def head_norms_dve(dve, M, name, srcs, gains):
    n = len(srcs)
    dve.wait_ge(M.sem("norm_root"), 1 + M.past(name, "root"))
    dve.reciprocal(M.inv[:, 0:8 * n], M.root[:, 0:8 * n]).then_inc(M.sem("norm_inverse"), 1)
    for k, (src, gain) in enumerate(zip(srcs, gains)):
        dve.wait_ge(M.sem("norm_spread"), k + 1 + M.past(name, "spread"))
        dve.scalar_tensor_tensor(out=src, in0=src, scalar=gain, in1=M.bank(6 + k % 2),
                                 op0=ALU.mult, op1=ALU.mult).then_inc(M.sem("norm_scaled"), 1)
    dve.drain()


class Pairs:

    def __init__(self, M, name, unroll, q, att, staged, kinds, y, more=None):
        self.more = more
        self.name, self.unroll, self.q, self.att, self.staged, self.kinds, self.y = \
            name, unroll, q, att, staged, kinds, y
        self.units = [(u, half, kind) for u in range(unroll) for half in range(2) for kind in range(len(kinds))]
        self.turns = PAIRS // unroll

    def stage_pool(self, pool, M, i, again):
        if again:
            pool.wait_ge(M.sem(f"{self.name}_scores"), i * len(self.units))
        for u in range(self.unroll):
            if again:
                pool.nop()
            pool.tensor_copy(self.staged[:, u, :], tile_at(self.q, i * self.unroll + u))
        if self.more is not None:
            if again:
                pool.wait_ge(M.sem(f"{self.name}_out"), i * len(self.units))
            self.more(pool, i)
        pool.drain().then_inc(M.sem(f"{self.name}_staged"), 1)

    def pe(self, pe, M, extra=None):
        A, V, per = self.name, self.att, len(self.units)
        with pe.Fori(0, self.turns) as i:
            base = i * per
            pe.wait_ge(M.sem(f"{A}_staged"), i + 1)

            def scores(n):
                u, half, kind = self.units[n]
                if n:
                    pe.wait_ge(M.sem(f"{A}_masked"), base + n)
                rows = HALVES[half]
                att_scores_pe(pe, M, A, [(self.staged[rows, u, :], self.kinds[kind][0][rows, :])])

            scores(0)
            scores(1)
            for n, (u, half, kind) in enumerate(self.units):
                att_turn_pe(pe, M, A, V, n, base)
                if n + 2 < per:
                    scores(n + 2)
                rows = HALVES[half]
                pe.wait_ge(M.sem(f"{A}_kept"), base + (n + 1))
                bank = 6 + u % 2
                first = kind == 0
                if extra and kind == 0:
                    extra(i, u, half, bank)
                    first = False
                values = self.kinds[kind][1]
                for k in range(QT):
                    mm = pe.matmul(M.ps[rows, bank * T + k * P:(bank + 1) * T],
                                   values[:, k * P + 64 * half:k * P + 64 * half + 64],
                                   V.pt[:, PT_AT[k]:PT_AT[k] + PT_LEN[k]],
                                   start=(first and k == 0), stop=(kind == len(self.kinds) - 1 and k == QT - 1),
                                   skip_group_check=True)
                mm.then_inc(M.sem(f"{A}_out"), 1)

    def act(self, act, M):
        A, V, per = self.name, self.att, len(self.units)
        with act.Fori(0, self.turns) as i:
            base = i * per
            att_exp_act(act, M, A, V, 0, base)
            att_exp_act(act, M, A, V, 1, base)
            for n, (u, half, kind) in enumerate(self.units):
                att_turned_act(act, M, A, V, n, base)
                if n + 2 < per:
                    att_exp_act(act, M, A, V, n + 2, base)
                if half and kind == len(self.kinds) - 1:
                    act.wait_ge(M.sem(f"{A}_out"), base + (n + 1))
                    act.activation(tile_at(self.y, i * self.unroll + u), M.bank(6 + u % 2), ACT.Copy)\
                       .then_inc(M.sem(f"{A}_y"), 1)

    def dve(self, dve, M, gate=None):
        A, V, per = self.name, self.att, len(self.units)
        with dve.Fori(0, self.turns) as i:
            base = i * per

            def mask(n):
                u, half, kind = self.units[n]
                m = self.kinds[kind][2](half)
                att_mask_dve(dve, M, A, V, n, base,
                             lambda t: m[:, CAUSAL_AT[t]:CAUSAL_AT[t] + S_LEN[t]], SCALE_64)

            def divide(n):
                u, half, kind = self.units[n]
                att_divide_dve(dve, M, A, V, n, base, gate and gate(i, u, half, kind))

            mask(0)
            mask(1)
            divide(0)
            for n in range(1, per):
                divide(n)
                if n + 1 < per:
                    mask(n + 1)



def branch_out_pe(pe, M, name, y, per_tile, unroll, wait_y=None):
    used = M.sem("blocks_used")
    with pe.Fori(0, NT // unroll) as i:
        for u in range(unroll):
            pe.wait_ge(M.sem(f"{name}_free"), i * unroll + (u + 1))
            b = FIRST[name] + u * (1 + per_tile)
            wait_block(pe, M, b, i, unroll * (1 + per_tile))
            for k in range(BLK):
                mm = pe.matmul(M.bank(2 * (u % 2)), block_tile(M, b, k), M.a[:, k, :], start=(k == 0), stop=(k == 7))
            mm.then_inc(used, 1)
            for blk in range(per_tile):
                wait_block(pe, M, b + 1 + blk, i, unroll * (1 + per_tile))
                if wait_y:
                    wait_y(blk)
                for k in range(BLK):
                    kk = blk * BLK + k
                    mm = pe.matmul(M.bank(2 * (u % 2) + 1), block_tile(M, b + 1 + blk, k), y(kk),
                                   start=(kk == 0), stop=(kk == per_tile * BLK - 1))
                mm.then_inc(used, 1)


def branch_out_act(act, M, name, per_tile, unroll):
    with act.Fori(0, NT // unroll) as i:
        for u in range(unroll):
            act.wait_ge(M.sem(f"{name}_free"), i * unroll + (u + 1))
            act.wait_ge(M.sem("blocks_used"), i * (unroll * (1 + per_tile)) + FIRST[name] + u * (1 + per_tile) + 1)
            act.activation(M.sq[:, u % 2, :], M.bank(2 * (u % 2)), ACT.Sigmoid).then_inc(M.sem(f"{name}_gate"), 1)


def branch_out_dve(dve, M, name, per_tile, unroll, first):
    dve.drain().then_inc(M.sem(f"{name}_free"), 2)
    with dve.Fori(0, NT // unroll) as i:
        for u in range(unroll):
            dve.wait_ge(M.sem(f"{name}_gate"), i * unroll + (u + 1))
            dve.wait_ge(M.sem("blocks_used"), i * (unroll * (1 + per_tile)) + FIRST[name] + (u + 1) * (1 + per_tile))
            m = tile_at(M.m, i * unroll + u)
            if first:
                dve.tensor_tensor(m, M.bank(2 * (u % 2) + 1), M.sq[:, u % 2, :], ALU.mult)
            else:
                dve.tensor_tensor(M.ssum[:, :], M.bank(2 * (u % 2) + 1), M.sq[:, u % 2, :], ALU.mult)
                dve.drain()
                dve.tensor_tensor(m, m, M.ssum[:, :], ALU.add)
            dve.drain().then_inc(M.sem(f"{name}_free"), 1)



class Dsa:
    def __init__(self, M):
        b = M.big
        self.proj = b[:, 0:14, :]
        self.key, self.value_t = b[:, 0, :], b[:, 1, :]
        self.iq = b[:, 2:4, :]
        self.q = b[:, 6:14, :]
        self.value = b[:, 14, :]
        self.y = b[:, 24:32, :]
        self.relu = b[:, 15:17, :]
        self.ikz = b[:, 17:21, :]
        self.att = AttView(M, 0)
        self.mask, at = M.carve(self.att.end, 1280)
        self.staged, at = M.carve(at, 4, T)
        self.iw, at = M.carve(at, QT, 8)
        self.best, at = M.carve(at, 8)
        self.pairs = Pairs(M, "dsa", 4, self.q, self.att, self.staged,
                           [(self.key, self.value, lambda half: self.mask)], self.y)


def dsa_pe(pe, M, R):
    used, free = M.sem("blocks_used"), M.sem("dsa_in_free")

    def project(t):
        pe.wait_ge(free, t + 1)
        b = FIRST["dsa_in"] + t
        wait_block(pe, M, b)
        for k in range(BLK):
            if t == 0:
                wait_scaled(pe, M, "norm_4")(k)
            mm = pe.matmul(M.bank(t % 2), block_tile(M, b, k), M.a[:, k, :], start=(k == 0), stop=(k == 7))
        mm.then_inc(used, 1)

    for t in range(6):
        project(t)
    pe.wait_ge(free, 2 + 6)
    for n, src in enumerate((R.value_t, R.proj[:, 5, :])):
        for t in range(QT):
            mm = pe.transpose(M.bank(2 + n)[:, t * P:(t + 1) * P], src[:, t * P:(t + 1) * P], M.t("ident", P))
    mm.then_inc(M.sem("dsa_turned_in"), 1)
    pe.wait_ge(M.sem("dsa_ikz"), 1)
    n = 0
    for i in range(1, QT):
        for h in range(IDX_H):
            if n >= 2:
                pe.wait_ge(M.sem("dsa_relu"), n - 1)
            pe.matmul(M.bank(4 + n % 2)[:, 0:S_LEN[i]], R.iq[:, h // 4, i * P:(i + 1) * P],
                      R.ikz[:, h % 4, 0:S_LEN[i]], start=True, stop=True).then_inc(M.sem("dsa_index"), 1)
            n += 1
    for t in range(6, 14):
        project(t)
    head_norms_pe(pe, M, "dsa_norm", 9)
    R.pairs.pe(pe, M)
    pe.wait_ge(M.sem("dsa_y"), PAIRS)
    branch_out_pe(pe, M, "dsa_out", lambda k: R.y[:, k, :], 1, 2)


def dsa_act(act, M, R):
    def out(t):
        act.wait_ge(M.sem("blocks_used"), FIRST["dsa_in"] + t + 1)
        if t == 4:
            for j in range(4):
                rows = slice(32 * j, 32 * j + 32)
                act.activation(R.ikz[rows, j, :], M.bank(0, rows), ACT.Copy)
            act.drain().then_inc(M.sem("dsa_ikz"), 1)
            act.nop().then_inc(M.sem("dsa_in_free"), 1)
        else:
            act.activation(R.proj[:, t, :], M.bank(t % 2), ACT.Copy).then_inc(M.sem("dsa_in_free"), 1)

    act.wait_ge(M.sem("dsa_zeroed"), 1)
    act.drain().then_inc(M.sem("dsa_in_free"), 2)
    for t in range(6):
        out(t)
    act.wait_ge(M.sem("dsa_turned_in"), 1)
    act.activation(R.value, M.bank(2), ACT.Copy)
    act.activation(R.iw, M.bank(3).rearrange("p (t c) -> p t c", t=QT)[:, :, 0:8], ACT.Copy)
    act.drain().then_inc(M.sem("dsa_iw"), 1)
    n = 0
    for i in range(1, QT):
        for h in range(IDX_H):
            act.wait_ge(M.sem("dsa_index"), n + 1)
            if n >= 2:
                act.wait_ge(M.sem("dsa_weighted"), n - 1)
            act.activation(R.relu[:, n % 2, 0:S_LEN[i]], M.bank(4 + n % 2)[:, 0:S_LEN[i]], ACT.Relu)\
               .then_inc(M.sem("dsa_relu"), 1)
            n += 1
    for t in range(6, 14):
        out(t)
    act.drain()
    head_norms_act(act, M, "dsa_norm", [R.key] + [R.q[:, k, :] for k in range(8)])
    R.pairs.act(act, M)
    branch_out_act(act, M, "dsa_out", 1, 2)


def dsa_dve(dve, M, R):
    dve.memset(R.ikz, 0.0)
    dve.tensor_copy(R.mask[:, 0:P], M.t("causal", P))
    dve.drain().then_inc(M.sem("dsa_zeroed"), 1)
    dve.wait_ge(M.sem("dsa_iw"), 1)
    n = 0
    for i in range(1, QT):
        s = R.mask[:, CAUSAL_AT[i]:CAUSAL_AT[i] + S_LEN[i]]
        for h in range(IDX_H):
            dve.wait_ge(M.sem("dsa_relu"), n + 1)
            dve.scalar_tensor_tensor(out=s, in0=R.relu[:, n % 2, 0:S_LEN[i]], scalar=R.iw[:, i, h:h + 1],
                                     in1=s if h else M.t("causal", S_LEN[i], at=CAUSAL_AT[i]),
                                     op0=ALU.mult, op1=ALU.add)
            dve.drain().then_inc(M.sem("dsa_weighted"), 1)
            n += 1
    for i in range(1, QT):
        s = R.mask[:, CAUSAL_AT[i]:CAUSAL_AT[i] + S_LEN[i]]
        for r in range(TOPK // 8):
            dve.max(R.best, s)
            dve.drain()
            dve.match_replace(s, R.best, s, TAKEN)
            dve.drain()
        dve.tensor_scalar(s, s, TAKEN, NEG, ALU.not_equal, ALU.mult)
    dve.drain()
    head_norms_dve(dve, M, "dsa_norm", [R.key] + [R.q[:, k, :] for k in range(8)],
                   [M.c("dsa_k")] + [M.c("dsa_q")] * 8)
    R.pairs.dve(dve, M)
    branch_out_dve(dve, M, "dsa_out", 1, 2, first=True)


def dsa_pool(pool, M, R):
    pairs_pool(pool, M, R.pairs, "dsa_norm", 9)


def pairs_pool(pool, M, pairs, normed, n):
    pool.wait_ge(M.sem("norm_scaled"), n + M.past(normed, "scaled"))
    pairs.stage_pool(pool, M, 0, False)
    with pool.Fori(1, pairs.turns) as i:
        pairs.stage_pool(pool, M, i, True)



assert T <= 512, "the window of 512 tokens holds all keys up to the query"


class Nsa:
    def __init__(self, M):
        b = M.big
        self.proj = b[:, 0:15, :]
        self.kc, self.vc, self.ks, self.vs, self.kw, self.vw, self.ng = [b[:, n, :] for n in range(7)]
        self.q = b[:, 7:15, :]
        flat = lambda t, n: b[:, t:t + 2, :].rearrange("p a b -> p (a b)")[:, 0:n]
        self.kin = flat(15, 32 * NCMP).rearrange("p (l n) -> p l n", n=NCMP)
        self.vin = flat(17, 32 * NCMP).rearrange("p (l n) -> p l n", n=NCMP)
        self.p = b[:, 19:23, :]
        self.pt = b[:, 15:19, :]
        self.pt_flat = self.pt.rearrange("p a b -> p (a b)")
        self.kcmp = b[:, 23, :]
        self.val_s, self.val_w = b[:, 0, :], b[:, 1, :]
        self.y = b[:, 24:32, :]
        self.att = AttView(M, 0)
        self.masks, at = M.carve(self.att.end, 2, 1280)
        self.staged, at = M.carve(at, 2, T)
        self.pt_staged, at = M.carve(at, 2, 2 * P)
        self.vcmp, at = M.carve(at, 4, 32)
        self.vz, at = M.carve(at, QT, P)
        self.gates, at = M.carve(at, 48, QT)
        self.imp, at = M.carve(at, 8, SEL_N)
        self.z, at = M.carve(at, 8, 36)
        self.rank, at = M.carve(at, 64)
        self.gt, at = M.carve(at, 8, 64)
        self.eq, at = M.carve(at, 8, 64)
        self.scores, at = M.carve(at, 8, SEL_N)
        self.top, at = M.carve(at, 16)
        self.sum, at = M.carve(at, 16)
        self.part, at = M.carve(at, P)
        self.pairs = Pairs(M, "nsa", 2, self.q, self.att, self.staged,
                           [(self.ks, self.val_s, lambda half: self.masks[:, half, :]),
                            (self.kw, self.val_w, lambda half: M.t("causal", 1280))], self.y, self.stage_pt)

    def stage_pt(self, pool, i):
        for half in range(2):
            pool.tensor_copy(self.pt_staged[:, half, :], self.pt_flat[:, bass.ds(i * (2 * P) + 8 * P * half, 2 * P)])


def nsa_pe(pe, M, R):
    used = M.sem("blocks_used")
    pe.wait_ge(M.sem("dsa_out_free"), NT + 2)
    gemm_pe(pe, M, "nsa_in", 15, 1, lambda k: M.a[:, k, :], 15, looped=False)
    pe.wait_ge(M.sem("nsa_windows"), 1)
    for b in range(8):
        wait_block(pe, M, FIRST["nsa_cmp"] + b)
        for j in range(4):
            l = 4 * b + j
            for n, src in enumerate((R.kin, R.vin)):
                mm = pe.matmul(M.bank(4 + n)[:, 0:NCMP], block_tile(M, FIRST["nsa_cmp"] + b, 2 * j + n),
                               src[:, l, :], start=(l == 0), stop=(l == 31))
        mm.then_inc(used, 1)
    gemm_ready(pe, M, "nsa_in", 15, 4)
    for n, src in enumerate((R.vs, R.vw, R.ng)):
        for t in range(QT):
            mm = pe.transpose(M.bank(n)[:, t * P:(t + 1) * P], src[:, t * P:(t + 1) * P], M.t("ident", P))
    mm.then_inc(M.sem("nsa_turned_in"), 1)
    pe.wait_ge(M.sem("nsa_vcmp"), 1)
    pe.transpose(M.bank(3)[:, 0:P], R.vcmp.rearrange("p a b -> p (a b)"), M.t("ident", P))\
      .then_inc(M.sem("nsa_vcmp_turned"), 1)
    head_norms_pe(pe, M, "nsa_norm", 11)
    pe.wait_ge(M.sem("norm_scaled"), 11 + M.past("nsa_norm", "scaled"))
    for n in range(4):
        half, quad = n // 2, n % 2
        for j in range(4):
            for i in range(QT):
                at = j * P + i * 32
                mm = pe.matmul(M.bank(n)[:, at:at + 32], R.q[HALVES[half], 4 * quad + j, i * P:(i + 1) * P],
                               R.kcmp[HALVES[half], 0:32], start=True, stop=True)
        mm.then_inc(M.sem("nsa_cmp_scores"), 1)
    for n in range(4):
        pe.wait_ge(M.sem("nsa_cmp_gated"), n + 1)
        if n >= 2:
            pe.wait_ge(M.sem("nsa_cmp_kept"), n - 1)
        for j in range(4):
            mm = pe.transpose(M.bank(4 + n % 2)[:, j * P:(j + 1) * P], R.p[:, n, j * P:(j + 1) * P], M.t("ident", P))
        mm.then_inc(M.sem("nsa_cmp_turned"), 1)
    pe.wait_ge(M.sem("nsa_cmp_kept"), 4)

    def compressed(i, u, half, bank):
        for t in range(QT):
            pe.matmul(M.ps[HALVES[half], bank * T + t * P:bank * T + (t + 1) * P],
                      R.vz[:, t, 64 * half:64 * half + 64],
                      R.pt_staged[:, half, u * P:(u + 1) * P],
                      start=(t == 0), stop=False, skip_group_check=True)

    R.pairs.pe(pe, M, compressed)
    pe.wait_ge(M.sem("nsa_y"), PAIRS)
    branch_out_pe(pe, M, "nsa_out", lambda k: R.y[:, k, :], 1, 2)


def nsa_act(act, M, R):
    def out(t, u):
        if t == 6:
            return act.activation(R.ng, M.bank(u % 4), ACT.Sigmoid)
        return act.activation(R.proj[:, t, :], M.bank(u % 4), ACT.Copy)

    gemm_out(act, M, "nsa_in", 15, 1, 15, 4, out, looped=False)
    act.wait_ge(M.sem("blocks_used"), FIRST["nsa_cmp"] + 8)
    act.wait_ge(M.sem("nsa_zeroed"), 1)
    act.activation(R.kcmp[:, 0:NCMP], M.bank(4)[:, 0:NCMP], ACT.Copy)
    for c in range(4):
        act.activation(R.vcmp[:, c, 0:NCMP], M.bank(5)[:, 0:NCMP], ACT.Copy)
    act.drain().then_inc(M.sem("nsa_vcmp"), 1)
    act.wait_ge(M.sem("nsa_turned_in"), 1)
    act.activation(R.val_s, M.bank(0), ACT.Copy)
    act.activation(R.val_w, M.bank(1), ACT.Copy)
    act.activation(R.gates.rearrange("p g t -> p t g"),
                   M.bank(2).rearrange("p (t c) -> p t c", t=QT)[:, :, 0:48], ACT.Copy)
    act.wait_ge(M.sem("nsa_vcmp_turned"), 1)
    for c in range(4):
        rows = slice(32 * c, 32 * c + 32)
        act.activation(R.vz[rows, c, :], M.bank(3, rows)[:, 0:P], ACT.Copy)
    act.drain().then_inc(M.sem("nsa_turned_kept"), 1)
    head_norms_act(act, M, "nsa_norm", [R.kcmp, R.ks, R.kw] + [R.q[:, k, :] for k in range(8)])
    for n in range(4):
        act.wait_ge(M.sem("nsa_cmp_less_top"), n + 1)
        act.activation(R.p[:, n, :], R.p[:, n, :], ACT.Exp).then_inc(M.sem("nsa_cmp_exp"), 1)
    for n in range(4):
        act.wait_ge(M.sem("nsa_cmp_turned"), n + 1)
        act.activation(R.pt[:, n, :], M.bank(4 + n % 2), ACT.Copy).then_inc(M.sem("nsa_cmp_kept"), 1)
    R.pairs.act(act, M)
    branch_out_act(act, M, "nsa_out", 1, 2)


def nsa_dve(dve, M, R):
    dve.memset(R.kcmp, 0.0)
    dve.memset(R.vcmp, 0.0)
    dve.memset(R.vz, 0.0)
    dve.memset(R.z, 0.0)
    dve.drain().then_inc(M.sem("nsa_zeroed"), 1)
    dve.wait_ge(M.sem("nsa_in_free"), 4 + 2)
    for n, (src, dst) in enumerate(((R.kc, R.kin), (R.vc, R.vin))):
        tok = src.rearrange("p (n l) -> p l n", l=16)
        for part in range(2):
            at = COLS["cmp_pos"] + 32 * n + 16 * part
            pos = M.col[:, at:at + 16].unsqueeze(2).broadcast_to([P, 16, NCMP])
            dve.tensor_tensor(dst[:, 16 * part:16 * part + 16, :], tok[:, :, part:part + NCMP], pos, ALU.add)
    dve.drain().then_inc(M.sem("nsa_windows"), 1)
    dve.wait_ge(M.sem("nsa_turned_kept"), 1)
    head_norms_dve(dve, M, "nsa_norm", [R.kcmp, R.ks, R.kw] + [R.q[:, k, :] for k in range(8)],
                   [M.c("nsa_k", k) for k in range(3)] + [M.c("nsa_q")] * 8)
    rows16 = lambda x: x.rearrange("p (g n) -> p g n", n=32)
    wide = lambda x: x.unsqueeze(2).broadcast_to([P, 16, 32])
    four = lambda x: x.unsqueeze(1).broadcast_to([P, 4, P])
    heads = lambda x: x.rearrange("p (j x) -> p j x", j=4)
    for n in range(4):
        dve.wait_ge(M.sem("nsa_cmp_scores"), n + 1)
        p = R.p[:, n, :]
        dve.scalar_tensor_tensor(out=heads(p), in0=heads(M.bank(n)), scalar=SCALE_64,
                                 in1=four(M.t("cmp_bias", P)), op0=ALU.mult, op1=ALU.add)
        dve.drain()
        dve.tensor_reduce(R.top, rows16(p), AX_X, ALU.max)
        dve.drain()
        dve.tensor_tensor(rows16(p), rows16(p), wide(R.top), ALU.subtract)
        dve.drain().then_inc(M.sem("nsa_cmp_less_top"), 1)
    for n in range(4):
        half, quad = n // 2, n % 2
        dve.wait_ge(M.sem("nsa_cmp_exp"), n + 1)
        p = R.p[:, n, :]
        dve.tensor_reduce(R.sum, rows16(p), AX_X, ALU.add)
        dve.drain()
        dve.reciprocal(R.top, R.sum)
        dve.drain()
        dve.tensor_tensor(rows16(p), rows16(p), wide(R.top), ALU.mult)
        dve.drain()
        dve.tensor_tensor(heads(p), heads(p), four(M.t("cmp_seen", P)), ALU.mult)
        dve.drain()
        z = R.z[:, 4 * half:4 * half + 4, 1:33]
        dve.tensor_reduce(R.part, p.rearrange("p (j x) -> p x j", j=4), AX_X, ALU.add)
        dve.drain()
        part = R.part.rearrange("p (i n) -> p i n", n=32)
        dve.tensor_tensor(z, z, part, ALU.add)
        g = R.gates[:, 8 * half + 4 * quad:8 * half + 4 * quad + 4, :].rearrange("p j i -> p (j i)")
        dve.tensor_tensor(rows16(p), rows16(p), wide(g), ALU.mult)
        dve.drain().then_inc(M.sem("nsa_cmp_gated"), 1)
    dve.tensor_reduce(R.imp, R.z[:, :, 0:32].rearrange("p g (j m) -> p g j m", m=4), AX_X, ALU.add)
    dve.drain()
    dve.tensor_tensor(R.imp, R.imp, R.z[:, :, 4:36:4], ALU.add)
    dve.drain()
    bias = M.t("sel_bias", 32).rearrange("p (i j) -> p i j", j=SEL_N)
    for g in range(2):
        dve.tensor_tensor(R.imp[:, 4 * g:4 * g + 4, :], R.imp[:, 4 * g:4 * g + 4, :], bias, ALU.add)
    dve.drain()
    for r in range(8):
        own = R.imp[:, r, :].unsqueeze(2).broadcast_to([P, 8, 8])
        other = R.imp[:, r, :].unsqueeze(1).broadcast_to([P, 8, 8])
        square = lambda x: x.rearrange("p (a b) -> p a b", b=8)
        dve.tensor_tensor(square(R.gt[:, r, :]), other, own, ALU.is_gt)
        dve.tensor_tensor(square(R.eq[:, r, :]), other, own, ALU.is_equal)
    dve.drain()
    dve.tensor_tensor(R.eq, R.eq, M.t("before", 64).unsqueeze(1).broadcast_to([P, 8, 64]), ALU.mult)
    dve.drain()
    dve.tensor_tensor(R.gt, R.gt, R.eq, ALU.add)
    dve.drain()
    dve.tensor_reduce(R.rank, R.gt.rearrange("p r (j a) -> p (r j) a", a=8), AX_X, ALU.add)
    dve.drain()
    dve.tensor_scalar(R.rank, R.rank, 3.5, NEG, ALU.is_gt, ALU.mult)
    dve.drain()
    for g in range(2):
        for i in range(QT):
            n = 2 * (i + 1)
            sel = R.rank[:, (4 * g + i) * 8:(4 * g + i) * 8 + n].unsqueeze(2).broadcast_to([P, n, 64])
            blocks = lambda x: x.rearrange("p (b k) -> p b k", k=64)
            dve.tensor_tensor(blocks(R.masks[:, g, CAUSAL_AT[i]:CAUSAL_AT[i] + S_LEN[i]]),
                              blocks(M.t("causal", S_LEN[i], at=CAUSAL_AT[i])), sel, ALU.add)
    dve.drain()
    R.pairs.dve(dve, M, lambda i, u, half, kind: R.gates[:, bass.ds(i * 2 + (16 * (kind + 1) + 8 * half + u), 1), :]
                .rearrange("p a b -> p (a b)"))
    branch_out_dve(dve, M, "nsa_out", 1, 2, first=False)



def input_norm_pe(pe, M, name):
    for k in range(NT):
        pe.wait_ge(M.sem("norm_squared"), k + 1 + M.past(name, "squared"))
        mm = norm_total_pe(pe, M, M.norm_bank(name), M.sq[:, k % 2, :], first=(k == 0), last=(k == NT - 1))
        mm.then_inc(M.sem("norm_summed"), 1)
    norm_root_pe(pe, M, name)


def wait_scaled(pe, M, name):
    return lambda k: pe.wait_ge(M.sem("norm_scaled"), k + 1 + M.past(name, "scaled"))


def input_norm_act(act, M, name, after):
    for k in range(NT):
        if after:
            act.wait_ge(M.sem("norm_added"), k + 1 + M.past(after, "added"))
        if k >= 2:
            act.wait_ge(M.sem("norm_summed"), k - 1 + M.past(name, "summed"))
        act.activation(M.sq[:, k % 2, :], M.h[:, k, :], ACT.Square).then_inc(M.sem("norm_squared"), 1)
    act.wait_ge(M.sem("norm_summed"), NT + M.past(name, "summed"))
    act.activation(M.root[:, 0:QT], M.norm_bank(name)[:, 0:QT], ACT.Sqrt, bias=M.eps, scale=1.0 / D)\
       .then_inc(M.sem("norm_root"), 1)


def input_norm_dve(dve, M, name, gain):
    norm_dve_root(dve, M, name)
    scale_dve(dve, M, name, lambda k: M.h[:, k, :], lambda k: M.a[:, k, :], gain, NT)



STEPS = 10
N_STATE = QT - 1


class Ssd:
    def __init__(self, M):
        tiles = [M.big[:, n, :] for n in range(16)]
        at = 0
        for _ in range(21):
            t, at = M.carve(at, T)
            tiles.append(t)
        take = lambda n: [tiles.pop(0) for _ in range(n)]
        self.conv = [take(6), take(6)]
        self.gate = [take(4), take(4)]
        self.x_tok = take(4)
        self.b_tok, self.cb = take(2)
        self.decay = take(2)
        self.c_dec = take(2)
        self.state = [None] + take(3)
        self.xw = take(3)
        self.sig = [M.sq[:, 0, :], M.sq[:, 1, :]]
        self.acum = M.extra[:, 0, :]
        self.dt = M.extra[:, 1, :]
        self.acol = M.extra[:, 2, 0:128].rearrange("p (c h) -> p c h", c=QT)
        self.dtc = M.extra[:, 2, 128:256].rearrange("p (c h) -> p c h", c=QT)
        self.to_end = M.extra[:, 2, 256:384].rearrange("p (c h) -> p c h", c=QT)
        self.chunk_decay = M.extra[:, 2, 384:512].rearrange("p (c h) -> p c h", c=QT)
        self.a = M.extra[:, 3, 0:2]
        self.y = M.big[:, 16:32, :]


def ssd_block(g, s):
    return FIRST["ssd_in"] + 1 + STEPS * g + s


def head_cols(x, e):
    return x[:, e * 64:(e + 1) * 64]


def ssd_pe(pe, M, R):
    used = M.sem("blocks_used")
    ones_row = lambda k: M.t("ident", 1, at=k).broadcast_to([P, P])

    def project(g, s):
        n = STEPS * g + s + 1
        pe.wait_ge(M.sem("ssd_free"), n + 1)
        wait_block(pe, M, FIRST["ssd_in"] + n)
        for k in range(BLK):
            mm = pe.matmul(M.bank(n % 2), block_tile(M, FIRST["ssd_in"] + n, k), M.a[:, k, :],
                           start=(k == 0), stop=(k == 7))
        mm.then_inc(used, 1)

    def turn(g):
        cv = R.conv[g % 2]
        pe.wait_ge(M.sem("ssd_x"), 6 * (g + 1))
        if g:
            pe.wait_ge(M.sem("ssd_y"), 4 * g)
        for c in range(QT):
            s = slice(c * P, (c + 1) * P)
            mm = pe.transpose(M.bank(2)[:, s], cv[4][:, s], M.t("ident", P))
        mm.then_inc(M.sem("ssd_b_turned"), 1)
        for c in range(QT):
            s = slice(c * P, (c + 1) * P)
            for k in range(4):
                mm = pe.transpose(M.bank(3 + c)[:, k * P:(k + 1) * P], cv[k][:, s], M.t("ident", P))
            mm.then_inc(M.sem("ssd_x_turned"), 1)
        for c in range(QT):
            s = slice(c * P, (c + 1) * P)
            mm = pe.matmul(M.bank(7)[:, s], cv[4][:, s], cv[5][:, s], start=True, stop=True)
        mm.then_inc(M.sem("ssd_cb"), 1)

    def states(g):
        pe.wait_ge(M.sem("ssd_b_kept"), g + 1)
        for c in range(N_STATE):
            pe.wait_ge(M.sem("ssd_xw"), N_STATE * g + c + 1)
            pe.matmul(M.bank(3 + c), R.b_tok[:, c * P:(c + 1) * P], R.xw[c], start=True, stop=True)\
              .then_inc(M.sem("ssd_added"), 1)

    def cumulated(g, e):
        h = 8 * g + e
        if e == 0:
            pe.wait_ge(M.sem("ssd_state"), N_STATE * (g + 1))
        if h >= 2:
            pe.wait_ge(M.sem("ssd_exp_c"), h - 1)
            pe.wait_ge(M.sem("ssd_seg"), h - 1)
        pe.matmul(M.bank(4 + e % 2), ones_row(h), R.acum, start=True, stop=True)\
          .then_inc(M.sem("ssd_cumulated"), 1)

    def output(g, e):
        h = 8 * g + e
        pe.wait_ge(M.sem("ssd_decay_cb"), h + 1)
        pe.wait_ge(M.sem("ssd_c_dec"), h + 1)
        pair = h // 2
        if pair >= 2:
            pe.wait_ge(M.sem("ssd_y"), pair - 1)
        bank = 6 if pair % 2 == 0 else 3
        rows = HALVES[e % 2]
        for c in range(QT):
            s = slice(c * P, (c + 1) * P)
            mm = pe.matmul(M.bank(bank, rows)[:, s], head_cols(R.x_tok[c], e), R.decay[e % 2][:, s],
                           start=(c == 0), stop=False, skip_group_check=True)
            if c:
                mm = pe.matmul(M.bank(bank, rows)[:, s], head_cols(R.state[c], e), R.c_dec[e % 2][:, s],
                               start=False, stop=(c == QT - 1), skip_group_check=True)
        mm.then_inc(M.sem("ssd_out_mm"), 1)

    pe.wait_ge(M.sem("nsa_out_free"), NT + 2)
    project(0, -1)
    for s in range(2):
        project(0, s)
    pe.wait_ge(M.sem("ssd_dt"), 1)
    for n, src in enumerate((R.acum, R.dt)):
        for c in range(QT):
            mm = pe.transpose(M.bank(2 + n)[:, c * P:(c + 1) * P], src[:, c * P:(c + 1) * P], M.t("ident", P))
    mm.then_inc(M.sem("ssd_dt_turned"), 1)
    project(0, 2)
    pe.wait_ge(M.sem("ssd_dt_kept"), 1)
    pe.matmul(M.bank(4)[:, 0:P], ones_row(P - 1), R.acol.rearrange("p c h -> p (c h)"), start=True, stop=True)\
      .then_inc(M.sem("ssd_last"), 1)
    for s in range(3, STEPS):
        project(0, s)
    pe.wait_ge(M.sem("ssd_to_end"), 1)
    for g in range(GRPS):
        for s in range(STEPS):
            if s == 0:
                turn(g)
            if s == 1:
                states(g)
            if 2 <= s <= 8:
                cumulated(g, s - 1)
            if g + 1 < GRPS:
                project(g + 1, s)
            if s == 1:
                cumulated(g, 0)
            if s >= 2:
                output(g, s - 2)
    norm_pe(pe, M, "ssd_norm", 16)
    branch_out_pe(pe, M, "ssd_out", lambda k: R.y[:, k, :], 2, 4,
                  lambda blk: pe.wait_ge(M.sem("norm_scaled"), BLK * (blk + 1) + M.past("ssd_norm", "scaled")))


def ssd_act(act, M, R):
    def project(g, s):
        n = STEPS * g + s + 1
        if s < 6:
            act.wait_ge(M.sem("ssd_conv"), 6 * g + s + 1)
            src = R.conv[g % 2][s]
        else:
            act.wait_ge(M.sem("blocks_used"), FIRST["ssd_in"] + n + 1)
            src = M.bank(n % 2)
        if n >= 3:
            act.wait_ge(M.sem("ssd_x"), conv_tiles(n - 2))
            if gate_tiles(n - 2):
                act.wait_ge(M.sem("ssd_gate"), gate_tiles(n - 2))
        act.activation(R.sig[n % 2], src, ACT.Sigmoid).then_inc(M.sem("ssd_sig"), 1)

    def mix(g, s):
        if s == 0:
            act.wait_ge(M.sem("ssd_b_turned"), g + 1)
            act.activation(R.b_tok, M.bank(2), ACT.Copy).then_inc(M.sem("ssd_b_kept"), 1)
        if 1 <= s <= 8:
            e = s - 1
            h = 8 * g + e
            act.wait_ge(M.sem("ssd_seg"), h + 1)
            act.activation(R.c_dec[e % 2], M.bank(4 + e % 2), ACT.Exp).then_inc(M.sem("ssd_exp_c"), 1)
            act.activation(R.decay[e % 2], R.decay[e % 2], ACT.Exp).then_inc(M.sem("ssd_decay"), 1)

    def squares(s):
        for k in ssd_squares(s):
            act.wait_ge(M.sem("ssd_y"), k + 1)
            if k >= 2:
                act.wait_ge(M.sem("norm_summed"), k - 1 + M.past("ssd_norm", "summed"))
            act.activation(M.sq[:, k % 2, :], R.y[:, k, :], ACT.Square).then_inc(M.sem("norm_squared"), 1)

    act.activation(R.a[0:32, 0:1], M.c("a_log", rows=slice(0, 32)), ACT.Exp).then_inc(M.sem("ssd_a"), 1)
    act.wait_ge(M.sem("ssd_abs"), 1)
    act.activation(R.conv[1][1][0:32, :], R.conv[1][1][0:32, :], ACT.Exp, scale=-1.0).then_inc(M.sem("ssd_abs_exp"), 1)
    project(0, 0)
    project(0, 1)
    act.wait_ge(M.sem("ssd_dt_turned"), 1)
    for n, dst in enumerate((R.acol, R.dtc)):
        act.activation(dst, M.bank(2 + n).rearrange("p (c x) -> p c x", c=QT)[:, :, 0:32], ACT.Copy)
    act.drain().then_inc(M.sem("ssd_dt_kept"), 1)
    project(0, 2)
    act.wait_ge(M.sem("ssd_last"), 1)
    act.activation(R.chunk_decay.rearrange("p c h -> p (c h)"), M.bank(4)[:, 0:P], ACT.Exp)\
       .then_inc(M.sem("ssd_chunk_decay"), 1)
    act.wait_ge(M.sem("ssd_to_end_log"), 1)
    act.activation(R.to_end, R.to_end, ACT.Exp).then_inc(M.sem("ssd_to_end"), 1)
    for s in range(3, STEPS):
        project(0, s)
    for g in range(GRPS):
        for s in range(STEPS):
            if s != 1:
                mix(g, s)
            if g + 1 < GRPS:
                project(g + 1, s)
            if s == 1:
                mix(g, s)
            if g + 1 == GRPS:
                squares(s)
    norm_act_root(act, M, "ssd_norm", 2048)
    branch_out_act(act, M, "ssd_out", 2, 4)


def ssd_squares(s):
    return {9: [14, 15]}.get(s, [2 * (s - 1), 2 * s - 1] if 1 <= s <= 7 else [])


def conv_tiles(n):
    return 6 * ((n - 1) // STEPS) + min((n - 1) % STEPS + 1, 6) if n else 0


def gate_tiles(n):
    return n - conv_tiles(n)


def ssd_dve(dve, M, R):
    dve.drain().then_inc(M.sem("ssd_free"), 2)
    r32 = slice(0, 32)

    def project(g, s):
        n = STEPS * g + s + 1
        if s < 6:
            dve.wait_ge(M.sem("blocks_used"), FIRST["ssd_in"] + n + 1)
            tile = 4 * g + s if s < 4 else (16 + g if s == 4 else 20 + g)
            w = [M.c("conv_w", 24 * k + tile) for k in range(4)]
            out, src = R.conv[g % 2][s], M.bank(n % 2)
            dve.tensor_scalar(out, src, w[3], M.c("conv_b", tile), ALU.mult, ALU.add)
            dve.drain()
            for back in (1, 2, 3):
                dve.scalar_tensor_tensor(out=out[:, back:T], in0=src[:, 0:T - back], scalar=w[3 - back],
                                         in1=out[:, back:T], op0=ALU.mult, op1=ALU.add)
                dve.drain()
            dve.nop().then_inc(M.sem("ssd_conv"), 1)
            dve.nop().then_inc(M.sem("ssd_free"), 1)
        else:
            dve.wait_ge(M.sem("ssd_sig"), n)
            dve.tensor_tensor(R.gate[g % 2][s - 6], M.bank(n % 2), R.sig[n % 2], ALU.mult)
            dve.drain().then_inc(M.sem("ssd_gate"), 1)
            dve.nop().then_inc(M.sem("ssd_free"), 1)

    heads = lambda x: x.rearrange("p (h d) -> p h d", d=64)

    def by_head(x, c, g):
        return x[:, c, 8 * g:8 * g + 8].unsqueeze(2).broadcast_to([P, 8, 64])

    def mix(g, s):
        if s == 0:
            for c in range(QT):
                dve.wait_ge(M.sem("ssd_x_turned"), QT * g + c + 1)
                dve.tensor_tensor(heads(R.x_tok[c]), heads(M.bank(3 + c)), by_head(R.dtc, c, g), ALU.mult)\
                   .then_inc(M.sem("ssd_xdt"), 1)
            dve.wait_ge(M.sem("ssd_cb"), g + 1)
            four = lambda x: x.rearrange("p (c i) -> p c i", c=QT)
            dve.tensor_tensor(four(R.cb), four(M.bank(7)), M.t("tri", P).unsqueeze(1).broadcast_to([P, QT, P]),
                              ALU.mult)
            dve.drain()
        if s == 1:
            for c in range(N_STATE):
                dve.wait_ge(M.sem("ssd_added"), N_STATE * g + c + 1)
                if c == 0:
                    dve.tensor_copy(R.state[1], M.bank(3))
                else:
                    dve.tensor_tensor(heads(R.state[c + 1]), heads(R.state[c]), by_head(R.chunk_decay, c, g), ALU.mult)
                    dve.drain()
                    dve.tensor_tensor(R.state[c + 1], R.state[c + 1], M.bank(3 + c), ALU.add)
                dve.drain().then_inc(M.sem("ssd_state"), 1)
        if s >= 2:
            e = s - 2
            h = 8 * g + e
            dve.wait_ge(M.sem("ssd_decay"), h + 1)
            dve.tensor_tensor(R.decay[e % 2], R.decay[e % 2], R.cb, ALU.mult).then_inc(M.sem("ssd_decay_cb"), 1)
        if 1 <= s <= 8:
            e = s - 1
            h = 8 * g + e
            dve.wait_ge(M.sem("ssd_cumulated"), h + 1)
            if h >= 2:
                dve.wait_ge(M.sem("ssd_out_mm"), h - 1)
            for c in range(QT):
                w = slice(c * P, (c + 1) * P)
                dve.tensor_scalar(R.decay[e % 2][:, w], M.bank(4 + e % 2)[:, w], R.acol[:, c, h:h + 1], 0.0,
                                  ALU.subtract, ALU.min)
            dve.drain().then_inc(M.sem("ssd_seg"), 1)
        if s >= 4 and s % 2 == 0:
            pair_out(g, s // 2 - 2)

    def sums(s):
        for k in ssd_squares(s):
            dve.wait_ge(M.sem("norm_squared"), k + 1 + M.past("ssd_norm", "squared"))
            if k == 0:
                dve.tensor_copy(M.ssum[:, :], M.sq[:, 0, :])
            else:
                dve.tensor_tensor(M.ssum[:, :], M.ssum[:, :], M.sq[:, k % 2, :], ALU.add)
            dve.drain().then_inc(M.sem("norm_summed"), 1)

    def pair_out(g, k):
        pair = 4 * g + k
        dve.wait_ge(M.sem("ssd_out_mm"), 2 * (pair + 1))
        y = R.y[:, pair, :]
        dve.scalar_tensor_tensor(out=y, in0=R.conv[g % 2][k], scalar=M.c("ssd_d", pair),
                                 in1=M.bank(6 if pair % 2 == 0 else 3), op0=ALU.mult, op1=ALU.add)
        dve.drain()
        dve.tensor_tensor(y, y, R.gate[g % 2][k], ALU.mult)
        dve.drain().then_inc(M.sem("ssd_y"), 1)

    xa, ab, s_, t_, p_ = [R.conv[1][k][r32, :] for k in range(5)]
    dve.memset(R.acum, 0.0)
    dve.memset(R.dt, 0.0)
    dve.wait_ge(M.sem("blocks_used"), FIRST["ssd_in"] + 1)
    dve.tensor_scalar(xa, M.bank(0, r32), M.c("dt_bias", rows=r32), None, ALU.add)
    dve.drain().then_inc(M.sem("ssd_free"), 1)
    dve.scalar_tensor_tensor(out=ab, in0=xa, scalar=-1.0, in1=xa, op0=ALU.mult, op1=ALU.max)
    dve.drain().then_inc(M.sem("ssd_abs"), 1)
    dve.wait_ge(M.sem("ssd_abs_exp"), 1)
    dve.tensor_scalar(t_, ab, 2.0, None, ALU.add)
    dve.drain()
    dve.reciprocal(s_, t_)
    dve.drain()
    dve.tensor_tensor(s_, s_, ab, ALU.mult)
    dve.drain()
    dve.tensor_tensor(t_, s_, s_, ALU.mult)
    dve.drain()
    dve.tensor_scalar(p_, t_, 1.0 / 17, None, ALU.mult)
    dve.drain()
    for k in range(15, 2, -2):
        dve.scalar_tensor_tensor(out=p_, in0=p_, scalar=1.0 / k, in1=t_, op0=ALU.add, op1=ALU.mult)
        dve.drain()
    dve.scalar_tensor_tensor(out=p_, in0=p_, scalar=1.0, in1=s_, op0=ALU.add, op1=ALU.mult)
    dve.tensor_scalar(xa, xa, 0.0, None, ALU.max)
    dve.drain()
    dve.scalar_tensor_tensor(out=R.dt[r32, :], in0=p_, scalar=2.0, in1=xa, op0=ALU.mult, op1=ALU.add)
    dve.wait_ge(M.sem("ssd_a"), 1)
    dve.tensor_scalar(R.a[r32, 1:2], R.a[r32, 0:1], -1.0, None, ALU.mult)
    dve.drain()
    dve.tensor_scalar(t_, R.dt[r32, :], R.a[r32, 1:2], None, ALU.mult)
    dve.drain()
    dve.tensor_tensor_scan(R.acum[r32, :], M.t("restart128", T, rows=r32), t_, 0.0, ALU.mult, ALU.add)
    dve.drain().then_inc(M.sem("ssd_dt"), 1)
    for s in range(3):
        project(0, s)
    dve.wait_ge(M.sem("ssd_last"), 1)
    flat = lambda x: x.rearrange("p c h -> p (c h)")
    dve.wait_ge(M.sem("ssd_chunk_decay"), 1)
    dve.tensor_tensor(flat(R.to_end), M.bank(4)[:, 0:P], flat(R.acol), ALU.subtract)
    dve.drain().then_inc(M.sem("ssd_to_end_log"), 1)
    for s in range(3, STEPS):
        project(0, s)
    for g in range(GRPS):
        for s in range(STEPS):
            if s != 1:
                mix(g, s)
            if s == 9:
                pair_out(g, 3)
            if g + 1 < GRPS:
                project(g + 1, s)
            if s == 1:
                mix(g, s)
            if g + 1 == GRPS:
                sums(s)
    norm_dve_root(dve, M, "ssd_norm")
    scale_dve(dve, M, "ssd_norm", lambda k: R.y[:, k, :], lambda k: R.y[:, k, :], lambda k: M.c("ssd_norm", k), 16)
    branch_out_dve(dve, M, "ssd_out", 2, 4, first=False)


def ssd_pool(pool, M, R):
    heads = lambda x: x.rearrange("p (h d) -> p h d", d=64)

    def project(g, s):
        if s < 6:
            n = STEPS * g + s + 1
            pool.wait_ge(M.sem("ssd_sig"), n)
            x = R.conv[g % 2][s]
            pool.tensor_tensor(x, x, R.sig[n % 2], ALU.mult).then_inc(M.sem("ssd_x"), 1)

    def mix(g, s):
        if s == 0:
            for c in range(N_STATE):
                pool.wait_ge(M.sem("ssd_xdt"), QT * g + c + 1)
                if g == 0 and c == 0:
                    pool.wait_ge(M.sem("ssd_to_end"), 1)
                w = R.to_end[:, c, 8 * g:8 * g + 8].unsqueeze(2).broadcast_to([P, 8, 64])
                pool.tensor_tensor(heads(R.xw[c]), heads(R.x_tok[c]), w, ALU.mult).then_inc(M.sem("ssd_xw"), 1)
        if 1 <= s <= 8:
            e = s - 1
            pool.wait_ge(M.sem("ssd_exp_c"), 8 * g + e + 1)
            pool.tensor_tensor(R.c_dec[e % 2], R.c_dec[e % 2], R.conv[g % 2][5], ALU.mult)\
                .then_inc(M.sem("ssd_c_dec"), 1)

    for s in range(STEPS):
        project(0, s)
    for g in range(GRPS):
        for s in range(STEPS):
            if s != 1:
                mix(g, s)
            if g + 1 < GRPS:
                project(g + 1, s)
            if s == 1:
                mix(g, s)



def to_h_dve(dve, M, name, per_tile, unroll, banks):
    def move(t, u):
        h = tile_at(M.h, t)
        return dve.tensor_tensor(h, h, M.bank(u % banks), ALU.add)

    gemm_out(dve, M, name, NT, per_tile, unroll, banks, move)


def tail_pe(pe, M):
    pe.wait_ge(M.sem("ssd_out_free"), NT + 2)
    gemm_pe(pe, M, "mix_out", NT, 1, lambda k: M.m[:, k, :], 4)
    mlp_norm_pe(pe, M, "ff", "norm_5")


def tail_act(act, M):
    gemm_ready(act, M, "mix_out", NT, 4)
    input_norm_act(act, M, "norm_5", None)
    for part in range(2):
        hidden_act(act, M, "ff", part)


def tail_dve(dve, M):
    to_h_dve(dve, M, "mix_out", 1, 4, 4)
    norm_dve_root(dve, M, "norm_5")
    split_input_dve(dve, M, "norm_5", lambda k: M.c("norm2", k))
    for part in range(2):
        hidden_dve(dve, M, "ff", part)
        to_h_dve(dve, M, f"ff_down{part}", 2, 2, 2)


def program(nc, wall, cols, tabs, pos, x, out):
    with ExitStack() as ctx:
        M = Memory(nc, ctx)
        M.eps = EPS
        mla = Mla(M)
        hgrn = Hgrn(M)
        dsa = Dsa(M)
        nsa = Nsa(M)
        ssd = Ssd(M)
        block = ctx.enter_context(nc.Block())

        @block.sync
        def _(sp):
            sp.dma_start(M.h[:, :, :], x.rearrange("(k p) t -> p k t", p=P)).then_inc(M.sem("x_in"), 16)
            sp.dma_start(M.col[:, :], cols).then_inc(M.sem("tables_in"), 16)
            sp.dma_start(M.tab[:, :], tabs).then_inc(M.sem("tables_in"), 16)
            sp.dma_start(mla.pos, pos.partition_broadcast(P).rearrange("p a t -> p (a t)"))\
              .then_inc(M.sem("positions_in"), 16)
            stream_weights(sp, M, wall, N_BLOCKS)

        @block.gpsimd
        def _(pool):
            pool.wait_ge(M.sem("tables_in"), 32)
            pool.wait_ge(M.sem("mla_y_free"), MLA_H)
            mlp_split_pool(pool, M, "mlp0")
            pool.wait_ge(M.sem("hg_y"), MLA_H)
            mlp_split_pool(pool, M, "mlp1")
            dsa_pool(pool, M, dsa)
            pool.wait_ge(M.sem("nsa_cmp_kept"), 4)
            pairs_pool(pool, M, nsa.pairs, "nsa_norm", 11)
            ssd_pool(pool, M, ssd)
            pool.wait_ge(M.sem("norm_scaled"), 16 + M.past("ssd_norm", "scaled"))
            mlp_split_pool(pool, M, "ff")
            pool.wait_ge(M.sem("ff_down1_free"), NT + 2)
            pool.dma_start(out.rearrange("(k p) t -> p k t", p=P), M.h[:, :, :]).then_inc(M.sem("out_done"), 16)
            pool.wait_ge(M.sem("out_done"), 16)

        @block.tensor
        def _(pe):
            pe.wait_ge(M.sem("tables_in"), 32)
            input_norm_pe(pe, M, "norm_0")
            mla_pe(pe, M, mla)
            mlp_norm_pe(pe, M, "mlp0", "norm_1")
            norm_pe(pe, M, "mlp0_down", NT)
            input_norm_pe(pe, M, "norm_2")
            hgrn_pe(pe, M, hgrn)
            mlp_norm_pe(pe, M, "mlp1", "norm_3")
            norm_pe(pe, M, "mlp1_down", NT)
            input_norm_pe(pe, M, "norm_4")
            dsa_pe(pe, M, dsa)
            nsa_pe(pe, M, nsa)
            ssd_pe(pe, M, ssd)
            tail_pe(pe, M)

        @block.scalar
        def _(act):
            act.wait_ge(M.sem("x_in"), 16)
            input_norm_act(act, M, "norm_0", None)
            mla_act(act, M, mla)
            input_norm_act(act, M, "norm_1", "mla_o")
            mlp_act(act, M, "mlp0")
            input_norm_act(act, M, "norm_2", "mlp0_down")
            hgrn_act(act, M, hgrn)
            input_norm_act(act, M, "norm_3", "hgrn_o")
            mlp_act(act, M, "mlp1")
            input_norm_act(act, M, "norm_4", "mlp1_down")
            dsa_act(act, M, dsa)
            nsa_act(act, M, nsa)
            ssd_act(act, M, ssd)
            tail_act(act, M)

        @block.vector
        def _(dve):
            dve.wait_ge(M.sem("tables_in"), 32)
            input_norm_dve(dve, M, "norm_0", lambda k: M.c("gains", k))
            rope_angles_dve(dve, M, mla)
            mla_dve(dve, M, mla)
            norm_dve_root(dve, M, "norm_1")
            split_input_dve(dve, M, "norm_1", lambda k: M.c("gains", 16 + k))
            mlp_dve(dve, M, "mlp0", lambda k: M.c("gains", 24 + k))
            input_norm_dve(dve, M, "norm_2", lambda k: M.c("gains", 32 + k))
            hgrn_dve(dve, M, hgrn)
            norm_dve_root(dve, M, "norm_3")
            split_input_dve(dve, M, "norm_3", lambda k: M.c("gains", 48 + k))
            mlp_dve(dve, M, "mlp1", lambda k: M.c("gains", 56 + k))
            input_norm_dve(dve, M, "norm_4", lambda k: M.c("norm1", k))
            dsa_dve(dve, M, dsa)
            nsa_dve(dve, M, nsa)
            ssd_dve(dve, M, ssd)
            tail_dve(dve, M)





def pack(w, n_order=None, k_first=False):
    K, N = w.shape
    t = w.reshape(K // P, P, N // P, P).transpose(2, 0, 1, 3)
    return t.reshape(-1, P, P)


def lay_weights(v):
    wall = np.zeros((N_BLOCKS, P, BLK * P), np.float32)

    def put(name, tiles):
        n = dict(COUNTS)[name]
        tiles = np.asarray(tiles)
        full = np.zeros((n * BLK, P, P), np.float32)
        full[:len(tiles)] = tiles
        wall[FIRST[name]:FIRST[name] + n] = full.reshape(n, BLK, P, P).transpose(0, 2, 1, 3).reshape(n, P, BLK * P)

    def put_mlp(name, up, down):
        up, down = pack(up).reshape(2, -1, P, P), pack(down).reshape(NT, 2, -1, P, P)
        for part in range(2):
            put(f"{name}_up{part}", up[part])
            put(f"{name}_down{part}", down[:, part].reshape(-1, P, P))

    w_in = v["mla_w_in"][0]
    kr = w_in[:, 768:832]
    put("mla_in", pack(np.concatenate([w_in[:, :768], kr, kr], 1)))
    uq = v["mla_w_uq"][0].reshape(512, MLA_H, 192)
    put("mla_rope", pack(np.ascontiguousarray(uq[:, :, 128:]).reshape(512, 512)))
    ukv = v["mla_w_ukv"][0].reshape(256, MLA_H, 256)
    put("mla_heads", np.concatenate([np.concatenate([
        uq[:, h, :128].reshape(4, P, P), ukv[:, h, :128].reshape(2, P, P), ukv[:, h, 128:].reshape(2, P, P)])
        for h in range(MLA_H)]))
    put("mla_o", pack(v["mla_w_o"][0]))
    for l in range(2):
        put_mlp(f"mlp{l}", v["mlp_w1"][l], v["mlp_w2"][l])
    w = v["hgrn_w_in"][0].reshape(NT, P, 4, MLA_H, P).transpose(3, 2, 0, 1, 4)
    put("hgrn_heads", w.reshape(-1, P, P))
    put("hgrn_o", pack(v["hgrn_w_o"][0]))
    names = ["dq", "dk", "dv", "iq", "ik", "iw", "nq", "nkv", "ng", "sz", "sx", "sdt", "mg"]
    sizes = [1024, 64, 64, 256, 32, 8, 1024, 768, 48, 2048, 3072, 32, 3072]
    w = dict(zip(names, np.split(v["w_in_2"][0], np.cumsum(sizes)[:-1], axis=1)))
    none = np.zeros((D, P), np.float32)
    wide = lambda x: np.concatenate([x, none[:, x.shape[1]:]], 1)
    put("dsa_in", pack(np.concatenate([w["dk"]] * 2 + [w["dv"]] * 2 + [w["iq"]] + [w["ik"]] * 4
                                      + [wide(w["iw"]), w["dq"]], 1)))

    def branch(n, w_out):
        g = pack(w["mg"][:, n * D:(n + 1) * D]).reshape(NT, NT, P, P)
        o = pack(w_out).reshape(NT, -1, P, P)
        return np.concatenate([g, o], 1).reshape(-1, P, P)

    put("dsa_out", branch(0, v["w_br_dsa_2"][0]))
    nq = w["nq"].reshape(D, 2, 8, 64).transpose(0, 2, 1, 3).reshape(D, 1024)
    ng = w["ng"].reshape(D, 2, 8, 3).transpose(0, 3, 1, 2).reshape(D, 48)
    put("nsa_in", pack(np.concatenate([w["nkv"], wide(ng), nq], 1)))
    cw = v["nsa_cmp_w_2"][0]
    both = np.zeros((32, 2, P, P), np.float32)
    both[:, :, :64, :64] = cw.transpose(1, 0, 2, 3)
    both[:, :, 64:, 64:] = cw.transpose(1, 0, 2, 3)
    put("nsa_cmp", both.reshape(-1, P, P))
    w_nsa = v["w_br_nsa_2"][0].reshape(2, 8, 64, D).transpose(1, 0, 2, 3).reshape(D, D)
    put("nsa_out", branch(1, w_nsa))
    z, sx = w["sz"], w["sx"]
    order = [wide(w["sdt"])]
    for g in range(GRPS):
        order += [sx[:, 512 * g:512 * (g + 1)], sx[:, 2048 + P * g:2048 + P * (g + 1)],
                  sx[:, 2560 + P * g:2560 + P * (g + 1)], z[:, 512 * g:512 * (g + 1)]]
    put("ssd_in", pack(np.concatenate(order, 1)))
    put("ssd_out", branch(2, v["w_br_ssd_2"][0]))
    put("mix_out", pack(v["w_out_2"][0]))
    put_mlp("ff", v["w_ff1_2"][0], v["w_ff2_2"][0])
    return wall


def lay_columns(v):
    c = np.zeros((P, N_COLS), np.float32)

    def put(name, x, k=0):
        x = np.asarray(x)
        c[:x.shape[0], COLS[name] + k:COLS[name] + k + x.shape[1]] = x

    rows = lambda x: np.asarray(x).reshape(-1, P).T
    put("gains", rows(v["norm_gains"]))
    put("q_norm", rows(v["mla_q_norm"]))
    put("kv_norm", rows(v["mla_kv_norm"]))
    put("lb", rows(v["hgrn_lb_logits"]))
    put("o_norm", rows(v["hgrn_o_norm"]))
    put("norm1", rows(v["norm1_g_2"]))
    twice = lambda x: np.concatenate([np.asarray(x)] * 2, -1).reshape(-1, P).T
    put("dsa_q", twice(v["dsa_q_norm_2"]))
    put("dsa_k", twice(v["dsa_k_norm_2"]))
    put("nsa_q", twice(v["nsa_q_norm_2"]))
    put("nsa_k", twice(v["nsa_k_norm_2"][0]))
    put("cmp_pos", twice(v["nsa_cmp_pos_2"][0].reshape(64, 64)))
    put("conv_w", rows(v["ssd_conv_w_2"]))
    put("conv_b", rows(v["ssd_conv_b_2"]))
    put("dt_bias", v["ssd_dt_bias_2"].T)
    put("a_log", v["ssd_a_log_2"].T)
    put("ssd_d", rows(np.repeat(v["ssd_d_2"][0], 64)))
    put("ssd_norm", rows(v["ssd_norm_g_2"]))
    put("norm2", rows(v["norm2_g_2"]))
    freq = np.power(np.float32(10000.0), -np.arange(0, 64, 2, dtype=np.float32) / np.float32(64))
    put("freq", np.tile(freq, 4)[:, None])
    put("sign", np.tile(np.repeat([-1.0, 1.0], 32), 2)[:, None])
    return c


def kernel(**inputs):
    import concourse.bacc as _bacc
    from concourse import mybir as _mybir
    from concourse.bass_utils import run_bass_kernel_spmd as _run

    nc = _bacc.Bacc("TRN2", target_bir_lowering=False, num_devices=1)
    v = {k: np.asarray(a) for k, a in inputs.items()}
    arrays = {
        "weights": lay_weights(v),
        "columns": lay_columns(v),
        "tables": tables(),
        "positions": np.ascontiguousarray(v["positions"], dtype=np.int32),
        "x": np.ascontiguousarray(v["x"][0].T),
    }
    args = [nc.dram_tensor(n, a.shape, _mybir.dt.from_np(a.dtype), kind="ExternalInput").ap()
            for n, a in arrays.items()]
    out = nc.dram_tensor("out", (D, T), F32, kind="ExternalOutput").ap()
    program(nc, *args, out)
    r = _run(nc, [arrays], core_ids=[0])
    return np.ascontiguousarray(r.results[0]["out"].T)[None]
```
